# Optimizing a Trainium2 kernel written in Bass

```python
import math
import jax, jax.numpy as jnp
from jax import lax
import numpy as np

D_MODEL = 1024
BATCH = 1
SEQ = 256
DEPTH = 2

HEAD_DIM = 64
NSA_HEADS = 6
NSA_KV_GROUPS = 2
NSA_REP = NSA_HEADS // NSA_KV_GROUPS
N_BRANCH = 3
CMP_LEN = 32
CMP_STRIDE = 16
CMP_HIDDEN = 2 * HEAD_DIM
SEL_BLOCK = 64
SEL_TOP_N = 16
WINDOW = 512
NSA_Q_BLOCK = 32
MLA_HEADS = 5
MLA_Q_RANK = 256
MLA_KV_RANK = 128
MLA_NOPE_DIM = 64
MLA_ROPE_DIM = 32
MLA_V_DIM = 64
ATTN_Q_BLOCK = 128
RET_HEADS = 5
RET_CHUNK = 128
ROPE_THETA = 500000.0
PARTIAL_ROPE_DIM = HEAD_DIM // 4
RET_THETA = 10000.0
D_FF = 4 * D_MODEL
NORM_EPS = 1e-6
NEG_INF = -1e30
FORCE_SCORE = 1e9

NSA_Q_W = NSA_HEADS * HEAD_DIM
NSA_KV_W = NSA_KV_GROUPS * HEAD_DIM
NSA_GATE_W = NSA_HEADS * N_BRANCH
MLA_OUT_W = MLA_HEADS * MLA_V_DIM
RET_W = RET_HEADS * HEAD_DIM
MIX_WIDTH = NSA_Q_W + MLA_OUT_W + RET_W
IN_SIZES = (NSA_Q_W, NSA_KV_W, NSA_KV_W, NSA_KV_W, NSA_KV_W, NSA_KV_W, NSA_KV_W, NSA_GATE_W,
            MLA_Q_RANK, MLA_KV_RANK, MLA_ROPE_DIM, RET_W, RET_W, RET_W, RET_W)
N_IN = sum(IN_SIZES)


F32 = jnp.float32

def in_offsets():
    return [int(o) for o in np.cumsum(IN_SIZES)[:-1]]

def rms_norm(x, gain):
    xf = x.astype(F32)
    y = xf * lax.rsqrt(jnp.mean(xf * xf, axis=-1, keepdims=True) + NORM_EPS) * gain.astype(F32)
    return y.astype(x.dtype)

def masked_softmax(s, mask):
    s = jnp.where(mask, s.astype(F32), NEG_INF)
    m = jnp.max(s, axis=-1, keepdims=True)
    p = jnp.exp(s - m) * mask
    return p / jnp.maximum(jnp.sum(p, axis=-1, keepdims=True), 1e-30)

def rope_tables(positions, dim, theta):
    inv = 1.0 / (theta ** (jnp.arange(0, dim, 2, dtype=F32) / dim))
    ang = positions.astype(F32)[..., None] * inv
    return jnp.cos(ang), jnp.sin(ang)

def apply_rope(x, cos, sin):
    half = x.shape[-1] // 2
    x1 = x[..., :half].astype(F32)
    x2 = x[..., half:].astype(F32)
    c = cos[:, :, None, :]
    s = sin[:, :, None, :]
    return jnp.concatenate([x1 * c - x2 * s, x2 * c + x1 * s], axis=-1).astype(x.dtype)

def partial_rope(x, cos, sin):
    return jnp.concatenate([apply_rope(x[..., :PARTIAL_ROPE_DIM], cos, sin), x[..., PARTIAL_ROPE_DIM:]], axis=-1)

def selection_overlap(n_cmp, n_sel):
    cs = np.arange(n_cmp) * CMP_STRIDE
    ce = cs + CMP_LEN
    ss = np.arange(n_sel) * SEL_BLOCK
    se = ss + SEL_BLOCK
    ov = np.clip(np.minimum(ce[:, None], se[None, :]) - np.maximum(cs[:, None], ss[None, :]), 0, None) / CMP_LEN
    return jnp.asarray(ov.astype(np.float32))

def compress_blocks(tok, tok_idx, pos_emb, w1, w2):
    b, _, g, dh = tok.shape
    blk = tok[:, tok_idx] + pos_emb[None, None, :, None, :]
    flat = blk.transpose(0, 1, 3, 2, 4).reshape(b, tok_idx.shape[0], g, CMP_LEN * dh)
    return jax.nn.gelu(flat @ w1) @ w2

def nsa_mixer(q, k_cmp, v_cmp, k_slc, v_slc, k_win, v_win, gates, pos_k, w1_k, w2_k, pos_v, w1_v, w2_v):
    b, s, _, dh = q.shape
    g, r = NSA_KV_GROUPS, NSA_REP
    n_cmp = (s - CMP_LEN) // CMP_STRIDE + 1
    n_sel = s // SEL_BLOCK
    top_n = min(SEL_TOP_N, n_sel)
    scale = dh ** -0.5
    qb_len = NSA_Q_BLOCK

    tok_idx = np.arange(n_cmp)[:, None] * CMP_STRIDE + np.arange(CMP_LEN)[None, :]
    kc = compress_blocks(k_cmp, tok_idx, pos_k, w1_k, w2_k)
    vc = compress_blocks(v_cmp, tok_idx, pos_v, w1_v, w2_v)
    cmp_end = jnp.arange(n_cmp) * CMP_STRIDE + CMP_LEN - 1
    overlap = selection_overlap(n_cmp, n_sel)

    ks_blk = k_slc.reshape(b, n_sel, SEL_BLOCK, g, dh).transpose(0, 3, 1, 2, 4)
    vs_blk = v_slc.reshape(b, n_sel, SEL_BLOCK, g, dh).transpose(0, 3, 1, 2, 4)
    kw_pad = jnp.pad(k_win, ((0, 0), (WINDOW, 0), (0, 0), (0, 0)))
    vw_pad = jnp.pad(v_win, ((0, 0), (WINDOW, 0), (0, 0), (0, 0)))

    n_qb = s // qb_len
    q_blocks = q.reshape(b, n_qb, qb_len, g, r, dh).transpose(1, 0, 2, 3, 4, 5)
    gate_blocks = jax.nn.sigmoid(gates.astype(F32)).reshape(b, n_qb, qb_len, g, r, N_BRANCH).transpose(1, 0, 2, 3, 4, 5)
    b_idx = jnp.arange(b)[:, None, None, None]
    g_idx = jnp.arange(g)[None, :, None, None]
    sel_ids = jnp.arange(n_sel)[None, :]

    def block(args):
        qb, gb, i = args
        q0 = i * qb_len
        t = q0 + jnp.arange(qb_len)
        s_c = jnp.einsum('bqgrd,bngd->bgrqn', qb, kc) * scale
        p_c = masked_softmax(s_c, cmp_end[None, :] <= t[:, None])
        o_c = jnp.einsum('bgrqn,bngd->bqgrd', p_c, vc)
        imp = jnp.einsum('bgrqn,nm->bgqm', p_c, overlap)
        cur = (t // SEL_BLOCK)[:, None]
        valid = sel_ids <= cur
        forced = (sel_ids == 0) | (sel_ids == cur) | (sel_ids == cur - 1)
        imp = jnp.where(valid & forced, FORCE_SCORE, imp)
        imp = jnp.where(valid, imp, NEG_INF)
        _, idx = lax.top_k(imp, top_n)
        k_sel = ks_blk[b_idx, g_idx, idx]
        v_sel = vs_blk[b_idx, g_idx, idx]
        key_pos = idx[..., None] * SEL_BLOCK + jnp.arange(SEL_BLOCK)
        mask_s = (key_pos <= t[None, None, :, None, None]).reshape(b, g, 1, qb_len, top_n * SEL_BLOCK)
        s_s = jnp.einsum('bqgrd,bgqjsd->bgrqjs', qb, k_sel).reshape(b, g, r, qb_len, top_n * SEL_BLOCK) * scale
        p_s = masked_softmax(s_s, mask_s).reshape(b, g, r, qb_len, top_n, SEL_BLOCK)
        o_s = jnp.einsum('bgrqjs,bgqjsd->bqgrd', p_s, v_sel)
        kw = lax.dynamic_slice_in_dim(kw_pad, q0, qb_len + WINDOW, axis=1)
        vw = lax.dynamic_slice_in_dim(vw_pad, q0, qb_len + WINDOW, axis=1)
        kp = (q0 - WINDOW + jnp.arange(qb_len + WINDOW))[None, :]
        mask_w = (kp <= t[:, None]) & (kp > t[:, None] - WINDOW) & (kp >= 0)
        s_w = jnp.einsum('bqgrd,bkgd->bgrqk', qb, kw) * scale
        p_w = masked_softmax(s_w, mask_w)
        o_w = jnp.einsum('bgrqk,bkgd->bqgrd', p_w, vw)
        return gb[..., 0:1] * o_c + gb[..., 1:2] * o_s + gb[..., 2:3] * o_w

    out = lax.map(block, (q_blocks, gate_blocks, jnp.arange(n_qb)))
    return out.transpose(1, 0, 2, 3, 4, 5).reshape(b, s, NSA_HEADS * dh)

def causal_block_attention(q, k, v, scale):
    b, s, h, dq = q.shape
    n_qb = s // ATTN_Q_BLOCK
    q_blocks = q.reshape(b, n_qb, ATTN_Q_BLOCK, h, dq).transpose(1, 0, 2, 3, 4)
    kp = jnp.arange(s)[None, :]

    def block(args):
        qi, i = args
        t = (i * ATTN_Q_BLOCK + jnp.arange(ATTN_Q_BLOCK))[:, None]
        sc = jnp.einsum('bqhd,bkhd->bhqk', qi, k) * scale
        p = masked_softmax(sc, kp <= t)
        return jnp.einsum('bhqk,bkhd->bqhd', p, v)

    out = lax.map(block, (q_blocks, jnp.arange(n_qb)))
    return out.transpose(1, 0, 2, 3, 4).reshape(b, s, h, v.shape[-1])

def mla_mixer(c_q, c_kv, k_pe, q_norm, w_uq, kv_norm, w_ukv, cos, sin):
    b, s, _ = c_q.shape
    q = (rms_norm(c_q, q_norm) @ w_uq).reshape(b, s, MLA_HEADS, MLA_NOPE_DIM + MLA_ROPE_DIM)
    q_nope, q_pe = q[..., :MLA_NOPE_DIM], apply_rope(q[..., MLA_NOPE_DIM:], cos, sin)
    kv = (rms_norm(c_kv, kv_norm) @ w_ukv).reshape(b, s, MLA_HEADS, MLA_NOPE_DIM + MLA_V_DIM)
    k_nope, v = kv[..., :MLA_NOPE_DIM], kv[..., MLA_NOPE_DIM:]
    k_pe = apply_rope(k_pe[:, :, None, :], cos, sin)
    q_full = jnp.concatenate([q_nope, q_pe], axis=-1)
    k_full = jnp.concatenate([k_nope, jnp.broadcast_to(k_pe, (b, s, MLA_HEADS, MLA_ROPE_DIM)).astype(k_nope.dtype)], axis=-1)
    o = causal_block_attention(q_full, k_full, v, (MLA_NOPE_DIM + MLA_ROPE_DIM) ** -0.5)
    return o.reshape(b, s, MLA_OUT_W)

def chunkwise_retention(q, k, v):
    b, s, h, d = q.shape
    n = s // RET_CHUNK
    log_g = jnp.log(1.0 - 2.0 ** (-5.0 - jnp.arange(h, dtype=F32)))
    i = jnp.arange(RET_CHUNK, dtype=F32)
    diff = i[:, None] - i[None, :]
    intra = jnp.where(diff >= 0, jnp.exp(jnp.maximum(diff, 0.0)[None] * log_g[:, None, None]), 0.0)
    read_decay = jnp.exp((i + 1.0)[None, :] * log_g[:, None])[None, :, :, None]
    write_decay = jnp.exp((RET_CHUNK - 1.0 - i)[None, :] * log_g[:, None])[None, :, :, None]
    chunk_decay = jnp.exp(RET_CHUNK * log_g)[None, :, None, None]

    def to_chunks(a):
        return a.reshape(b, n, RET_CHUNK, h, d).transpose(1, 0, 3, 2, 4)

    def step(state, xs):
        qc, kc, vc = xs
        sc = jnp.einsum('bhid,bhjd->bhij', qc, kc) * intra
        o = jnp.einsum('bhij,bhjd->bhid', sc, vc) + jnp.einsum('bhid,bhde->bhie', qc, state) * read_decay
        state = state * chunk_decay + jnp.einsum('bhjd,bhje->bhde', kc * write_decay, vc)
        return state, o

    state0 = jnp.zeros((b, h, d, d), F32)
    _, outs = lax.scan(step, state0, (to_chunks(q), to_chunks(k), to_chunks(v)))
    return outs.transpose(1, 0, 3, 2, 4).reshape(b, s, h, d)

def retention_mixer(q, k, v, gate, gn_gain, cos, sin):
    b, s, _ = q.shape
    h, d = RET_HEADS, HEAD_DIM
    q = apply_rope(q.reshape(b, s, h, d), cos, sin).astype(F32)
    k = apply_rope(k.reshape(b, s, h, d), cos, sin).astype(F32) * (d ** -0.5)
    v = v.reshape(b, s, h, d).astype(F32)
    o = chunkwise_retention(q, k, v)
    mu = jnp.mean(o, axis=-1, keepdims=True)
    var = jnp.mean(jnp.square(o - mu), axis=-1, keepdims=True)
    o = (o - mu) * lax.rsqrt(var + NORM_EPS) * gn_gain.astype(F32)
    return jax.nn.silu(gate.astype(F32)) * o.reshape(b, s, h * d)

def first_inputs(seed: int = 0) -> dict:
    key = jax.random.key(seed)
    ks = jax.random.split(key, 24)

    def nrm(k, shape, scale):
        return scale * jax.random.normal(k, shape, F32)

    def gain(k, shape):
        return 1.0 + 0.02 * jax.random.normal(k, shape, F32)

    offs = jax.random.randint(ks[1], (BATCH, 1), 0, 4096)
    positions = (jnp.arange(SEQ, dtype=jnp.int32)[None, :] + offs).astype(jnp.int32)
    return {
        'x': nrm(ks[0], (BATCH, SEQ, D_MODEL), 1.0),
        'positions': positions,
        'ln1_gain': gain(ks[2], (DEPTH, D_MODEL)),
        'w_in': nrm(ks[3], (DEPTH, D_MODEL, N_IN), D_MODEL ** -0.5),
        'cmp_pos_k': nrm(ks[4], (DEPTH, CMP_LEN, HEAD_DIM), 0.1),
        'cmp_w1_k': nrm(ks[5], (DEPTH, CMP_LEN * HEAD_DIM, CMP_HIDDEN), (CMP_LEN * HEAD_DIM) ** -0.5),
        'cmp_w2_k': nrm(ks[6], (DEPTH, CMP_HIDDEN, HEAD_DIM), CMP_HIDDEN ** -0.5),
        'cmp_pos_v': nrm(ks[7], (DEPTH, CMP_LEN, HEAD_DIM), 0.1),
        'cmp_w1_v': nrm(ks[8], (DEPTH, CMP_LEN * HEAD_DIM, CMP_HIDDEN), (CMP_LEN * HEAD_DIM) ** -0.5),
        'cmp_w2_v': nrm(ks[9], (DEPTH, CMP_HIDDEN, HEAD_DIM), CMP_HIDDEN ** -0.5),
        'mla_q_norm': gain(ks[10], (DEPTH, MLA_Q_RANK)),
        'mla_w_uq': nrm(ks[11], (DEPTH, MLA_Q_RANK, MLA_HEADS * (MLA_NOPE_DIM + MLA_ROPE_DIM)), MLA_Q_RANK ** -0.5),
        'mla_kv_norm': gain(ks[12], (DEPTH, MLA_KV_RANK)),
        'mla_w_ukv': nrm(ks[13], (DEPTH, MLA_KV_RANK, MLA_HEADS * (MLA_NOPE_DIM + MLA_V_DIM)), MLA_KV_RANK ** -0.5),
        'ret_gn_gain': gain(ks[14], (DEPTH, RET_HEADS, HEAD_DIM)),
        'w_out': nrm(ks[15], (DEPTH, MIX_WIDTH, D_MODEL), MIX_WIDTH ** -0.5),
        'ln2_gain': gain(ks[16], (DEPTH, D_MODEL)),
        'w_up': nrm(ks[17], (DEPTH, D_MODEL, D_FF), D_MODEL ** -0.5),
        'w_down': nrm(ks[18], (DEPTH, D_FF, D_MODEL), D_FF ** -0.5),
        'final_gain': gain(ks[19], (D_MODEL,)),
    }

def first_block(x, positions, ln1_gain, w_in, cmp_pos_k, cmp_w1_k, cmp_w2_k, cmp_pos_v, cmp_w1_v, cmp_w2_v,
              mla_q_norm, mla_w_uq, mla_kv_norm, mla_w_ukv, ret_gn_gain, w_out, ln2_gain, w_up, w_down,
              final_gain):
    b, s, _ = x.shape
    cos_p, sin_p = rope_tables(positions, PARTIAL_ROPE_DIM, ROPE_THETA)
    cos_m, sin_m = rope_tables(positions, MLA_ROPE_DIM, ROPE_THETA)
    cos_r, sin_r = rope_tables(positions, HEAD_DIM, RET_THETA)
    offsets = in_offsets()
    for l in range(DEPTH):
        h = rms_norm(x, ln1_gain[l])
        proj = h @ w_in[l]
        (nsa_q, k_cmp, v_cmp, k_slc, v_slc, k_win, v_win, nsa_gate,
         mla_cq, mla_ckv, mla_kpe, ret_q, ret_k, ret_v, ret_gate) = jnp.split(proj, offsets, axis=-1)

        def kv_heads(a):
            return a.reshape(b, s, NSA_KV_GROUPS, HEAD_DIM)

        o_nsa = nsa_mixer(
            partial_rope(nsa_q.reshape(b, s, NSA_HEADS, HEAD_DIM), cos_p, sin_p),
            partial_rope(kv_heads(k_cmp), cos_p, sin_p), kv_heads(v_cmp),
            partial_rope(kv_heads(k_slc), cos_p, sin_p), kv_heads(v_slc),
            partial_rope(kv_heads(k_win), cos_p, sin_p), kv_heads(v_win),
            nsa_gate.reshape(b, s, NSA_HEADS, N_BRANCH),
            cmp_pos_k[l], cmp_w1_k[l], cmp_w2_k[l], cmp_pos_v[l], cmp_w1_v[l], cmp_w2_v[l])
        o_mla = mla_mixer(mla_cq, mla_ckv, mla_kpe, mla_q_norm[l], mla_w_uq[l], mla_kv_norm[l], mla_w_ukv[l],
                          cos_m, sin_m)
        o_ret = retention_mixer(ret_q, ret_k, ret_v, ret_gate, ret_gn_gain[l], cos_r, sin_r)
        mixed = jnp.concatenate([o_nsa.astype(x.dtype), o_mla.astype(x.dtype), o_ret.astype(x.dtype)], axis=-1)
        x = x + mixed @ w_out[l]
        h = rms_norm(x, ln2_gain[l])
        x = x + jnp.square(jax.nn.relu(h @ w_up[l])) @ w_down[l]
    return rms_norm(x, final_gain)


POOL_WIDTH = D_MODEL // 4
POOL_WINDOWS = (2, 4, 8, 16)
POOL_GROUPS = len(POOL_WINDOWS)
POOL_GROUP_DIM = POOL_WIDTH // POOL_GROUPS
CONV_WIDTH = D_MODEL // 4
CONV_K = 3
ATTN_HEADS = 8
ATTN_WIDTH = ATTN_HEADS * HEAD_DIM
ROPE_DIM = HEAD_DIM // 4
MOBA_BLOCK = 256
MOBA_TOPK = 3
Q_CHUNK = 32
IN_WIDTH = POOL_WIDTH + 3 * CONV_WIDTH + 3 * ATTN_WIDTH + N_BRANCH * D_MODEL
D_FF_2 = -(-8 * D_MODEL // (3 * 256)) * 256
EPS = 1e-6
NEG = -1e30
POS_OFFSET_MAX = 1024


def rmsnorm(x, w):
    xf = x.astype(jnp.float32)
    xf = xf * lax.rsqrt(jnp.mean(xf * xf, axis=-1, keepdims=True) + EPS)
    return xf.astype(x.dtype) * w

def rotary_tables(positions):
    freqs = ROPE_THETA ** (-jnp.arange(0, ROPE_DIM, 2, dtype=jnp.float32) / ROPE_DIM)
    ang = positions.astype(jnp.float32)[..., None] * freqs
    return jnp.cos(ang), jnp.sin(ang)

def apply_partial_rope(x, cos, sin):
    half = ROPE_DIM // 2
    xr = x[..., :ROPE_DIM].astype(jnp.float32)
    x1, x2 = xr[..., :half], xr[..., half:]
    c = cos[:, :, None, :]
    s = sin[:, :, None, :]
    rot = jnp.concatenate([x1 * c - x2 * s, x2 * c + x1 * s], axis=-1).astype(x.dtype)
    return jnp.concatenate([rot, x[..., ROPE_DIM:]], axis=-1)

def pool_mixer(u, pool_w, pool_scale):
    B, S, _ = u.shape
    uf = u.astype(jnp.float32)
    cs = jnp.pad(jnp.cumsum(uf, axis=1), ((0, 0), (1, 0), (0, 0)))
    t = jnp.arange(S)
    outs = []
    for g, w in enumerate(POOL_WINDOWS):
        sl = slice(g * POOL_GROUP_DIM, (g + 1) * POOL_GROUP_DIM)
        lo = jnp.maximum(t + 1 - w, 0)
        cs_g = cs[..., sl]
        window_sum = cs_g[:, 1:] - jnp.take(cs_g, lo, axis=1)
        count = (t + 1 - lo).astype(jnp.float32)[None, :, None]
        outs.append(window_sum / count - uf[..., sl])
    pooled = jnp.concatenate(outs, axis=-1).astype(u.dtype).reshape(B, S, POOL_GROUPS, POOL_GROUP_DIM)
    y = jnp.einsum('bsgi,gio->bsgo', pooled, pool_w).reshape(B, S, POOL_WIDTH)
    return y * pool_scale

def causal_short_conv(u, conv_w):
    C = u.shape[-1]
    return lax.conv_general_dilated(
        u, conv_w[:, None, :], window_strides=(1,), padding=((CONV_K - 1, 0),),
        dimension_numbers=('NWC', 'WIO', 'NWC'), feature_group_count=C)

def moba_attention(q, k, v):
    B, H, S, hd = q.shape
    nb = -(-S // MOBA_BLOCK)
    pad = nb * MOBA_BLOCK - S
    kb = jnp.pad(k, ((0, 0), (0, 0), (0, pad), (0, 0))).reshape(B, H, nb, MOBA_BLOCK, hd)
    vb = jnp.pad(v, ((0, 0), (0, 0), (0, pad), (0, 0))).reshape(B, H, nb, MOBA_BLOCK, hd)
    kmean = jnp.mean(kb.astype(jnp.float32), axis=3)
    n_sel = max(1, min(MOBA_TOPK, nb - 1))
    nc = S // Q_CHUNK
    q_chunks = q.reshape(B, H, nc, Q_CHUNK, hd).transpose(2, 0, 1, 3, 4)
    starts = jnp.arange(nc, dtype=jnp.int32) * Q_CHUNK
    scale = 1.0 / math.sqrt(hd)
    gather_blocks = jax.vmap(jax.vmap(lambda blocks, ix: blocks[ix]))

    def one_chunk(args):
        q_i, start = args
        qpos = start + jnp.arange(Q_CHUNK, dtype=jnp.int32)
        blk = start // MOBA_BLOCK
        gate = jnp.einsum('bhqd,bhnd->bhqn', q_i.astype(jnp.float32), kmean)
        past = jnp.arange(nb) < blk
        gate = jnp.where(past, gate, NEG)
        _, idx = lax.top_k(gate, n_sel)
        valid = idx < blk
        k_sel = gather_blocks(kb, idx)
        v_sel = gather_blocks(vb, idx)
        s_sel = jnp.einsum('bhqd,bhqjkd->bhqjk', q_i, k_sel).astype(jnp.float32) * scale
        s_sel = jnp.where(valid[..., None], s_sel, NEG).reshape(B, H, Q_CHUNK, n_sel * MOBA_BLOCK)
        k_own = lax.dynamic_index_in_dim(kb, blk, axis=2, keepdims=False)
        v_own = lax.dynamic_index_in_dim(vb, blk, axis=2, keepdims=False)
        s_own = jnp.einsum('bhqd,bhkd->bhqk', q_i, k_own).astype(jnp.float32) * scale
        kpos = blk * MOBA_BLOCK + jnp.arange(MOBA_BLOCK, dtype=jnp.int32)
        s_own = jnp.where(kpos[None, :] <= qpos[:, None], s_own, NEG)
        p = jax.nn.softmax(jnp.concatenate([s_sel, s_own], axis=-1), axis=-1).astype(v.dtype)
        p_sel = p[..., :n_sel * MOBA_BLOCK].reshape(B, H, Q_CHUNK, n_sel, MOBA_BLOCK)
        p_own = p[..., n_sel * MOBA_BLOCK:]
        return (jnp.einsum('bhqjk,bhqjkd->bhqd', p_sel, v_sel)
                + jnp.einsum('bhqk,bhkd->bhqd', p_own, v_own))

    out = lax.map(one_chunk, (q_chunks, starts))
    return out.transpose(1, 2, 0, 3, 4).reshape(B, H, S, hd)

def hybrid_layer(x, c_act, cos, sin, norm1_w, norm2_w, w_ada, b_ada, w_in, pool_w, pool_scale,
                 conv_w, q_norm_w, k_norm_w, p_pool, p_conv, p_attn, w_out, w_gate, w_up, w_down):
    B, S, D = x.shape
    mod = (c_act @ w_ada + b_ada)[:, None, :]
    sh1, sc1, g1, sh2, sc2, g2 = jnp.split(mod, 6, axis=-1)
    h = rmsnorm(x, norm1_w) * (1 + sc1) + sh1
    u = h @ w_in
    widths = [POOL_WIDTH, CONV_WIDTH, CONV_WIDTH, CONV_WIDTH, ATTN_WIDTH, ATTN_WIDTH, ATTN_WIDTH]
    offsets = [int(o) for o in np.cumsum(widths)]
    u_pool, u_conv, b_conv, c_conv, q, k, v, gate_logits = jnp.split(u, offsets, axis=-1)
    y_pool = pool_mixer(u_pool, pool_w, pool_scale)
    y_conv = b_conv * causal_short_conv(c_conv * u_conv, conv_w)
    q = apply_partial_rope(rmsnorm(q.reshape(B, S, ATTN_HEADS, HEAD_DIM), q_norm_w), cos, sin)
    k = apply_partial_rope(rmsnorm(k.reshape(B, S, ATTN_HEADS, HEAD_DIM), k_norm_w), cos, sin)
    v = v.reshape(B, S, ATTN_HEADS, HEAD_DIM)
    o = moba_attention(q.transpose(0, 2, 1, 3), k.transpose(0, 2, 1, 3), v.transpose(0, 2, 1, 3))
    y_attn = o.transpose(0, 2, 1, 3).reshape(B, S, ATTN_WIDTH)
    gates = jax.nn.sigmoid(gate_logits).reshape(B, S, N_BRANCH, D)
    merged = (gates[:, :, 0] * (y_pool @ p_pool)
              + gates[:, :, 1] * (y_conv @ p_conv)
              + gates[:, :, 2] * (y_attn @ p_attn))
    x = x + g1 * (merged @ w_out)
    h2 = rmsnorm(x, norm2_w) * (1 + sc2) + sh2
    x = x + g2 * ((jax.nn.silu(h2 @ w_gate) * (h2 @ w_up)) @ w_down)
    return x

def second_inputs(seed: int = 0) -> dict:
    key = jax.random.key(seed)
    ks = jax.random.split(key, 24)
    L = DEPTH

    def nrm(k, shape, fan_in, gain=1.0):
        return gain * fan_in ** -0.5 * jax.random.normal(k, shape, jnp.float32)

    def gain_init(k, shape):
        return 1.0 + 0.1 * jax.random.normal(k, shape, jnp.float32)

    x = jax.random.normal(ks[0], (BATCH, SEQ, D_MODEL), jnp.float32)
    c = jax.random.normal(ks[1], (BATCH, D_MODEL), jnp.float32)
    positions = (jnp.arange(SEQ, dtype=jnp.int32)[None, :]
                 + jax.random.randint(ks[2], (BATCH, 1), 0, POS_OFFSET_MAX, dtype=jnp.int32))
    return {
        "x": x,
        "c": c,
        "positions": positions,
        "norm1_w": gain_init(ks[3], (L, D_MODEL)),
        "norm2_w": gain_init(ks[4], (L, D_MODEL)),
        "w_ada": nrm(ks[5], (L, D_MODEL, 6 * D_MODEL), D_MODEL, 0.5),
        "b_ada": 0.02 * jax.random.normal(ks[6], (L, 6 * D_MODEL), jnp.float32),
        "w_in": nrm(ks[7], (L, D_MODEL, IN_WIDTH), D_MODEL),
        "pool_w": nrm(ks[8], (L, POOL_GROUPS, POOL_GROUP_DIM, POOL_GROUP_DIM), POOL_GROUP_DIM),
        "pool_scale": gain_init(ks[9], (L, POOL_WIDTH)),
        "conv_w": nrm(ks[10], (L, CONV_K, CONV_WIDTH), CONV_K),
        "q_norm_w": gain_init(ks[11], (L, HEAD_DIM)),
        "k_norm_w": gain_init(ks[12], (L, HEAD_DIM)),
        "p_pool": nrm(ks[13], (L, POOL_WIDTH, D_MODEL), POOL_WIDTH),
        "p_conv": nrm(ks[14], (L, CONV_WIDTH, D_MODEL), CONV_WIDTH),
        "p_attn": nrm(ks[15], (L, ATTN_WIDTH, D_MODEL), ATTN_WIDTH),
        "w_out": nrm(ks[16], (L, D_MODEL, D_MODEL), D_MODEL),
        "w_gate": nrm(ks[17], (L, D_MODEL, D_FF_2), D_MODEL),
        "w_up": nrm(ks[18], (L, D_MODEL, D_FF_2), D_MODEL),
        "w_down": nrm(ks[19], (L, D_FF_2, D_MODEL), D_FF_2),
    }

def second_block(x, c, positions, norm1_w, norm2_w, w_ada, b_ada, w_in, pool_w, pool_scale, conv_w,
              q_norm_w, k_norm_w, p_pool, p_conv, p_attn, w_out, w_gate, w_up, w_down):
    c_act = jax.nn.silu(c)
    cos, sin = rotary_tables(positions)
    for l in range(DEPTH):
        x = hybrid_layer(x, c_act, cos, sin, norm1_w[l], norm2_w[l], w_ada[l], b_ada[l], w_in[l],
                         pool_w[l], pool_scale[l], conv_w[l], q_norm_w[l], k_norm_w[l],
                         p_pool[l], p_conv[l], p_attn[l], w_out[l], w_gate[l], w_up[l], w_down[l])
    return x


def setup_inputs(seed=0):
    out = dict(first_inputs(seed))
    for name, value in second_inputs(seed + 1).items():
        if name != "x":
            out[name + "_2"] = value
    return out


def reference(
    x, positions, ln1_gain, w_in, cmp_pos_k, cmp_w1_k, cmp_w2_k, cmp_pos_v, cmp_w1_v, cmp_w2_v,
    mla_q_norm, mla_w_uq, mla_kv_norm, mla_w_ukv, ret_gn_gain, w_out, ln2_gain, w_up, w_down,
    final_gain, c_2, positions_2, norm1_w_2, norm2_w_2, w_ada_2, b_ada_2, w_in_2, pool_w_2,
    pool_scale_2, conv_w_2, q_norm_w_2, k_norm_w_2, p_pool_2, p_conv_2, p_attn_2, w_out_2,
    w_gate_2, w_up_2, w_down_2,
):
    x = first_block(
        x, positions, ln1_gain, w_in, cmp_pos_k, cmp_w1_k, cmp_w2_k, cmp_pos_v, cmp_w1_v,
        cmp_w2_v, mla_q_norm, mla_w_uq, mla_kv_norm, mla_w_ukv, ret_gn_gain, w_out, ln2_gain,
        w_up, w_down, final_gain,
    )
    return second_block(
        x, c_2, positions_2, norm1_w_2, norm2_w_2, w_ada_2, b_ada_2, w_in_2, pool_w_2,
        pool_scale_2, conv_w_2, q_norm_w_2, k_norm_w_2, p_pool_2, p_conv_2, p_attn_2, w_out_2,
        w_gate_2, w_up_2, w_down_2,
    )


_drawn_inputs = setup_inputs


def setup_inputs(seed=0):
    import zlib

    import numpy as np

    out = dict(_drawn_inputs(seed))
    spreads = {}
    factors = {'cmp_pos_k': 8.0,
     'mla_q_norm': 8.0,
     'mla_kv_norm': 8.0,
     'ret_gn_gain': 6.011,
     'pool_scale_2': 3.314,
     'q_norm_w_2': 8.0,
     'k_norm_w_2': 8.0}
    for name, (base, spread) in spreads.items():
        noise = np.random.default_rng([zlib.crc32(name.encode()), seed]).standard_normal(out[name].shape)
        drawn = base * np.exp(spread * noise) if base else spread * noise
        out[name] = __import__('jax').numpy.asarray(drawn.astype(out[name].dtype))
    for name, factor in factors.items():
        out[name] = (out[name] * factor).astype(out[name].dtype)
    return out
```

```python
import concourse.bass as bass
from concourse import mybir
from contextlib import ExitStack
import numpy as np

F32 = mybir.dt.float32
I32 = mybir.dt.int32
ALU = mybir.AluOpType
ACT = mybir.ActivationFunctionType
AX = mybir.AxisListType

P = 128
D = 1024
S = 256
TT = S // P
KC = D // P
LAYERS = 2
HD = 64
NSA_HEADS, REP, N_BRANCH = 6, 3, 3
CMP_LEN, CMP_STRIDE = 32, 16
N_CMP = (S - CMP_LEN) // CMP_STRIDE + 1
NP16 = 16
MLA_HEADS, MLA_Q, MLA_PE = 5, 96, 32
RET_HEADS = 5
D_FF1 = 4096
F1 = D_FF1 // P
ATTN_HEADS = 8
D_FF2 = 2816
F2 = D_FF2 // P
GATES = 3 * KC
EPS = 1e-6
NEG = -1e30
GELU_C = 0.7978845608028654

TILE = 2048
RING = 9
assert KC * 256 == TILE

UNITS1 = ["q0", "q1", "q2", "ks", "kw", "kc", "vc", "cq0", "cq1", "ckv", "kpe", "rqa", "rqb", "rka", "rkb", "r4"]
ROPED1 = ["q0", "q1", "q2", "ks", "kw", "kc", "kpe", "rqa", "rqb", "rka", "rkb", "r4"]
UNITS2 = [f"q{b}" for b in range(4)] + [f"k{b}" for b in range(4)]
LATER2 = ["pa", "pb", "cua", "cub", "cba", "cbb", "cca", "ccb"]
MIXERS = ["P", "C", "A"]
VS, VW, GT, RV, RG = 0, 128, 256, 274, 594
TM1 = 914
TM_W = [256, 256, 256, TM1 - 768]

TILES1 = (
    [(UNITS1[2 * i], UNITS1[2 * i + 1]) for i in range(8)]
    + [("tm", j) for j in range(4)]
    + [("cmpk", 0), ("cmpv", 0), ("small", 0)]
    + [("wout", j) for j in range(4)]
    + [("up", j) for j in range(F1 // 2)]
    + [("down", j) for j in range(2 * KC)]
)
TILES2 = (
    [("ada", j) for j in range(24)]
    + [(UNITS2[2 * i], UNITS2[2 * i + 1]) for i in range(4)]
    + [("v", j) for j in range(2)]
    + [(LATER2[2 * i], LATER2[2 * i + 1]) for i in range(4)]
    + [("gate", j) for j in range(GATES // 2)]
    + [("ppool", 0), ("pconv", 0), ("pattn", 0), ("pattn", 1)]
    + [("wout", j) for j in range(4)]
    + [("gu", j) for j in range(F2)]
    + [("down", j) for j in range(KC * F2 // 16)]
)
T1, T2 = len(TILES1), len(TILES2)

HEADS1 = [("slc", h) for h in range(NSA_HEADS)] + [("win", h) for h in range(NSA_HEADS)] \
    + [("mla", h) for h in range(MLA_HEADS)]
NH1, NH2 = len(HEADS1), ATTN_HEADS


def order1():
    out = ["ss1"]
    for i, u in enumerate(UNITS1):
        out.append(u)
        if i >= 1 and UNITS1[i - 1] in ROPED1:
            out.append("rot_" + UNITS1[i - 1])
    out += ["ssq", "ssk"]
    for j in range(4):
        for t in range(TT):
            out.append(f"tm{j}{t}")
            if (j, t) == (0, 0):
                out.append("rot_r4")
    out += ["hidk", "hidv"]
    for h in range(MLA_HEADS):
        out.append(f"mq{h}")
        if h >= 1:
            out.append(f"rot_mq{h - 1}")
    out.append(f"rot_mq{MLA_HEADS - 1}")
    out += [f"mk{h}" for h in range(MLA_HEADS)] + [f"mv{t}" for t in range(TT)]
    out += ["kcc", "vbd", "cs0", "cs1", "ct", "co0", "co1"]
    for h in range(RET_HEADS + 1):
        if h < RET_HEADS:
            out.append(f"rs{h}")
        if h >= 1:
            out.append(f"ro{h - 1}")
    out += [f"mt{c}" for c in range(KC)] + [f"wo{n}" for n in range(KC)] + ["ss2"]
    out += [f"up{n}" for n in range(F1)] + [f"dn{n}" for n in range(KC)]
    return out


def gates_at(i):
    steps = NH2 + 2
    return range(GATES * i // steps, GATES * (i + 1) // steps)


def order2():
    out = [f"ada{j}" for j in range(4)] + ["ss1"] + [f"ada{j}" for j in range(4, 8)]
    for b in range(len(UNITS2) + 3):
        if b < 8:
            out.append(UNITS2[b])
        if 1 <= b < 9:
            out.append("ss_" + UNITS2[b - 1])
        if b >= 3:
            out.append("rot_" + UNITS2[b - 3])
    out += [f"v{j}{t}" for j in range(2) for t in range(TT)] + LATER2 + ["pw0", "pw1"]
    for i in range(NH2 + 2):
        out += [f"g{n}" for n in gates_at(i)]
    out += [f"yt{c}" for c in range(4)]
    for n in range(KC):
        out += [f"{m}{n}" for m in MIXERS]
    out += [f"wo{n}" for n in range(KC)] + ["ss2"]
    for n in range(F2):
        out += [f"gt{n}", f"up{n}"]
    return out + [f"dn{n}" for n in range(KC)]


BANKS = 4


class Turns:

    def __init__(self, names, full, drained):
        self.names, self.base, self.free_base = names, full, drained
        self.at = {n: i for i, n in enumerate(names)}
        assert len(self.at) == len(names)
        self.total = len(names)
        self.uses = [len([i for i in range(self.total) if i % BANKS == b]) for b in range(BANKS)]

    def bank(self, name):
        return self.at[name] % BANKS

    def full(self, name, layer):
        return layer * self.total + (self.base + self.at[name] + 1)

    def free(self, name, layer):
        b = self.bank(name)
        return layer * self.uses[b] + (self.free_base[b] + self.at[name] // BANKS)

    def drained(self, name, layer):
        return self.free(name, layer) + 1

    def after(self, layers):
        return self.base + layers * self.total, [f + layers * u for f, u in zip(self.free_base, self.uses)]


A1 = Turns(order1(), 0, [1] * BANKS)
AF = Turns(["ssf"], *A1.after(LAYERS))
A2 = Turns(order2(), *AF.after(1))

CONSTS = {}


def _place(table, items):
    at = 0
    for name, width in items:
        table[name] = (at, width)
        at += width
    return at


N_CONST = _place(CONSTS, [("ident", 128), ("rotp", 128), ("rotm", 128), ("rotr", 128), ("half", 128), ("ones", 128),
                          ("mask", 384), ("cmask", 192), ("ckeep", 192), ("bmask", 6), ("inv", 4),
                          ("decay", RET_HEADS * S), ("invc", 2 * S)])
VEC1, VEC2 = {}, {}
N_V1 = _place(VEC1, [("ln1", 8), ("ln2", 8), ("qn", 2), ("kvn", 1), ("posk", 16), ("posv", 16), ("gn", 320)])
N_V2 = _place(VEC2, [("n1", 8), ("n2", 8), ("bada", 48), ("pscale", 2), ("conv", 6), ("qn", 1), ("kn", 1), ("poolw", 256)])
N_ONCE = 16
UQ, UKV, W2K, W2V = 0, 960, 1600, 1728


def constants():
    c = np.zeros((P, N_CONST), np.float32)

    def put(name, a):
        at, w = CONSTS[name]
        c[:a.shape[0], at:at + w] = a.reshape(a.shape[0], w)

    def rotation(starts, half):
        m = np.zeros((P, P), np.float32)
        for s in starts:
            for i in range(half):
                m[s + half + i, s + i] = -1.0
                m[s + i, s + half + i] = 1.0
        return m

    i = np.arange(P)
    put("ident", np.eye(P, dtype=np.float32))
    put("rotp", rotation((0, 64), 8))
    put("rotm", rotation((64,), 16))
    put("rotr", rotation((0, 64), 32))
    put("half", (i[:, None] // HD == i[None, :] // HD).astype(np.float32))
    put("ones", np.ones((P, P), np.float32))
    tri = np.where(i[None, :] > i[:, None], NEG, 0.0)
    put("mask", np.concatenate([tri, np.zeros((P, P)), tri], axis=1))
    n = np.arange(NP16)
    t = (np.arange(TT)[None, :] * P + i[:, None])[:, :, None]
    seen = (n * CMP_STRIDE + CMP_LEN - 1 <= t) & (n < N_CMP)
    seen = np.broadcast_to(seen[:, :, None, :], (P, TT, NSA_HEADS, NP16))
    put("cmask", np.where(seen, 0.0, NEG).reshape(P, 192))
    put("ckeep", seen.astype(np.float32).reshape(P, 192))
    r = np.arange(NSA_HEADS * NP16)
    put("bmask", ((r[:, None] // NP16 == np.arange(NSA_HEADS)[None, :]) & (r[:, None] % NP16 < N_CMP)).astype(np.float32))
    inv = np.zeros((P, 4), np.float32)
    e16, e32, e64 = (np.arange(0, d, 2, dtype=np.float32) / np.float32(d) for d in (16, 32, 64))
    power = lambda base, e: np.power(base, e.astype(np.float64)).astype(np.float32)
    one = np.float32(1.0)
    for s in (0, 64):
        inv[s:s + 16, 0] = np.tile(one / power(5e5, e16), 2)
        inv[s:s + 64, 2] = np.tile(one / power(1e4, e64), 2)
        inv[s:s + 16, 3] = np.tile(power(5e5, -e16), 2)
    inv[64:96, 1] = np.tile(one / power(5e5, e32), 2)
    put("inv", inv)
    g = np.log(1.0 - 2.0 ** (-5.0 - np.arange(RET_HEADS)))
    diff = (np.arange(S)[None, :] - i[:, None])[:, None, :]
    put("decay", np.where(diff >= 0, np.exp(np.maximum(diff, 0) * g[None, :, None]), 0.0) * HD ** -0.5)
    win = np.array([[2, 8], [4, 16]])
    w = win[i // HD]
    put("invc", 1.0 / np.minimum(np.arange(S)[None, None, :] + 1, w[:, :, None]))
    return c


def trn_kernel(nc, consts, vec1, vec2, once, pos, xin, stream, out):
    ctx = ExitStack()
    with ctx:
        def sb(name, shape, dt=F32):
            return ctx.enter_context(nc.sbuf_tensor(name, shape, dt))

        def bank(name):
            return ctx.enter_context(nc.psum_tensor(name, [P, 512], F32))

        def sem(name):
            return ctx.enter_context(nc.semaphore(name))

        cst = sb("cst", [P, N_CONST])
        v1all = sb("v1all", [P, LAYERS, N_V1])
        v1 = sb("v1", [P, N_V1])
        v2all = sb("v2all", [P, LAYERS, N_V2])
        v2 = sb("v2", [P, N_V2])
        onc = sb("onc", [P, N_ONCE])
        trig = sb("trig", [P, 2, 4, S])
        ring = sb("ring", [P, RING, TILE])
        x = sb("x", [P, KC, S])
        h = sb("h", [P, KC, S])
        big = sb("big", [P, 32, S])
        nv = sb("nv", [P, 2, S])
        ny = sb("ny", [P, 2, S])
        nt = sb("nt", [P, S])
        rstd = sb("rstd", [P, S])
        tcs = sb("tcs", [P, 2, S])
        tss = sb("tss", [P, 2, S])
        tc, ts = tcs[:, 0, :], tss[:, 0, :]
        WORK = 9500
        work = sb("work", [P, WORK])
        cursor = [0]

        def piece(*shape):
            n = 1
            for s_ in shape:
                n *= s_
            a = work[:, cursor[0]:cursor[0] + n]
            cursor[0] += n
            assert cursor[0] <= WORK
            if len(shape) == 2:
                a = a.rearrange("p (a b) -> p a b", a=shape[0])
            elif len(shape) == 3:
                a = a.rearrange("p (a b c) -> p a b c", a=shape[0], b=shape[1])
            return a

        rope1 = piece(11, S)
        tokm = piece(TT, 1024)
        qm = piece(MLA_HEADS, S)
        km = piece(MLA_HEADS, S)
        vm = piece(TT, 320)
        hid = piece(2, 32)
        gel = piece(3, 64)
        kcT = piece(NP16)
        grep = piece(2, 96)
        vbd = piece(384)
        pc = piece(192)
        pcT = piece(S)
        cst12 = piece(3, 12)
        gate = piece(TT, 18)
        gnst = piece(6, 10)
        cursor[0] = 0
        qk2 = piece(8, S)
        vv = piece(TT, 512)
        ya = piece(TT, 512)
        yaT = piece(4, S)
        up_ = piece(2, 16 + S)
        sw = piece(4, 16 + S)
        yp = piece(2, S)
        yc = piece(2, S)
        cu = piece(2, S)
        cb = piece(2, S)
        cv = piece(2, 2 + S)
        cursor[0] = 0
        merged = piece(KC, S)
        mod = sb("mod", [P, 48])
        mods = sb("mods", [P, 2, KC])
        csil = sb("csil", [P, 3, KC])
        sm = sb("sm", [P, 2, 384])
        pr = sb("pr", [P, 2, 384])
        prT = sb("prT", [P, 2, 384])
        nmax = sb("nmax", [P, NH1, 2])
        psumv = sb("psumv", [P, NH1, 2])
        coef = sb("coef", [P, NH1, 2])
        sq = big[:, 24:32, :]
        raw = big[:, 0:16, :]
        mixed = big[:, 16:24, :].rearrange("p a s -> p (a s)").rearrange("p (t f) -> p t f", t=TT)
        fk = [big[:, 16 + 2 * j:18 + 2 * j, :].rearrange("p a s -> p (a s)")[:, 0:480]
              .rearrange("p (m g n) -> p m g n", m=16, g=2) for j in range(2)]
        xk = [big[:, 20 + 2 * j:22 + 2 * j, :] for j in range(2)]
        cqn = big[:, 12:15, :]

        acc = [bank(f"acc{i}") for i in range(BANKS)]
        ps_s = [bank(f"ps_s{i}") for i in range(2)]
        ps_t = bank("ps_t")
        ps_o = bank("ps_o")

        def C(name, rows=P):
            at, w = CONSTS[name]
            return cst[0:rows, at:at + w]

        def V1(name, i=None):
            at, w = VEC1[name]
            return v1[:, at:at + w] if i is None else v1[:, at + i:at + i + 1]

        def V2(name, i=None):
            at, w = VEC2[name]
            return v2[:, at:at + w] if i is None else v2[:, at + i:at + i + 1]

        decay = C("decay").rearrange("p (h s) -> p h s", h=RET_HEADS)
        invc = C("invc").rearrange("p (b s) -> p b s", b=2)

        inputs_in = sem("inputs_in")
        got = [sem(f"got{i}") for i in range(RING)]
        acc_full = sem("acc_full")
        acc_drained = [sem(f"acc_drained{i}") for i in range(BANKS)]
        x_ready = sem("x_ready")
        vec_ready = sem("vec_ready")
        trig_arg = sem("trig_arg")
        trig_ready = sem("trig_ready")
        sq_ready = sem("sq_ready")
        y_ready = sem("y_ready")
        h_ready = sem("h_ready")
        h_pre = sem("h_pre")
        rope_ready = sem("rope_ready")
        lat_ready = sem("lat_ready")
        latsq = sem("latsq")
        f_ready = sem("f_ready")
        xk_ready = sem("xk_ready")
        ge = sem("ge")
        hid_ready = sem("hid_ready")
        gel_ready = sem("gel_ready")
        grep_ready = sem("grep_ready")
        km_ready = sem("km_ready")
        kcT_ready = sem("kcT_ready")
        vbd_ready = sem("vbd_ready")
        csub = sem("csub")
        cexp = sem("cexp")
        pc_ready = sem("pc_ready")
        gexp = sem("gexp")
        gate_ready = sem("gate_ready")
        rw_ready = sem("rw_ready")
        gn_v = sem("gn_v")
        gn_y = sem("gn_y")
        mixed_ready = sem("mixed_ready")
        mixT_ready = sem("mixT_ready")
        a_ready = sem("a_ready")
        s_full, s_drained = sem("s_full"), sem("s_drained")
        nmax_ready, p_ready = sem("nmax_ready"), sem("p_ready")
        pt_full, pt_copied = sem("pt_full"), sem("pt_copied")
        o_full, o_drained = sem("o_full"), sem("o_drained")
        csil_e, csil_ready = sem("csil_e"), sem("csil_ready")
        mod_ready = sem("mod_ready")
        raw2_sq = sem("raw2_sq")
        qn2_ready = sem("qn2_ready")
        qk2_ready = sem("qk2_ready")
        pool_in = sem("pool_in")
        pad_ready = sem("pad_ready")
        pooled = sem("pooled")
        yc_ready = sem("yc_ready")
        gsig_e = sem("gsig_e")
        gsig_a = sem("gsig_a")
        gsig = sem("gsig")
        merged_ready = sem("merged_ready")
        ya_ready = sem("ya_ready")
        silu_e = sem("silu_e")
        a2_ready = sem("a2_ready")
        stored = sem("stored")
        dve_step, act_step, pool_step = sem("dve_step"), sem("act_step"), sem("pool_step")

        ROPE1 = {"q0": 0, "q1": 1, "q2": 2, "ks": 3, "kw": 4, "rqa": 5, "rqb": 6, "rka": 7, "rkb": 8}

        def q_nsa(hh):
            g, r = hh // REP, hh % REP
            return slice(64 * g, 64 * g + 64), r

        def ret_q(hh):
            return (slice(64 * (hh % 2), 64 * (hh % 2) + 64), 5 + hh // 2) if hh < 4 else (slice(0, 64), 9)

        def ret_k(hh):
            return (slice(64 * (hh % 2), 64 * (hh % 2) + 64), 7 + hh // 2) if hh < 4 else (slice(0, 64), 10)

        def head1(i):
            kind, hh = HEADS1[i]
            if kind == "mla":
                return qm[0:96, hh, :], km[0:96, hh, :], [vm[:, t, 64 * hh:64 * hh + 64] for t in range(TT)]
            rows, r = q_nsa(hh)
            g = hh // REP
            c = (VS if kind == "slc" else VW) + 64 * g
            return (rope1[rows, r, :], rope1[rows, 3 if kind == "slc" else 4, :],
                    [tokm[:, t, c:c + 64] for t in range(TT)])

        def scale1(i):
            return 96 ** -0.5 if HEADS1[i][0] == "mla" else HD ** -0.5

        def head2(i):
            rows = slice(64 * (i % 2), 64 * (i % 2) + 64)
            return qk2[rows, i // 2, :], qk2[rows, 4 + i // 2, :], [vv[:, t, 64 * i:64 * i + 64] for t in range(TT)]

        X2 = LAYERS * 2 * KC + KC
        X_FINAL = X2 + (2 * LAYERS - 1) * KC
        H2 = LAYERS * 2 * KC
        Q2 = LAYERS * 8 + 4
        Y1, Y2N = 4, 10
        YF, Y2 = LAYERS * Y1, LAYERS * Y1 + 1

        def ro_all(k):
            return big[:, 3 * k:3 * k + 3, :].rearrange("p a s -> p (a s)")[:, 0:640]

        def ro_(hh):
            return ro_all(0).rearrange("p (t f) -> p t f", t=TT)[:, :, 64 * hh:64 * hh + 64]

        def rgx_():
            return ro_all(1).rearrange("p (t f) -> p t f", t=TT)

        block = ctx.enter_context(nc.Block())

        @block.sync
        def _(sp):
            sp.dma_start(x[:], xin).then_inc(inputs_in, 16)
            sp.dma_start(cst[:], consts).then_inc(inputs_in, 16)

            def last_user(tiles, t):
                kind, j = tiles[t]
                one = tiles is TILES1
                if kind == "tm":
                    return f"tm{j}{TT - 1}"
                if kind == "v":
                    return f"v{j}{TT - 1}"
                if kind in ("cmpk", "cmpv"):
                    return "hid" + kind[-1]
                if kind == "small":
                    return "vbd"
                if kind == "wout":
                    return f"wo{2 * j + 1}"
                if kind == "up":
                    return f"up{2 * j + 1}"
                if kind == "gu":
                    return f"up{j}"
                if kind == "down":
                    return f"dn{j // 2}" if one else f"dn{min(KC - 1, (16 * j + 15) // F2)}"
                if kind == "ada":
                    return f"ada{j // 3}"
                if kind == "gate":
                    return f"g{2 * j + 1}"
                if kind in ("ppool", "pconv"):
                    return f"{'PC'[kind == 'pconv']}{KC - 1}"
                if kind == "pattn":
                    return f"A{4 * j + 3}"
                return j

            def load(slot, at):
                sp.dma_start(ring[:, slot, :], stream[at]).then_inc(got[slot], 16)

            def rest(tiles, turns, layer, first):
                for t in range(RING, len(tiles)):
                    sp.wait_ge(acc_full, turns.full(last_user(tiles, t - RING), layer))
                    load(t % RING, first + t)

            def ahead(tiles, turns, layer, first):
                n = len(tiles)
                for s_ in range(RING):
                    t = max(u for u in range(n) if u % RING == s_)
                    sp.wait_ge(acc_full, turns.full(last_user(tiles, t), layer))
                    load(s_, first + n + s_)

            for s_ in range(RING):
                load(s_, s_)
            sp.dma_start(v2all[:], vec2).then_inc(inputs_in, 16)
            with sp.Fori(0, LAYERS) as layer:
                rest(TILES1, A1, layer, layer * T1)
                ahead(TILES1, A1, layer, layer * T1)
            with sp.Fori(0, LAYERS - 1) as layer:
                rest(TILES2, A2, layer, layer * T2 + LAYERS * T1)
                ahead(TILES2, A2, layer, layer * T2 + LAYERS * T1)
            rest(TILES2, A2, LAYERS - 1, (LAYERS - 1) * T2 + LAYERS * T1)
            for c in range(0, KC, 2):
                sp.wait_ge(x_ready, X_FINAL + c + 2)
                sp.dma_start(out[:, c:c + 2, :], x[:, c:c + 2, :]).then_inc(stored, 16)
            sp.wait_ge(stored, 16 * KC // 2)


        @block.tensor
        def _(pe):
            for b in range(BANKS):
                pe.sem_inc(acc_drained[b], 1)
            pe.wait_ge(inputs_in, 16 * 6)

            state = {}

            def enter(turns, layer, tiles, visits_base):
                state.update(turns=turns, layer=layer, next=0, tiles=tiles, visits=visits_base)

            def open_acc(name):
                tn = state["turns"]
                assert tn.names[state["next"]] == name, (tn.names[state["next"]], name)
                state["next"] += 1
                pe.wait_ge(acc_drained[tn.bank(name)], tn.free(name, state["layer"]))
                return acc[tn.bank(name)]

            def tile(kind, j):
                t = state["tiles"].index((kind, j))
                slot = t % RING
                n = len([u for u in range(len(state["tiles"])) if u % RING == slot])
                pe.wait_ge(got[slot], state["layer"] * (16 * n) + 16 * (state["visits"][slot] + t // RING + 1))
                return ring[:, slot, :]

            def project(name, w, rows, rhs, h_base=None):
                a = open_acc(name)
                for c in range(KC):
                    if h_base is not None:
                        pe.wait_ge(h_ready, state["layer"] * (2 * KC) + (h_base + c + 1))
                    last = pe.matmul(a[0:rows, 0:S], w[:, c, :], rhs(c), start=c == 0, stop=c == KC - 1)
                last.then_inc(acc_full, 1)

            def unit(tl, i):
                return tl[:, 1024 * i:1024 * (i + 1)].rearrange("p (c n) -> p c n", c=KC)

            def sum_squares(name, base, sq=sq):
                a = open_acc(name)
                for c in range(KC):
                    if c % 2 == 0:
                        pe.wait_ge(sq_ready, base + c // 2 + 1)
                    last = pe.matmul(a[:, 0:S], C("ones"), sq[:, c, :], start=c == 0, stop=c == KC - 1)
                last.then_inc(acc_full, 1)

            def rotate(name, m, src, rows=slice(0, P)):
                a = open_acc("rot_" + name)
                pe.matmul(a[rows, 0:S], m, src, start=True, stop=True).then_inc(acc_full, 1)

            def drained(name):
                tn = state["turns"]
                pe.wait_ge(acc_drained[tn.bank(name)], tn.drained(name, state["layer"]))

            def attention(head, n, base, filler):
                L = state["layer"]
                for i in range(n + 2):
                    if i < n:
                        q, k, _ = head(i)
                        pe.wait_ge(s_drained, L * n + (base + i + 1))
                        b = ps_s[i % 2]
                        pe.matmul(b[:, 0:P], q[:, 0:P], k[:, 0:P], start=True, stop=True)
                        pe.matmul(b[:, P:3 * P], q[:, P:S], k, start=True, stop=True).then_inc(s_full, 1)
                    if 1 <= i <= n:
                        j = i - 1
                        pe.wait_ge(p_ready, L * n + (base + j + 1))
                        pe.wait_ge(pt_copied, L * n + (base + j + 1))
                        for c in range(3):
                            last = pe.transpose(ps_t[:, c * P:(c + 1) * P], pr[:, j % 2, c * P:(c + 1) * P], C("ident"))
                        last.then_inc(pt_full, 1)
                    if i >= 2:
                        j = i - 2
                        _, _, v = head(j)
                        pe.wait_ge(pt_copied, L * n + (base + j + 2))
                        pe.wait_ge(o_drained, L * n + (base + j + 1))
                        pe.matmul(ps_o[:, 0:HD], prT[:, j % 2, 0:P], v[0], start=True, stop=True)
                        pe.matmul(ps_o[:, HD:2 * HD], prT[:, j % 2, P:2 * P], v[0], start=True, stop=False)
                        pe.matmul(ps_o[:, HD:2 * HD], prT[:, j % 2, 2 * P:3 * P], v[1], start=False, stop=True)\
                            .then_inc(o_full, 1)
                    filler(i)

            pe.sem_inc(s_drained, 2)
            pe.sem_inc(pt_copied, 1)
            pe.sem_inc(o_drained, 1)

            hs = lambda c: h[:, c, :]
            with pe.Fori(0, LAYERS) as L:
                enter(A1, L, TILES1, [0] * RING)
                sum_squares("ss1", L * 8)

                def rot1(u):
                    drained(u)
                    i = UNITS1.index(u)
                    if u == "kpe":
                        rotate(u, C("rotm")[0:96, 0:96], raw[0:96, i, :], slice(0, 96))
                    else:
                        rotate(u, C("rotr" if u[0] == "r" else "rotp"), raw[:, i, :])

                for i, u in enumerate(UNITS1):
                    if i % 2 == 0:
                        tl = tile(u, UNITS1[i + 1])
                    project(u, unit(tl, i % 2), P, hs, 0 if i == 0 else None)
                    if i >= 1 and UNITS1[i - 1] in ROPED1:
                        rot1(UNITS1[i - 1])
                pe.wait_ge(latsq, L * 3 + 2)
                a = open_acc("ssq")
                pe.matmul(a[:, 0:S], C("ones"), sq[:, 0, :], start=True, stop=False)
                pe.matmul(a[:, 0:S], C("ones"), sq[:, 1, :], start=False, stop=True).then_inc(acc_full, 1)
                pe.wait_ge(latsq, L * 3 + 3)
                a = open_acc("ssk")
                pe.matmul(a[:, 0:S], C("ones"), sq[:, 2, :], start=True, stop=True).then_inc(acc_full, 1)
                for j in range(4):
                    tl = tile("tm", j).rearrange("p (c n) -> p c n", c=KC)
                    for t in range(TT):
                        a = open_acc(f"tm{j}{t}")
                        for c in range(KC):
                            last = pe.matmul(a[:, 0:TM_W[j]], h[:, c, t * P:(t + 1) * P], tl[:, c, 0:TM_W[j]],
                                             start=c == 0, stop=c == KC - 1)
                        last.then_inc(acc_full, 1)
                        if (j, t) == (0, 0):
                            rot1("r4")
                for j, kind in enumerate(("k", "v")):
                    tl = tile("cmp" + kind, 0).rearrange("p (m n) -> p m n", m=16)
                    pe.wait_ge(f_ready, L * 2 + (j + 1))
                    a = open_acc("hid" + kind)
                    for m in range(16):
                        last = pe.matmul(a[:, 0:30], tl[:, m, :], fk[j][:, m, :, :].rearrange("p g n -> p (g n)"),
                                         start=m == 0, stop=m == 15)
                    last.then_inc(acc_full, 1)
                tl = tile("small", 0)
                uq = tl[:, UQ:UQ + 960].rearrange("p (c n) -> p c n", c=2)
                pe.wait_ge(lat_ready, L * 3 + 2)
                for hh in range(MLA_HEADS + 1):
                    if hh < MLA_HEADS:
                        a = open_acc(f"mq{hh}")
                        for c in range(2):
                            last = pe.matmul(a[0:96, 0:S], uq[:, c, 96 * hh:96 * hh + 96], cqn[:, c, :],
                                             start=c == 0, stop=c == 1)
                        last.then_inc(acc_full, 1)
                    if hh >= 1:
                        drained(f"mq{hh - 1}")
                        rotate(f"mq{hh - 1}", C("rotm")[0:96, 0:96], qm[0:96, hh - 1, :], slice(0, 96))
                pe.wait_ge(lat_ready, L * 3 + 3)
                ukv = tl[:, UKV:UKV + 640]
                for hh in range(MLA_HEADS):
                    a = open_acc(f"mk{hh}")
                    pe.matmul(a[0:64, 0:S], ukv[:, 128 * hh:128 * hh + 64], cqn[:, 2, :], start=True, stop=True)\
                        .then_inc(acc_full, 1)
                for t in range(TT):
                    a = open_acc(f"mv{t}")
                    pe.matmul(a[:, 0:320], cqn[:, 2, t * P:(t + 1) * P],
                              ukv.rearrange("p (h n) -> p h n", h=MLA_HEADS)[:, :, 64:128], start=True, stop=True)\
                        .then_inc(acc_full, 1)
                pe.wait_ge(gel_ready, L + 1)
                a = open_acc("kcc")
                pe.matmul(a[:, 0:32], tl[:, W2K:W2K + 128], hid[:, 0, :], start=True, stop=True).then_inc(acc_full, 1)
                pe.wait_ge(grep_ready, L + 1)
                a = open_acc("vbd")
                for g in range(2):
                    last = pe.matmul(a[0:96, 192 * g:192 * g + 192], grep[:, g, :], tl[:, W2V:W2V + 192],
                                     start=True, stop=True)
                last.then_inc(acc_full, 1)
                pe.wait_ge(kcT_ready, L * 2 + 2)
                pe.wait_ge(rope_ready, L * 17 + 3)
                for g in range(2):
                    a = open_acc(f"cs{g}")
                    for t in range(TT):
                        for r in range(REP):
                            rows = slice(64 * g, 64 * g + 64)
                            at = 48 * t + 16 * r
                            last = pe.matmul(a[:, at:at + 16], rope1[rows, r, t * P:(t + 1) * P], kcT[rows, :],
                                             start=True, stop=True)
                    last.then_inc(acc_full, 1)
                pe.wait_ge(pc_ready, L + 1)
                a = open_acc("ct")
                for t in range(TT):
                    last = pe.transpose(a[0:96, t * P:(t + 1) * P], pc[:, 96 * t:96 * t + 96], C("ident"))
                last.then_inc(acc_full, 1)
                drained("ct")
                pe.wait_ge(vbd_ready, L + 1)
                for t in range(TT):
                    a = open_acc(f"co{t}")
                    pe.matmul(a[:, 0:384], pcT[0:96, t * P:(t + 1) * P], vbd[0:96, :], start=True, stop=True)\
                        .then_inc(acc_full, 1)
                pe.wait_ge(rope_ready, L * 17 + 12)
                for hh in range(RET_HEADS + 1):
                    if hh < RET_HEADS:
                        a = open_acc(f"rs{hh}")
                        rq, iq = ret_q(hh)
                        rk, ik = ret_k(hh)
                        pe.matmul(a[:, 0:S], rope1[rk, ik, 0:P], rope1[rq, iq, :], start=True, stop=True)
                        pe.matmul(a[:, S:S + P], rope1[rk, ik, P:S], rope1[rq, iq, P:S], start=True, stop=True)\
                            .then_inc(acc_full, 1)
                    if hh >= 1:
                        j = hh - 1
                        pe.wait_ge(rw_ready, L * RET_HEADS + (j + 1))
                        a = open_acc(f"ro{j}")
                        w = sm[:, j % 2, :]
                        v = [tokm[:, t, RV + 64 * j:RV + 64 * j + 64] for t in range(TT)]
                        pe.matmul(a[:, 0:HD], w[:, 0:P], v[0], start=True, stop=True)
                        pe.matmul(a[:, HD:2 * HD], w[:, P:S], v[0], start=True, stop=False)
                        pe.matmul(a[:, HD:2 * HD], w[:, S:S + P], v[1], start=False, stop=True).then_inc(acc_full, 1)
                pe.wait_ge(km_ready, L + 1)
                pe.wait_ge(rope_ready, L * 17 + 17)
                attention(head1, NH1, 0, lambda i: None)
                pe.wait_ge(mixed_ready, L + 1)
                for c in range(KC):
                    a = open_acc(f"mt{c}")
                    for t in range(TT):
                        last = pe.transpose(a[:, t * P:(t + 1) * P], mixed[:, t, c * P:(c + 1) * P], C("ident"))
                    last.then_inc(acc_full, 1)
                for n in range(KC):
                    if n % 2 == 0:
                        tl = tile("wout", n // 2)
                    if n == 0:
                        drained(f"mt{KC - 1}")
                        drained(f"mt{KC - 2}")
                    project(f"wo{n}", unit(tl, n % 2), P, hs)
                sum_squares("ss2", L * 8 + 4)
                for n in range(F1):
                    if n % 2 == 0:
                        tl = tile("up", n // 2)
                    project(f"up{n}", unit(tl, n % 2), P, hs, KC if n == 0 else None)
                for n in range(KC):
                    a = open_acc(f"dn{n}")
                    for half in range(2):
                        tl = tile("down", 2 * n + half).rearrange("p (c m) -> p c m", c=16)
                        for c in range(16):
                            k = 16 * half + c
                            if n == 0:
                                pe.wait_ge(a_ready, L * F1 + (k + 1))
                            last = pe.matmul(a[:, 0:S], tl[:, c, :], big[:, k, :], start=k == 0, stop=k == F1 - 1)
                    last.then_inc(acc_full, 1)

            visits = [LAYERS * len([u for u in range(T1) if u % RING == s_]) for s_ in range(RING)]
            enter(AF, 0, TILES2, visits)
            sum_squares("ssf", LAYERS * 8, h)

            with pe.Fori(0, LAYERS) as L:
                enter(A2, L, TILES2, visits)
                pe.wait_ge(csil_ready, 1)

                def ada(j):
                    a = open_acc(f"ada{j}")
                    for col in range(6):
                        if col % 2 == 0:
                            tl = tile("ada", 3 * j + col // 2)
                        w = unit(tl, col % 2)
                        for c in range(KC):
                            last = pe.matmul(a[:, col:col + 1], w[:, c, :], csil[:, 2, c:c + 1],
                                             start=c == 0, stop=c == KC - 1)
                    last.then_inc(acc_full, 1)

                for j in range(4):
                    ada(j)
                sum_squares("ss1", L * 8 + Q2)
                for j in range(4, 8):
                    ada(j)
                for b in range(len(UNITS2) + 3):
                    if b < 8:
                        u = UNITS2[b]
                        if b % 2 == 0:
                            tl = tile(u, UNITS2[b + 1])
                        a = open_acc(u)
                        w = unit(tl, b % 2)
                        for c in range(KC):
                            if b == 0:
                                pe.wait_ge(h_ready, L * (2 * KC) + (H2 + c + 1))
                            last = pe.matmul(a[:, 0:S], w[:, c, :], h[:, c, :], start=c == 0, stop=c == KC - 1)
                        last.then_inc(acc_full, 1)
                    if 1 <= b < 9:
                        pe.wait_ge(raw2_sq, L * 8 + b)
                        a = open_acc("ss_" + UNITS2[b - 1])
                        pe.matmul(a[:, 0:S], C("half"), sq[:, b - 1, :], start=True, stop=True).then_inc(acc_full, 1)
                    if b >= 3:
                        pe.wait_ge(qn2_ready, L * 8 + (b - 2))
                        rotate(UNITS2[b - 3], C("rotp"), qk2[:, b - 3, :])
                for j in range(2):
                    tl = tile("v", j).rearrange("p (c n) -> p c n", c=KC)
                    for t in range(TT):
                        a = open_acc(f"v{j}{t}")
                        for c in range(KC):
                            last = pe.matmul(a[:, 0:256], h[:, c, t * P:(t + 1) * P], tl[:, c, :],
                                             start=c == 0, stop=c == KC - 1)
                        last.then_inc(acc_full, 1)
                for i, u in enumerate(LATER2):
                    if i % 2 == 0:
                        tl = tile(u, LATER2[i + 1])
                    project(u, unit(tl, i % 2), P, hs)
                for b in range(2):
                    pe.wait_ge(pooled, L * 2 + (b + 1))
                    a = open_acc(f"pw{b}")
                    pe.matmul(a[:, 0:S], V2("poolw")[:, 128 * b:128 * b + 128], sw[:, 2 * b, 16:16 + S],
                              start=True, stop=True).then_inc(acc_full, 1)

                def gates(i):
                    for n in gates_at(i):
                        if n % 2 == 0 or n == gates_at(i)[0]:
                            state["gate"] = tile("gate", n // 2)
                        project(f"g{n}", unit(state["gate"], n % 2), P, hs)

                pe.wait_ge(qk2_ready, L * 8 + 8)
                drained(f"v{1}{1}")
                drained(f"v{1}{0}")
                attention(head2, NH2, LAYERS * NH1, gates)
                pe.wait_ge(ya_ready, L + 1)
                for c in range(4):
                    a = open_acc(f"yt{c}")
                    for t in range(TT):
                        last = pe.transpose(a[:, t * P:(t + 1) * P], ya[:, t, c * P:(c + 1) * P], C("ident"))
                    last.then_inc(acc_full, 1)
                drained("pw1")
                pe.wait_ge(yc_ready, L * 2 + 2)
                for n in range(KC):
                    if n == 0:
                        tp, tcv = tile("ppool", 0), tile("pconv", 0)
                    for name, tl_, y, k in (("P", tp, yp, 2), ("C", tcv, yc, 2), ("A", None, yaT, 4)):
                        if name == "A":
                            if n == 0:
                                for c in range(4):
                                    drained(f"yt{c}") if c >= 2 else None
                            tl_ = tile("pattn", n // 4)
                        w = tl_.rearrange("p (c m) -> p c m", c=k)
                        at = P * n if name != "A" else P * (n % 4)
                        a = open_acc(f"{name}{n}")
                        for c in range(k):
                            last = pe.matmul(a[:, 0:S], w[:, c, at:at + P], y[:, c, :], start=c == 0, stop=c == k - 1)
                        last.then_inc(acc_full, 1)
                pe.wait_ge(merged_ready, L * KC + KC)
                for n in range(KC):
                    if n % 2 == 0:
                        tl = tile("wout", n // 2)
                    project(f"wo{n}", unit(tl, n % 2), P, lambda c: merged[:, c, :])
                sum_squares("ss2", L * 8 + (Q2 + 4))
                for n in range(F2):
                    tl = tile("gu", n)
                    project(f"gt{n}", unit(tl, 0), P, hs, H2 + KC if n == 0 else None)
                    project(f"up{n}", unit(tl, 1), P, hs)
                tl = None
                for n in range(KC):
                    a = open_acc(f"dn{n}")
                    for k in range(F2):
                        m = n * F2 + k
                        if m % 16 == 0 or tl is None:
                            tl = tile("down", m // 16).rearrange("p (c m) -> p c m", c=16)
                        if n == 0:
                            pe.wait_ge(a2_ready, L * F2 + (k + 1))
                        last = pe.matmul(a[:, 0:S], tl[:, m % 16, :], big[:, k, :], start=k == 0, stop=k == F2 - 1)
                    last.then_inc(acc_full, 1)

        def psum_of(tn, name):
            return acc[tn.bank(name)]

        @block.scalar
        def _(act):
            act.dma_start(v1all[:], vec1).then_inc(inputs_in, 16)
            act.dma_start(onc[:], once).then_inc(inputs_in, 16)
            act.dma_start(nv[:].bitcast(I32), pos).then_inc(inputs_in, 16)
            act.wait_ge(inputs_in, 16 * 6)
            act.wait_ge(trig_arg, 2)
            for j in range(2):
                act.activation(trig[:, j, :, :], trig[:, j, :, :], ACT.Sin).then_inc(trig_ready, 1)
            act.activation(csil[:, 0, :], onc[:, 8:16], ACT.Exp, scale=-1.0).then_inc(csil_e, 1)

            own = [0]

            def link(ins):
                own[0] += 1
                ins.then_inc(act_step, 1)
                act.wait_ge(act_step, own[0])

            def end_layer():
                act.sem_clear(act_step)
                own[0] = 0

            def full(tn, name, L):
                act.wait_ge(acc_full, tn.full(name, L))
                return psum_of(tn, name)

            def take(tn, name, L, dst, rows=slice(0, P), n=S, func=ACT.Copy, **kw):
                a = full(tn, name, L)
                act.activation(dst, a[rows, 0:n], func, **kw).then_inc(acc_drained[tn.bank(name)], 1)

            def squares(x_count, sq=sq):
                for i in range(4):
                    if x_count is not None:
                        act.wait_ge(x_ready, x_count + 2 * i + 2)
                    act.activation(sq[:, 2 * i:2 * i + 2, :], x[:, 2 * i:2 * i + 2, :], ACT.Square).then_inc(sq_ready, 1)

            def estimate(tn, name, L, i):
                act.wait_ge(acc_drained[tn.bank(name)], tn.drained(name, L))
                link(act.activation(ny[:, i, :], nv[:, i, :], ACT.Ln))
                act.activation(ny[:, i, :], ny[:, i, :], ACT.Exp, scale=-0.5).then_inc(y_ready, 1)

            def attention(n, base, L, extra):
                for i in range(n + 1):
                    if i < n:
                        act.wait_ge(nmax_ready, L * n + (base + i + 1))
                        act.activation(pr[:, i % 2, 0:P], sm[:, i % 2, 0:P], ACT.Exp,
                                       bias=nmax[:, i, 0:1], accum_out=psumv[:, i, 0:1])
                        act.activation(pr[:, i % 2, P:3 * P], sm[:, i % 2, P:3 * P], ACT.Exp,
                                       bias=nmax[:, i, 1:2], accum_out=psumv[:, i, 1:2]).then_inc(p_ready, 1)
                    if i >= 1:
                        act.wait_ge(pt_full, L * n + (base + i))
                        act.activation(prT[:, (i - 1) % 2, :], ps_t[:, 0:3 * P], ACT.Copy).then_inc(pt_copied, 1)
                    extra(i)

            with act.Fori(0, LAYERS) as L:
                act.wait_ge(vec_ready, L + 1)
                squares(None)
                estimate(A1, "ss1", L, 0)
                for i, u in enumerate(UNITS1):
                    if u == "vc":
                        take(A1, u, L, raw[:, i, :])
                        continue
                    take(A1, u, L, raw[:, i, :])
                    if u in ("cq0", "cq1", "ckv"):
                        k = ("cq0", "cq1", "ckv").index(u)
                        act.wait_ge(acc_drained[A1.bank(u)], A1.drained(u, L))
                        act.activation(sq[:, k, :], raw[:, i, :], ACT.Square).then_inc(latsq, 1)
                estimate(A1, "ssq", L, 0)
                estimate(A1, "ssk", L, 1)
                for j in range(4):
                    for t in range(TT):
                        take(A1, f"tm{j}{t}", L, tokm[:, t, 256 * j:256 * j + TM_W[j]], n=TM_W[j])
                act.wait_ge(acc_drained[A1.bank("tm11")], A1.drained("tm11", L))
                act.activation(gate, tokm[:, :, GT:GT + 18], ACT.Exp, scale=-1.0).then_inc(gexp, 1)
                for j, kind in enumerate(("k", "v")):
                    a = full(A1, "hid" + kind, L)
                    act.activation(gel[:, 0, 30 * j:30 * j + 30], a[:, 0:30], ACT.Copy)\
                        .then_inc(acc_drained[A1.bank("hid" + kind)], 1)
                for hh in range(MLA_HEADS):
                    take(A1, f"mq{hh}", L, qm[0:96, hh, :], rows=slice(0, 96))
                for hh in range(MLA_HEADS):
                    take(A1, f"mk{hh}", L, km[0:64, hh, :], rows=slice(0, 64))
                for t in range(TT):
                    take(A1, f"mv{t}", L, vm[:, t, :], n=320)
                act.wait_ge(ge, L * 2 + 1)
                act.activation(gel[:, 1, 0:60], gel[:, 1, 0:60], ACT.Exp, scale=-2.0 * GELU_C).then_inc(ge, 1)
                act.wait_ge(csub, L + 1)
                act.activation(pc[:], pc[:], ACT.Exp).then_inc(cexp, 1)
                take(A1, "ct", L, pcT[0:96, :], rows=slice(0, 96))
                for t in range(TT):
                    take(A1, f"co{t}", L, mixed[:, t, 0:384], n=384)
                for hh in range(RET_HEADS):
                    a = full(A1, f"ro{hh}", L)
                    act.activation(ro_(hh), a[:, 0:2 * HD].rearrange("p (t d) -> p t d", t=TT), ACT.Copy)\
                        .then_inc(acc_drained[A1.bank(f"ro{hh}")], 1)
                act.activation(rgx_(), tokm[:, :, RG:RG + 320], ACT.Exp, scale=-1.0).then_inc(gexp, 1)
                act.wait_ge(gn_v, L + 1)
                link(act.activation(gnst[:, 3, :], gnst[:, 2, :], ACT.Ln))
                act.activation(gnst[:, 3, :], gnst[:, 3, :], ACT.Exp, scale=-0.5).then_inc(gn_y, 1)
                attention(NH1, 0, L, lambda i: None)
                for c in range(KC):
                    take(A1, f"mt{c}", L, h[:, c, :])
                squares(L * (2 * KC))
                estimate(A1, "ss2", L, 0)
                for n in range(F1):
                    a = full(A1, f"up{n}", L)
                    act.activation(big[:, n, :], a[:, 0:S], ACT.Relu).then_inc(acc_drained[A1.bank(f"up{n}")], 1)
                    act.wait_ge(acc_drained[A1.bank(f"up{n}")], A1.drained(f"up{n}", L))
                    act.activation(big[:, n, :], big[:, n, :], ACT.Square).then_inc(a_ready, 1)
                end_layer()
            squares((LAYERS - 1) * 2 * KC + KC, h)
            estimate(AF, "ssf", 0, 0)
            end_layer()
            with act.Fori(0, LAYERS) as L:
                act.wait_ge(vec_ready, L + (LAYERS + 1))
                squares(None)
                estimate(A2, "ss1", L, 0)
                for c in range(KC):
                    act.wait_ge(h_pre, L * (2 * KC) + (c + 1))
                    act.activation(h[:, c, :], h[:, c, :], ACT.Identity, bias=mod[:, c:c + 1]).then_inc(h_ready, 1)
                for b in range(len(UNITS2) + 1):
                    if b < 8:
                        u = UNITS2[b]
                        a = full(A2, u, L)
                        take(A2, u, L, raw[:, b, :])
                        act.wait_ge(acc_drained[A2.bank(u)], A2.drained(u, L))
                        act.activation(sq[:, b, :], raw[:, b, :], ACT.Square).then_inc(raw2_sq, 1)
                    if b >= 1:
                        estimate(A2, "ss_" + UNITS2[b - 1], L, (b - 1) % 2)
                for j in range(2):
                    for t in range(TT):
                        take(A2, f"v{j}{t}", L, vv[:, t, 256 * j:256 * j + 256])
                act.wait_ge(pad_ready, 1)
                for b, u in enumerate(("pa", "pb")):
                    take(A2, u, L, up_[:, b, 16:16 + S])
                for b, u in enumerate(("cua", "cub")):
                    take(A2, u, L, cu[:, b, :])
                for b, u in enumerate(("cba", "cbb")):
                    take(A2, u, L, cb[:, b, :])
                for b in range(2):
                    take(A2, f"pw{b}", L, yp[:, b, :], func=ACT.Identity, scale=V2("pscale", b))

                def gates(i):
                    for n in gates_at(i):
                        a = full(A2, f"g{n}", L)
                        act.activation(big[:, n, :], a[:, 0:S], ACT.Exp, scale=-1.0)\
                            .then_inc(acc_drained[A2.bank(f"g{n}")], 1)

                attention(NH2, LAYERS * NH1, L, gates)
                gates(NH2 + 1)
                for c in range(4):
                    take(A2, f"yt{c}", L, yaT[:, c, :])
                squares(L * (2 * KC) + X2)
                estimate(A2, "ss2", L, 0)
                for c in range(KC):
                    act.wait_ge(h_pre, L * (2 * KC) + (KC + c + 1))
                    act.activation(h[:, c, :], h[:, c, :], ACT.Identity, bias=mod[:, 24 + c:25 + c]).then_inc(h_ready, 1)
                for n in range(F2):
                    a = full(A2, f"gt{n}", L)
                    if n >= 2:
                        act.wait_ge(a2_ready, L * F2 + (n - 1))
                    act.activation(nv[:, n % 2, :], a[:, 0:S], ACT.Exp, scale=-1.0).then_inc(silu_e, 1)
                end_layer()

        @block.vector
        def _(dve):
            own = [0]

            def link(ins):
                own[0] += 1
                ins.then_inc(dve_step, 1)
                dve.wait_ge(dve_step, own[0])

            def end_layer():
                dve.sem_clear(dve_step)
                own[0] = 0

            turn_of_rope = [0]
            TTN, TSC, STT = nc.vector.tensor_tensor, nc.vector.tensor_scalar, nc.vector.scalar_tensor_tensor

            dve.wait_ge(inputs_in, 16 * 6)
            posf, ang, k, r = big[:, 0:2, :], big[:, 2:6, :], big[:, 6:10, :], big[:, 10:14, :]
            link(nc.vector.tensor_copy(posf, nv[:].bitcast(I32)))
            iat = CONSTS["inv"][0]
            for j in range(4):
                last = TSC(ang[:, j, :], posf[:, j // 3, :], cst[:, iat + j:iat + j + 1], None, ALU.mult)
                link(last)
            magic = 12582912.0
            turn = 2.0 * np.pi
            c1 = 6.28125
            c2 = float(np.float32(turn - c1))
            c3 = float(np.float32(turn - c1 - np.float64(np.float32(turn - c1))))
            link(TSC(k, ang, float(1.0 / turn), None, ALU.mult))
            link(TSC(k, k, magic, None, ALU.add))
            link(TSC(k, k, magic, None, ALU.subtract))
            link(STT(r, k, -c1, ang, ALU.mult, ALU.add))
            link(STT(r, k, -c2, r, ALU.mult, ALU.add))
            link(STT(r, k, -c3, r, ALU.mult, ALU.add))
            lim = 3.1415925
            TSC(trig[:, 1, :, :], r, lim, -lim, ALU.min, ALU.max).then_inc(trig_arg, 1)
            link(STT(k, r, -1.0, r, ALU.mult, ALU.max))
            TSC(trig[:, 0, :, :], k, -1.0, float(np.pi / 2), ALU.mult, ALU.add).then_inc(trig_arg, 1)
            dve.wait_ge(csil_e, 1)
            link(TSC(csil[:, 0, :], csil[:, 0, :], 1.0, None, ALU.add))
            link(nc.vector.reciprocal(csil[:, 1, :], csil[:, 0, :]))
            TTN(csil[:, 2, :], onc[:, 8:16], csil[:, 1, :], ALU.mult).then_inc(csil_ready, 1)
            dve.wait_ge(trig_ready, 2)
            end_layer()

            def full(tn, name, L):
                dve.wait_ge(acc_full, tn.full(name, L))
                return psum_of(tn, name)

            def mean_square(tn, name, L, i, n):
                a = full(tn, name, L)
                TSC(nv[:, i, :], a[:, 0:S], 1.0 / n, EPS, ALU.mult, ALU.add).then_inc(acc_drained[tn.bank(name)], 1)

            def refine(i, count, v=None, y=None, t=None, dst=None):
                v = nv[:, i, :] if v is None else v
                y = ny[:, i, :] if y is None else y
                t = nt[:, :] if t is None else t
                dst = rstd[:, :] if dst is None else dst
                link(TTN(t, y, y, ALU.mult))
                link(STT(t, v, -0.5, t, ALU.mult, ALU.mult))
                link(STT(dst, t, 1.5, y, ALU.add, ALU.mult))

            def rope(tn, name, L, src, tab, outs, signal, rows=slice(0, P)):
                turn_of_rope[0] ^= 1
                tc, ts = tcs[:, turn_of_rope[0], :], tss[:, turn_of_rope[0], :]
                TTN(tc[rows, :], src, trig[rows, 0, tab, :], ALU.mult)
                a = full(tn, "rot_" + name, L)
                TTN(ts[rows, :], a[rows, 0:S], trig[rows, 1, tab, :], ALU.mult)\
                    .then_inc(acc_drained[tn.bank("rot_" + name)], 1)
                dve.wait_ge(acc_drained[tn.bank("rot_" + name)], tn.drained("rot_" + name, L))
                for dst, part in outs:
                    last = TTN(dst, tc[part, :], ts[part, :], ALU.add)
                last.then_inc(signal, 1)

            def scores(i, n, base, L, scale):
                if i >= 2:
                    dve.wait_ge(p_ready, L * n + (base + i - 1))
                dve.wait_ge(s_full, L * n + (base + i + 1))
                STT(sm[:, i % 2, :], ps_s[i % 2][:, 0:384], scale, C("mask"), ALU.mult, ALU.add).then_inc(s_drained, 1)
                dve.wait_ge(s_drained, L * n + (base + i + 3))
                nc.vector.tensor_reduce(nmax[:, i, 0:1], sm[:, i % 2, 0:P], AX.X, ALU.max, negate=True)
                nc.vector.tensor_reduce(nmax[:, i, 1:2], sm[:, i % 2, P:3 * P], AX.X, ALU.max, negate=True)\
                    .then_inc(nmax_ready, 1)

            with dve.Fori(0, LAYERS) as L:
                own[0] = 0
                nc.vector.tensor_copy(v1[:], v1all[:, L, :]).then_inc(vec_ready, 1)
                dve.wait_ge(vec_ready, L + 1)
                mean_square(A1, "ss1", L, 0, D)
                dve.wait_ge(y_ready, L * Y1 + 1)
                refine(0, None)
                for c in range(KC):
                    STT(h[:, c, :], x[:, c, :], V1("ln1", c), rstd[:], ALU.mult, ALU.mult).then_inc(h_ready, 1)

                def rope1_block(u):
                    i = UNITS1.index(u)
                    dve.wait_ge(acc_drained[A1.bank(u)], A1.drained(u, L))
                    allr = slice(0, P)
                    if u == "kpe":
                        rope(A1, u, L, raw[64:96, i, :], 1, [(km[64:96, 0, :], slice(64, 96))], rope_ready, slice(64, 96))
                        dve.wait_ge(rope_ready, L * 17 + 7)
                        nc.vector.tensor_copy(km[64:96, 1:5, :], km[64:96, 0:1, :].to_broadcast([32, 4, S]))\
                            .then_inc(km_ready, 1)
                    elif u == "kc":
                        rope(A1, u, L, raw[:, i, :], 0, [(nt[:, :], allr)], rope_ready)
                        dve.wait_ge(rope_ready, L * 17 + 6)
                        shifted(nt[:, :], 0)
                    elif u == "r4":
                        rope(A1, u, L, raw[:, i, :], 2, [(rope1[0:64, 9, :], slice(0, 64)), (rope1[0:64, 10, :], slice(64, 128))],
                             rope_ready)
                    else:
                        rope(A1, u, L, raw[:, i, :], 2 if u[0] == "r" else 0, [(rope1[:, ROPE1[u], :], allr)], rope_ready)

                def shifted(src, j):
                    cp = nc.vector.tensor_copy
                    cp(xk[j][0:64, 0, :], src[0:64, :])
                    cp(xk[j][64:128, 1, 0:S - 1], src[64:128, 1:S])
                    cp(xk[j][64:128, 0, 0:S - 1], src[0:64, 1:S])
                    link(cp(xk[j][0:64, 1, :], src[64:128, :]))
                    for g in range(2):
                        part = fk[j][:, :, g, :]
                        a0 = xk[j][:, g, 0:240].rearrange("p (n m two) -> p m two n", m=8, two=2)[:, :, 0, :]
                        a1 = xk[j][:, g, 16:256].rearrange("p (n m two) -> p m two n", m=8, two=2)[:, :, 0, :]
                        pos_ = V1("posk" if j == 0 else "posv")
                        TTN(part[:, 0:8, :], a0, pos_[:, 0:8].unsqueeze(2).to_broadcast([P, 8, N_CMP]), ALU.add)
                        last = TTN(part[:, 8:16, :], a1, pos_[:, 8:16].unsqueeze(2).to_broadcast([P, 8, N_CMP]), ALU.add)
                    last.then_inc(f_ready, 1)

                for i, u in enumerate(UNITS1):
                    if i >= 1 and UNITS1[i - 1] in ROPED1:
                        rope1_block(UNITS1[i - 1])
                    if u == "vc":
                        dve.wait_ge(acc_drained[A1.bank(u)], A1.drained(u, L))
                        vraw = raw[:, i, :]
                mean_square(A1, "ssq", L, 0, 256)
                mean_square(A1, "ssk", L, 1, 128)
                dve.wait_ge(y_ready, L * Y1 + 2)
                refine(0, None)
                for c in range(2):
                    STT(cqn[:, c, :], raw[:, 7 + c, :], V1("qn", c), rstd[:], ALU.mult, ALU.mult).then_inc(lat_ready, 1)
                dve.wait_ge(y_ready, L * Y1 + 3)
                refine(1, None)
                STT(cqn[:, 2, :], raw[:, 9, :], V1("kvn", 0), rstd[:], ALU.mult, ALU.mult).then_inc(lat_ready, 1)
                rope1_block("r4")
                shifted(vraw, 1)
                for kind in ("k", "v"):
                    dve.wait_ge(acc_drained[A1.bank("hid" + kind)], A1.drained("hid" + kind, L))
                gx, gu, gd = gel[:, 0, 0:60], gel[:, 1, 0:60], gel[:, 2, 0:60]
                link(TTN(gu, gx, gx, ALU.mult))
                link(TSC(gu, gu, 0.044715, 1.0, ALU.mult, ALU.add))
                TTN(gu, gu, gx, ALU.mult).then_inc(ge, 1)
                for hh in range(MLA_HEADS):
                    dve.wait_ge(acc_drained[A1.bank(f"mq{hh}")], A1.drained(f"mq{hh}", L))
                    rope(A1, f"mq{hh}", L, qm[64:96, hh, :], 1, [(qm[64:96, hh, :], slice(64, 96))], rope_ready, slice(64, 96))
                dve.wait_ge(ge, L * 2 + 2)
                link(TSC(gd, gu, 1.0, None, ALU.add))
                link(nc.vector.reciprocal(gu, gd))
                link(nc.vector.memset(hid[:, :, :], 0.0))
                TTN(hid[:, 0, :].rearrange("p (g n) -> p g n", g=2)[:, :, 0:N_CMP],
                    gel[:, 0, 0:30].rearrange("p (g n) -> p g n", g=2), gel[:, 1, 0:30].rearrange("p (g n) -> p g n", g=2),
                    ALU.mult)
                TTN(hid[:, 1, :].rearrange("p (g n) -> p g n", g=2)[:, :, 0:N_CMP],
                    gel[:, 0, 30:60].rearrange("p (g n) -> p g n", g=2), gel[:, 1, 30:60].rearrange("p (g n) -> p g n", g=2),
                    ALU.mult).then_inc(gel_ready, 1)
                dve.wait_ge(gel_ready, L + 1)
                for g in range(2):
                    last = nc.vector.tensor_copy(grep[:, g, :].rearrange("p (h n) -> p h n", h=NSA_HEADS),
                                                 hid[:, 1, 16 * g:16 * g + 16].unsqueeze(1).to_broadcast([P, NSA_HEADS, 16]))
                last.then_inc(grep_ready, 1)
                a = full(A1, "kcc", L)
                nc.vector.tensor_copy(kcT[0:64, :], a[0:64, 0:16]).then_inc(kcT_ready, 1)
                nc.vector.tensor_copy(kcT[64:128, :], a[64:128, 16:32]).then_inc(kcT_ready, 1)
                dve.wait_ge(kcT_ready, L * 2 + 2)
                dve.sem_inc(acc_drained[A1.bank("kcc")], 1)
                a = full(A1, "vbd", L)
                TTN(vbd[0:96, :].rearrange("p (h d) -> p h d", h=NSA_HEADS), a[0:96, 0:384].rearrange("p (h d) -> p h d", h=NSA_HEADS),
                    C("bmask", 96).unsqueeze(2).to_broadcast([96, NSA_HEADS, HD]), ALU.mult).then_inc(vbd_ready, 1)
                dve.wait_ge(vbd_ready, L + 1)
                dve.sem_inc(acc_drained[A1.bank("vbd")], 1)
                dve.wait_ge(gexp, L * 2 + 1)
                link(TSC(gate, gate, 1.0, None, ALU.add))
                nc.vector.reciprocal(gate, gate).then_inc(gate_ready, 1)
                dve.wait_ge(gate_ready, L + 1)
                split = lambda v: v.rearrange("p (t g n) -> p g t n", t=TT, g=2)
                for g in range(2):
                    a = full(A1, f"cs{g}", L)
                    STT(split(pc)[:, g, :, :], a[:, 0:96].rearrange("p (t n) -> p t n", t=TT), HD ** -0.5,
                        split(C("cmask"))[:, g, :, :], ALU.mult, ALU.add).then_inc(acc_drained[A1.bank(f"cs{g}")], 1)
                    dve.wait_ge(acc_drained[A1.bank(f"cs{g}")], A1.drained(f"cs{g}", L))
                pc3 = pc.rearrange("p (h n) -> p h n", n=NP16)
                bc = lambda v: v.unsqueeze(2).to_broadcast([P, 12, NP16])
                link(nc.vector.tensor_reduce(cst12[:, 0, :], pc3, AX.X, ALU.max))
                TTN(pc3, pc3, bc(cst12[:, 0, :]), ALU.subtract).then_inc(csub, 1)
                dve.wait_ge(cexp, L + 1)
                link(TTN(pc[:], pc[:], C("ckeep"), ALU.mult))
                link(nc.vector.tensor_reduce(cst12[:, 1, :], pc3, AX.X, ALU.add))
                link(TSC(cst12[:, 1, :], cst12[:, 1, :], 1e-30, None, ALU.max))
                link(nc.vector.reciprocal(cst12[:, 2, :], cst12[:, 1, :]))
                g4 = gate.rearrange("p t (h b) -> p t h b", b=N_BRANCH)
                link(TTN(cst12[:, 2, :].rearrange("p (t h) -> p t h", t=TT), cst12[:, 2, :].rearrange("p (t h) -> p t h", t=TT),
                         g4[:, :, :, 0], ALU.mult))
                TTN(pc3, pc3, bc(cst12[:, 2, :]), ALU.mult).then_inc(pc_ready, 1)
                for hh in range(RET_HEADS):
                    a = full(A1, f"rs{hh}", L)
                    w = sm[:, hh % 2, :]
                    if hh >= 2:
                        dve.wait_ge(acc_full, A1.full(f"ro{hh - 2}", L))
                    TTN(w[:, 0:S], a[:, 0:S], decay[:, hh, :], ALU.mult)
                    TTN(w[:, S:S + P], a[:, S:S + P], decay[:, hh, 0:P], ALU.mult).then_inc(rw_ready, 1)
                    dve.wait_ge(rw_ready, L * RET_HEADS + (hh + 1))
                    dve.sem_inc(acc_drained[A1.bank(f"rs{hh}")], 1)
                for hh in range(RET_HEADS):
                    dve.wait_ge(acc_drained[A1.bank(f"ro{hh}")], A1.drained(f"ro{hh}", L))
                o10 = ro_all(0).rearrange("p (h d) -> p h d", d=HD)
                s10 = ro_all(2).rearrange("p (h d) -> p h d", d=HD)
                bg = lambda v: v.unsqueeze(2).to_broadcast([P, 10, HD])
                link(nc.vector.tensor_reduce(gnst[:, 0, :], o10, AX.X, ALU.add))
                link(TSC(gnst[:, 1, :], gnst[:, 0, :], 1.0 / HD, None, ALU.mult))
                link(TTN(o10, o10, bg(gnst[:, 1, :]), ALU.subtract))
                link(TTN(s10, o10, o10, ALU.mult))
                link(nc.vector.tensor_reduce(gnst[:, 4, :], s10, AX.X, ALU.add))
                TSC(gnst[:, 2, :], gnst[:, 4, :], 1.0 / HD, EPS, ALU.mult, ALU.add).then_inc(gn_v, 1)
                dve.wait_ge(gexp, L * 2 + 2)
                gx_ = rgx_()
                link(TSC(gx_, gx_, 1.0, None, ALU.add))
                link(nc.vector.reciprocal(gx_, gx_))
                link(TTN(gx_, gx_, tokm[:, :, RG:RG + 320], ALU.mult))
                link(TTN(gx_, gx_, V1("gn").unsqueeze(1).to_broadcast([P, TT, 320]), ALU.mult))
                dve.wait_ge(gn_y, L + 1)
                refine(0, None, gnst[:, 2, :], gnst[:, 3, :], gnst[:, 4, :], gnst[:, 5, :])
                link(TTN(o10, o10, bg(gnst[:, 5, :]), ALU.mult))
                link(TTN(mixed[:, :, 704:1024], ro_all(0).rearrange("p (t f) -> p t f", t=TT), gx_, ALU.mult))
                for t in range(TT):
                    dve.wait_ge(acc_drained[A1.bank(f"co{t}")], A1.drained(f"co{t}", L))

                def output(i):
                    kind, hh = HEADS1[i]
                    dve.wait_ge(p_ready, L * NH1 + (i + 1))
                    link(nc.vector.reciprocal(coef[:, i, :], psumv[:, i, :]))
                    if kind != "mla":
                        b = 3 * hh + (1 if kind == "slc" else 2)
                        link(TTN(coef[:, i, :].unsqueeze(2), coef[:, i, :].unsqueeze(2), gate[:, :, b:b + 1], ALU.mult))
                    dve.wait_ge(o_full, L * NH1 + (i + 1))
                    for t in range(TT):
                        o = ps_o[:, 64 * t:64 * t + 64]
                        if kind == "mla":
                            m = mixed[:, t, 384 + 64 * hh:448 + 64 * hh]
                            last = TSC(m, o, coef[:, i, t:t + 1], None, ALU.mult)
                        else:
                            m = mixed[:, t, 64 * hh:64 * hh + 64]
                            last = STT(m, o, coef[:, i, t:t + 1], m, ALU.mult, ALU.add)
                    last.then_inc(o_drained, 1)

                for i in range(NH1 + 2):
                    if i < NH1:
                        scores(i, NH1, 0, L, scale1(i))
                    if i >= 2:
                        output(i - 2)
                dve.wait_ge(o_drained, L * NH1 + (NH1 + 1))
                dve.sem_inc(mixed_ready, 1)
                for n in range(KC):
                    a = full(A1, f"wo{n}", L)
                    TTN(x[:, n, :], a[:, 0:S], x[:, n, :], ALU.add).then_inc(x_ready, 1)
                    dve.wait_ge(x_ready, L * (2 * KC) + (n + 1))
                    dve.sem_inc(acc_drained[A1.bank(f"wo{n}")], 1)
                mean_square(A1, "ss2", L, 0, D)
                dve.wait_ge(y_ready, L * Y1 + 4)
                refine(0, None)
                for c in range(KC):
                    STT(h[:, c, :], x[:, c, :], V1("ln2", c), rstd[:], ALU.mult, ALU.mult).then_inc(h_ready, 1)
                for n in range(KC):
                    a = full(A1, f"dn{n}", L)
                    TTN(x[:, n, :], a[:, 0:S], x[:, n, :], ALU.add).then_inc(x_ready, 1)
                    dve.wait_ge(x_ready, L * (2 * KC) + (KC + n + 1))
                    dve.sem_inc(acc_drained[A1.bank(f"dn{n}")], 1)
                end_layer()

            nc.vector.memset(up_[:, :, 0:16], 0.0)
            nc.vector.memset(sw[:, :, 0:16], 0.0)
            nc.vector.memset(cv[:, :, 0:2], 0.0).then_inc(pad_ready, 1)
            mean_square(AF, "ssf", 0, 0, D)
            dve.wait_ge(y_ready, YF + 1)
            refine(0, None)
            for c in range(KC):
                STT(x[:, c, :], x[:, c, :], onc[:, c:c + 1], rstd[:], ALU.mult, ALU.mult).then_inc(x_ready, 1)
            dve.wait_ge(x_ready, X2)
            end_layer()

            with dve.Fori(0, LAYERS) as L:
                own[0] = 0
                nc.vector.tensor_copy(v2[:], v2all[:, L, :]).then_inc(vec_ready, 1)
                dve.wait_ge(vec_ready, L + (LAYERS + 1))
                bat = VEC2["bada"][0]

                def ada(j):
                    a = full(A2, f"ada{j}", L)
                    TTN(mod[:, 6 * j:6 * j + 6], a[:, 0:6], v2[:, bat + 6 * j:bat + 6 * j + 6], ALU.add)\
                        .then_inc(acc_drained[A2.bank(f"ada{j}")], 1)
                    dve.wait_ge(acc_drained[A2.bank(f"ada{j}")], A2.drained(f"ada{j}", L))

                for j in range(4):
                    ada(j)
                link(STT(mods[:, 0, :], mod[:, 8:16], 1.0, V2("n1"), ALU.add, ALU.mult))
                mean_square(A2, "ss1", L, 0, D)
                dve.wait_ge(y_ready, L * Y2N + (Y2 + 1))
                refine(0, None)
                for c in range(KC):
                    STT(h[:, c, :], x[:, c, :], mods[:, 0, c:c + 1], rstd[:], ALU.mult, ALU.mult).then_inc(h_pre, 1)
                for j in range(4, 8):
                    ada(j)
                link(STT(mods[:, 1, :], mod[:, 32:40], 1.0, V2("n2"), ALU.add, ALU.mult))
                for b in range(len(UNITS2) + 3):
                    if 1 <= b < 9:
                        mean_square(A2, "ss_" + UNITS2[b - 1], L, (b - 1) % 2, HD)
                    if 2 <= b < 10:
                        j = b - 2
                        dve.wait_ge(y_ready, L * Y2N + (Y2 + 2 + j))
                        refine(j % 2, None)
                        STT(qk2[:, j, :], raw[:, j, :], V2("qn" if j < 4 else "kn", 0), rstd[:], ALU.mult, ALU.mult)\
                            .then_inc(qn2_ready, 1)
                    if b >= 3:
                        j = b - 3
                        dve.wait_ge(qn2_ready, L * 8 + (j + 1))
                        rope(A2, UNITS2[j], L, qk2[:, j, :], 3, [(qk2[:, j, :], slice(0, P))], qk2_ready)
                for b, u in enumerate(("cca", "ccb")):
                    dve.wait_ge(acc_drained[A2.bank("cu" + "ab"[b])], A2.drained("cu" + "ab"[b], L))
                    dve.wait_ge(acc_drained[A2.bank("cb" + "ab"[b])], A2.drained("cb" + "ab"[b], L))
                    a = full(A2, u, L)
                    TTN(cv[:, b, 2:2 + S], a[:, 0:S], cu[:, b, :], ALU.mult).then_inc(acc_drained[A2.bank(u)], 1)
                    dve.wait_ge(acc_drained[A2.bank(u)], A2.drained(u, L))
                    link(TSC(tc, cv[:, b, 2:2 + S], V2("conv", 4 + b), None, ALU.mult))
                    link(STT(tc, cv[:, b, 1:1 + S], V2("conv", 2 + b), tc, ALU.mult, ALU.add))
                    link(STT(tc, cv[:, b, 0:S], V2("conv", b), tc, ALU.mult, ALU.add))
                    TTN(yc[:, b, :], tc, cb[:, b, :], ALU.mult).then_inc(yc_ready, 1)

                def output(i):
                    dve.wait_ge(p_ready, L * NH2 + (LAYERS * NH1 + i + 1))
                    link(nc.vector.reciprocal(coef[:, i, :], psumv[:, i, :]))
                    dve.wait_ge(o_full, L * NH2 + (LAYERS * NH1 + i + 1))
                    for t in range(TT):
                        last = TSC(ya[:, t, 64 * i:64 * i + 64], ps_o[:, 64 * t:64 * t + 64], coef[:, i, t:t + 1], None, ALU.mult)
                    last.then_inc(o_drained, 1)

                def gates(i):
                    g = gates_at(i)
                    dve.wait_ge(acc_drained[A2.bank(f"g{g[-1]}")], A2.drained(f"g{g[-1]}", L))
                    for n in g:
                        last = TSC(big[:, n, :], big[:, n, :], 1.0, None, ALU.add)
                    link(last)
                    for n in g:
                        last = nc.vector.reciprocal(big[:, n, :], big[:, n, :])
                    link(last)

                for i in range(NH2 + 2):
                    if i < NH2:
                        scores(i, NH2, LAYERS * NH1, L, HD ** -0.5)
                    if i >= 1:
                        gates(i - 1)
                    if i >= 2:
                        output(i - 2)
                dve.wait_ge(o_drained, L * NH2 + (LAYERS * NH1 + NH2 + 1))
                dve.sem_inc(ya_ready, 1)
                gates(NH2 + 1)
                for n in range(KC):
                    for m, name in enumerate(MIXERS):
                        a = full(A2, f"{name}{n}", L)
                        dst = tc if m else merged[:, n, :]
                        TTN(dst, a[:, 0:S], big[:, KC * m + n, :], ALU.mult).then_inc(acc_drained[A2.bank(f"{name}{n}")], 1)
                        dve.wait_ge(acc_drained[A2.bank(f"{name}{n}")], A2.drained(f"{name}{n}", L))
                        if m == 1:
                            link(TTN(merged[:, n, :], merged[:, n, :], tc, ALU.add))
                        if m == 2:
                            TTN(merged[:, n, :], merged[:, n, :], tc, ALU.add).then_inc(merged_ready, 1)
                for n in range(KC):
                    a = full(A2, f"wo{n}", L)
                    STT(x[:, n, :], a[:, 0:S], mod[:, 16 + n:17 + n], x[:, n, :], ALU.mult, ALU.add).then_inc(x_ready, 1)
                    dve.wait_ge(x_ready, L * (2 * KC) + (X2 + n + 1))
                    dve.sem_inc(acc_drained[A2.bank(f"wo{n}")], 1)
                mean_square(A2, "ss2", L, 0, D)
                dve.wait_ge(y_ready, L * Y2N + (Y2 + 10))
                refine(0, None)
                for c in range(KC):
                    STT(h[:, c, :], x[:, c, :], mods[:, 1, c:c + 1], rstd[:], ALU.mult, ALU.mult).then_inc(h_pre, 1)
                for n in range(F2):
                    dve.wait_ge(silu_e, L * F2 + (n + 1))
                    link(TSC(nt[:], nv[:, n % 2, :], 1.0, None, ALU.add))
                    link(nc.vector.reciprocal(ts, nt[:]))
                    g = psum_of(A2, f"gt{n}")
                    TTN(tc, g[:, 0:S], ts, ALU.mult).then_inc(acc_drained[A2.bank(f"gt{n}")], 1)
                    dve.wait_ge(acc_drained[A2.bank(f"gt{n}")], A2.drained(f"gt{n}", L))
                    u = full(A2, f"up{n}", L)
                    TTN(big[:, n, :], u[:, 0:S], tc, ALU.mult).then_inc(a2_ready, 1)
                    dve.wait_ge(a2_ready, L * F2 + (n + 1))
                    dve.sem_inc(acc_drained[A2.bank(f"up{n}")], 1)
                for n in range(KC):
                    a = full(A2, f"dn{n}", L)
                    STT(x[:, n, :], a[:, 0:S], mod[:, 40 + n:41 + n], x[:, n, :], ALU.mult, ALU.add).then_inc(x_ready, 1)
                    dve.wait_ge(x_ready, L * (2 * KC) + (X2 + KC + n + 1))
                    dve.sem_inc(acc_drained[A2.bank(f"dn{n}")], 1)
                end_layer()

        @block.gpsimd
        def _(pool):
            own = [0]

            def link(ins):
                own[0] += 1
                ins.then_inc(pool_step, 1)
                pool.wait_ge(pool_step, own[0])

            TTN = nc.gpsimd.tensor_tensor
            pool.wait_ge(pad_ready, 1)
            with pool.Fori(0, LAYERS) as L:
                own[0] = 0
                w0 = 16
                for b, u in enumerate(("pa", "pb")):
                    pool.wait_ge(acc_drained[A2.bank(u)], A2.drained(u, L))
                    for j in range(2 if b == 0 else 4):
                        src, dst = (up_[:, b, :] if j == 0 else sw[:, (j - 1) % 2 * 2 + 1, :]), sw[:, j % 2 * 2 + 1, :]
                        link(TTN(dst[:, w0:w0 + S], src[:, w0:w0 + S], src[:, w0 - 2 ** j:w0 - 2 ** j + S], ALU.add))
                    lo, hi = sw[:, 1, :], sw[:, 3, :]
                    res = sw[:, 2 * b, w0:w0 + S]
                    TTN(res[0:64, :], lo[0:64, w0:w0 + S], invc[0:64, b, :], ALU.mult)
                    link(TTN(res[64:128, :], hi[64:128, w0:w0 + S], invc[64:128, b, :], ALU.mult))
                    link(TTN(res, res, up_[:, b, w0:w0 + S], ALU.subtract))
                    pool.sem_inc(pooled, 1)
                pool.sem_clear(pool_step)


def _blocks(w):
    k, n = w.shape
    b = np.zeros((P, k // P, P), np.float32)
    b[:, :, :n] = w.reshape(k // P, P, n).transpose(1, 0, 2)
    return b.reshape(P, -1)


def _wide(w):
    b = np.zeros((P, KC, 256), np.float32)
    b[:, :, :w.shape[1]] = w.reshape(KC, P, -1).transpose(1, 0, 2)
    return b.reshape(P, -1)


def _columns(v):
    return v.reshape(-1, P).T


def _stream(i):
    out = np.zeros((LAYERS * (T1 + T2), P, TILE), np.float32)
    for l in range(LAYERS):
        w = i["w_in"][l]
        cols = {}
        for r in range(3):
            cols[f"q{r}"] = np.r_[64 * r:64 * r + 64, 64 * (3 + r):64 * (3 + r) + 64]
        cols.update(kc=np.r_[384:512], vc=np.r_[512:640], ks=np.r_[640:768], kw=np.r_[896:1024],
                    cq0=np.r_[1170:1298], cq1=np.r_[1298:1426], ckv=np.r_[1426:1554], kpe=np.r_[1490:1586],
                    rqa=np.r_[1586:1714], rqb=np.r_[1714:1842], rka=np.r_[1906:2034], rkb=np.r_[2034:2162],
                    r4=np.r_[1842:1906, 2162:2226])
        tm = np.r_[768:896, 1024:1152, 1152:1170, 2226:2546, 2546:2866]
        w1k, w1v = i["cmp_w1_k"][l], i["cmp_w1_v"][l]
        for t, (kind, j) in enumerate(TILES1):
            o = out[l * T1 + t]
            if kind in cols:
                o[:, :1024], o[:, 1024:] = _blocks(w[:, cols[kind]]), _blocks(w[:, cols[j]])
            elif kind == "tm":
                o[:] = _wide(w[:, tm[256 * j:256 * j + 256]])
            elif kind == "cmpk":
                o[:] = w1k.reshape(16, P, P).transpose(1, 0, 2).reshape(P, -1)
            elif kind == "cmpv":
                o[:] = w1v.reshape(16, P, P).transpose(1, 0, 2).reshape(P, -1)
            elif kind == "small":
                o[:, UQ:UQ + 960] = i["mla_w_uq"][l].reshape(2, P, 480).transpose(1, 0, 2).reshape(P, -1)
                o[:, UKV:UKV + 640] = i["mla_w_ukv"][l]
                o[:, W2K:W2K + 128] = np.tile(i["cmp_w2_k"][l], (1, 2))
                o[:, W2V:W2V + 192] = np.tile(i["cmp_w2_v"][l], (1, 3))
            elif kind in ("wout", "up"):
                m = i["w_out" if kind == "wout" else "w_up"][l]
                for b in range(2):
                    o[:, 1024 * b:1024 * b + 1024] = _blocks(m[:, P * (2 * j + b):P * (2 * j + b + 1)])
            else:
                m = i["w_down"][l][2048 * (j % 2):2048 * (j % 2 + 1), P * (j // 2):P * (j // 2 + 1)]
                o[:] = _blocks(m)
        w = i["w_in_2"][l]
        cols = {f"q{b}": np.r_[1024 + P * b:1024 + P * b + P] for b in range(4)}
        cols.update({f"k{b}": np.r_[1536 + P * b:1536 + P * b + P] for b in range(4)})
        for b, u in enumerate(LATER2):
            cols[u] = np.r_[P * b:P * b + P]
        down = i["w_down_2"][l].reshape(F2, P, KC, P).transpose(2, 0, 1, 3).reshape(KC * F2, P, P)
        for t, (kind, j) in enumerate(TILES2):
            o = out[LAYERS * T1 + l * T2 + t]
            if kind in cols:
                o[:, :1024], o[:, 1024:] = _blocks(w[:, cols[kind]]), _blocks(w[:, cols[j]])
            elif kind == "v":
                o[:] = _wide(w[:, 2048 + 256 * j:2048 + 256 * j + 256])
            elif kind in ("ada", "wout", "gate"):
                m, at = {"ada": (i["w_ada_2"][l], 0), "wout": (i["w_out_2"][l], 0), "gate": (w, 2560)}[kind]
                for b in range(2):
                    c = at + P * (2 * j + b)
                    o[:, 1024 * b:1024 * b + 1024] = _blocks(m[:, c:c + P])
            elif kind in ("ppool", "pconv"):
                o[:] = i["p_pool_2" if kind == "ppool" else "p_conv_2"][l].reshape(2, P, D).transpose(1, 0, 2).reshape(P, -1)
            elif kind == "pattn":
                o[:] = i["p_attn_2"][l][:, 512 * j:512 * j + 512].reshape(4, P, 512).transpose(1, 0, 2).reshape(P, -1)
            elif kind == "gu":
                for b, m in enumerate((i["w_gate_2"][l], i["w_up_2"][l])):
                    o[:, 1024 * b:1024 * b + 1024] = _blocks(m[:, P * j:P * j + P])
            else:
                o[:] = down[16 * j:16 * j + 16].transpose(1, 0, 2).reshape(P, -1)
    return out


def kernel(**inputs):
    import concourse.bacc as _bacc
    from concourse import mybir as _mybir
    from concourse.bass_utils import run_bass_kernel_spmd as _run

    i = {k: np.asarray(v) for k, v in inputs.items()}
    vec1 = np.zeros((P, LAYERS, N_V1), np.float32)
    vec2 = np.zeros((P, LAYERS, N_V2), np.float32)
    for l in range(LAYERS):
        def put(arr, table, name, a):
            at, w = table[name]
            arr[:, l, at:at + w] = a
        put(vec1, VEC1, "ln1", _columns(i["ln1_gain"][l]))
        put(vec1, VEC1, "ln2", _columns(i["ln2_gain"][l]))
        put(vec1, VEC1, "qn", _columns(i["mla_q_norm"][l]))
        put(vec1, VEC1, "kvn", _columns(i["mla_kv_norm"][l]))
        put(vec1, VEC1, "posk", i["cmp_pos_k"][l].reshape(16, P).T)
        put(vec1, VEC1, "posv", i["cmp_pos_v"][l].reshape(16, P).T)
        put(vec1, VEC1, "gn", np.broadcast_to(i["ret_gn_gain"][l].reshape(1, 320), (P, 320)))
        put(vec2, VEC2, "n1", _columns(i["norm1_w_2"][l]))
        put(vec2, VEC2, "n2", _columns(i["norm2_w_2"][l]))
        put(vec2, VEC2, "bada", _columns(i["b_ada_2"][l]))
        put(vec2, VEC2, "pscale", _columns(i["pool_scale_2"][l]))
        put(vec2, VEC2, "conv", i["conv_w_2"][l].reshape(3, 2, P).transpose(2, 0, 1).reshape(P, 6))
        put(vec2, VEC2, "qn", np.tile(i["q_norm_w_2"][l], 2)[:, None])
        put(vec2, VEC2, "kn", np.tile(i["k_norm_w_2"][l], 2)[:, None])
        bd = np.zeros((P, 2, P), np.float32)
        for g in range(4):
            r = 64 * (g % 2)
            bd[r:r + 64, g // 2, r:r + 64] = i["pool_w_2"][l][g]
        put(vec2, VEC2, "poolw", bd.reshape(P, 256))
    once = np.concatenate([_columns(i["final_gain"]), _columns(i["c_2"][0])], axis=1)
    pos = np.stack([i["positions"][0], i["positions_2"][0]])
    arrays = {
        "consts": constants(), "vec1": vec1, "vec2": vec2, "once": np.ascontiguousarray(once),
        "pos": np.ascontiguousarray(np.broadcast_to(pos[None].astype(np.int32), (P, 2, S))),
        "xin": np.ascontiguousarray(i["x"][0].T.reshape(KC, P, S).transpose(1, 0, 2)),
        "stream": _stream(i),
    }
    nc = _bacc.Bacc("TRN2", target_bir_lowering=False, num_devices=1)
    args = [nc.dram_tensor(n, a.shape, _mybir.dt.from_np(a.dtype), kind="ExternalInput").ap() for n, a in arrays.items()]
    out = nc.dram_tensor("out", (P, KC, S), _mybir.dt.float32, kind="ExternalOutput").ap()
    trn_kernel(nc, *args, out)
    r = _run(nc, [arrays], core_ids=[0])
    got = r.results[0]["out"]
    return np.ascontiguousarray(got.transpose(1, 0, 2).reshape(D, S).T)[None]
```

```python
import concourse.bass as bass
from concourse import mybir
from contextlib import ExitStack
import numpy as np

F32 = mybir.dt.float32
I32 = mybir.dt.int32
F32R = mybir.dt.float32r
ALU = mybir.AluOpType
ACT = mybir.ActivationFunctionType
AX = mybir.AxisListType

P = 128
D = 1024
S = 256
TT = S // P
KC = D // P
LAYERS = 2
HD = 64
NSA_HEADS, REP, N_BRANCH = 6, 3, 3
CMP_LEN, CMP_STRIDE = 32, 16
N_CMP = (S - CMP_LEN) // CMP_STRIDE + 1
NP16 = 16
MLA_HEADS, MLA_Q, MLA_PE = 5, 96, 32
RET_HEADS = 5
D_FF1 = 4096
F1 = D_FF1 // P
ATTN_HEADS = 8
D_FF2 = 2816
F2 = D_FF2 // P
GATES = 3 * KC
EPS = 1e-6
NEG = -1e30
GELU_C = 0.7978845608028654

TILE = 2048
RING = 4
UNIT = TILE // 2
SPLIT = 4
assert KC * 256 == TILE

UNITS1 = ["q0", "q1", "q2", "ks", "kw", "kc", "vc", "cq0", "cq1", "ckv", "kpe", "rqa", "rqb", "rka", "rkb", "r4"]
ROPED1 = ["q0", "q1", "q2", "ks", "kw", "kc", "kpe", "rqa", "rqb", "rka", "rkb", "r4"]
UNITS2 = [f"q{b}" for b in range(4)] + [f"k{b}" for b in range(4)]
LATER2 = ["pa", "pb", "cua", "cub", "cba", "cbb", "cca", "ccb"]
MIXERS = ["P", "C", "A"]
VS, VW, GT, RV, RG = 0, 128, 256, 274, 594
TM1 = 914
TM_W = [256, 256, 256, TM1 - 768]

TILES1 = (
    [(UNITS1[2 * i], UNITS1[2 * i + 1]) for i in range(8)]
    + [("tm", j) for j in range(4)]
    + [("cmpk", 0), ("cmpv", 0), ("small", 0)]
    + [("ada", j) for j in range(24)]
    + [("wout", j) for j in range(4)]
    + [("up", j) for j in range(F1 // 2)]
    + [("down", j) for j in range(2 * KC)]
)
TILES2 = (
    [(UNITS2[2 * i], UNITS2[2 * i + 1]) for i in range(4)]
    + [("v", j) for j in range(2)]
    + [(LATER2[2 * i], LATER2[2 * i + 1]) for i in range(4)]
    + [("gate", j) for j in range(GATES // 2)]
    + [("mix", j) for j in range(KC // 2)]
    + [("wout", j) for j in range(4)]
    + [("gu", j) for j in range(F2)]
    + [("down", j) for j in range(KC * F2 // 16)]
)
T1, T2 = len(TILES1), len(TILES2)
WHOLE = ("cmpk", "cmpv", "small", "ada")


def last_user(tiles, t, half):
    kind, j = tiles[t]
    n = 2 * j + half if isinstance(j, int) else None
    if kind in ("tm", "v"):
        return f"{kind}{j}{TT - 1}"
    if kind in ("cmpk", "cmpv"):
        return "hid" + kind[-1]
    if kind == "small":
        return "vbd"
    if kind in ("wout", "up", "gate", "mix"):
        return {"wout": "wo", "up": "up", "gate": "g", "mix": "A"}[kind] + str(n)
    if kind == "gu":
        return ("gt", "up")[half] + str(j)
    if kind == "down":
        k = F1 if tiles is TILES1 else F2
        m = 8 * n + 7
        return f"dn{m // k}" + (f".{m % k}" if m % k != k - 1 else "")
    return (kind, j)[half]


def split_units(tiles):
    return [(t, half, last_user(tiles, t, half)) for t, (kind, _) in enumerate(tiles) if kind not in WHOLE
            for half in range(2)]


SU1, SU2 = split_units(TILES1), split_units(TILES2)
NU1, NU2 = len(SU1), len(SU2)

HEADS1 = [("slc", h) for h in range(NSA_HEADS)] + [("win", h) for h in range(NSA_HEADS)] \
    + [("mla", h) for h in range(MLA_HEADS)]
NH1, NH2 = len(HEADS1), ATTN_HEADS


def down_steps(kf):
    out = []
    for n in range(KC):
        for k in range(kf):
            if (n * kf + k) % 8 == 7 and k < kf - 1:
                out.append(f"dn{n}.{k}")
        out.append(f"dn{n}")
    return out


def order1():
    out = ["ss1"]
    for i, u in enumerate(UNITS1):
        out.append(u)
        if i >= 1 and UNITS1[i - 1] in ROPED1:
            out.append("rot_" + UNITS1[i - 1])
    out += ["ssq", "ssk"]
    for j in range(4):
        for t in range(TT):
            out.append(f"tm{j}{t}")
            if (j, t) == (0, 0):
                out.append("rot_r4")
    out += ["hidk", "hidv"]
    for h in range(MLA_HEADS):
        out.append(f"mq{h}")
        if h >= 1:
            out.append(f"rot_mq{h - 1}")
    out.append(f"rot_mq{MLA_HEADS - 1}")
    out += [f"mk{h}" for h in range(MLA_HEADS)] + [f"mv{t}" for t in range(TT)]
    out += ["kcc", "vbd", "cs0", "cs1", "ct", "co0", "co1"]
    for h in range(RET_HEADS + 1):
        if h < RET_HEADS:
            out.append(f"rs{h}")
        if h >= 1:
            out.append(f"ro{h - 1}")
    out += [f"mt{c}" for c in range(KC)] + [f"wo{n}" for n in range(KC)] + ["ss2"]
    out += [f"up{n}" for n in range(F1)]
    return out + down_steps(F1)


N_ADA = 24


def ada_at(i):
    steps = NH1 + 2
    return range(N_ADA * i // steps, N_ADA * (i + 1) // steps)


def gates_at(i):
    steps = NH2 + 2
    return range(GATES * i // steps, GATES * (i + 1) // steps)


def order2():
    out = ["ss1"]
    for b in range(len(UNITS2) + 3):
        if b < 8:
            out.append(UNITS2[b])
        if 1 <= b < 9:
            out.append("ss_" + UNITS2[b - 1])
        if b >= 3:
            out.append("rot_" + UNITS2[b - 3])
    out += [f"v{j}{t}" for j in range(2) for t in range(TT)] + LATER2 + ["pw0", "pw1"]
    for i in range(NH2 + 2):
        out += [f"g{n}" for n in gates_at(i)]
    out += [f"yt{c}" for c in range(4)]
    for n in range(KC):
        out += [f"{m}{n}" for m in MIXERS]
    out += [f"wo{n}" for n in range(KC)] + ["ss2"]
    for n in range(F2):
        out += [f"gt{n}", f"up{n}"]
    return out + down_steps(F2)


BANKS = 4


class Turns:

    def __init__(self, names, full, drained):
        self.names, self.base, self.free_base = names, full, drained
        self.at = {n: i for i, n in enumerate(names)}
        assert len(self.at) == len(names)
        self.total = len(names)
        self.turn = {n: i for i, n in enumerate([n for n in names if "." not in n])}
        self.uses = [len([i for i in range(len(self.turn)) if i % BANKS == b]) for b in range(BANKS)]

    def bank(self, name):
        return self.turn[name] % BANKS

    def full(self, name, layer):
        return layer * self.total + (self.base + self.at[name] + 1)

    def free(self, name, layer):
        b = self.bank(name)
        return layer * self.uses[b] + (self.free_base[b] + self.turn[name] // BANKS)

    def drained(self, name, layer):
        return self.free(name, layer) + 1

    def after(self, layers):
        return self.base + layers * self.total, [f + layers * u for f, u in zip(self.free_base, self.uses)]


A1 = Turns(order1(), 0, [1] * BANKS)
AF = Turns(["ssf"], *A1.after(LAYERS))
A2 = Turns(order2(), *AF.after(1))

CONSTS = {}


def _place(table, items):
    at = 0
    for name, width in items:
        table[name] = (at, width)
        at += width
    return at


N_CONST = _place(CONSTS, [("ident", 128), ("rotp", 128), ("rotm", 128), ("rotr", 128), ("half", 128), ("ones", 128),
                          ("mask", 384), ("cmask", 192), ("ckeep", 192), ("bmask", 6), ("inv", 4),
                          ("decay", RET_HEADS * S), ("invc", 2 * S)])
VEC1, VEC2 = {}, {}
N_V1 = _place(VEC1, [("ln1", 8), ("ln2", 8), ("qn", 2), ("kvn", 1), ("posk", 16), ("posv", 16), ("gn", 320)])
N_V2 = _place(VEC2, [("n1", 8), ("n2", 8), ("pscale", 2), ("conv", 6), ("qn", 1), ("kn", 1), ("poolw", 256),
                      ("bada", 48)])
N_ONCE = KC + D
UQ, UKV, W2K, W2V = 0, 960, 1600, 1728


def constants():
    c = np.zeros((P, N_CONST), np.float32)

    def put(name, a):
        at, w = CONSTS[name]
        c[:a.shape[0], at:at + w] = a.reshape(a.shape[0], w)

    def rotation(starts, half):
        m = np.zeros((P, P), np.float32)
        for s in starts:
            for i in range(half):
                m[s + half + i, s + i] = -1.0
                m[s + i, s + half + i] = 1.0
        return m

    i = np.arange(P)
    put("ident", np.eye(P, dtype=np.float32))
    put("rotp", rotation((0, 64), 8))
    put("rotm", rotation((64,), 16))
    put("rotr", rotation((0, 64), 32))
    put("half", (i[:, None] // HD == i[None, :] // HD).astype(np.float32))
    put("ones", np.ones((P, P), np.float32))
    tri = np.where(i[None, :] > i[:, None], NEG, 0.0)
    put("mask", np.concatenate([tri, np.zeros((P, P)), tri], axis=1))
    n = np.arange(NP16)
    t = (np.arange(TT)[None, :] * P + i[:, None])[:, :, None]
    seen = (n * CMP_STRIDE + CMP_LEN - 1 <= t) & (n < N_CMP)
    seen = np.broadcast_to(seen[:, :, None, :], (P, TT, NSA_HEADS, NP16))
    put("cmask", np.where(seen, 0.0, NEG).reshape(P, 192))
    put("ckeep", seen.astype(np.float32).reshape(P, 192))
    r = np.arange(NSA_HEADS * NP16)
    put("bmask", ((r[:, None] // NP16 == np.arange(NSA_HEADS)[None, :]) & (r[:, None] % NP16 < N_CMP)).astype(np.float32))
    inv = np.zeros((P, 4), np.float32)
    e16, e32, e64 = (np.arange(0, d, 2, dtype=np.float32) / np.float32(d) for d in (16, 32, 64))
    power = lambda base, e: np.power(base, e.astype(np.float64)).astype(np.float32)
    one = np.float32(1.0)
    for s in (0, 64):
        inv[s:s + 16, 0] = np.tile(one / power(5e5, e16), 2)
        inv[s:s + 64, 2] = np.tile(one / power(1e4, e64), 2)
        inv[s:s + 16, 3] = np.tile(power(5e5, -e16), 2)
    inv[64:96, 1] = np.tile(one / power(5e5, e32), 2)
    put("inv", inv)
    g = np.log(1.0 - 2.0 ** (-5.0 - np.arange(RET_HEADS)))
    diff = (np.arange(S)[None, :] - i[:, None])[:, None, :]
    put("decay", np.where(diff >= 0, np.exp(np.maximum(diff, 0) * g[None, :, None]), 0.0) * HD ** -0.5)
    win = np.array([[2, 8], [4, 16]])
    w = win[i // HD]
    put("invc", 1.0 / np.minimum(np.arange(S)[None, None, :] + 1, w[:, :, None]))
    return c


def trn_kernel(nc, consts, vec1, vec2, once, pos, xin, stream, out):
    ctx = ExitStack()
    with ctx:
        def sb(name, shape, dt=F32):
            return ctx.enter_context(nc.sbuf_tensor(name, shape, dt))

        def bank(name):
            return ctx.enter_context(nc.psum_tensor(name, [P, 512], F32))

        def sem(name):
            return ctx.enter_context(nc.semaphore(name))

        cst = sb("cst", [P, N_CONST])
        v1all = sb("v1all", [P, LAYERS, N_V1])
        v1 = sb("v1", [P, N_V1])
        v2all = sb("v2all", [P, LAYERS, N_V2])
        v2 = sb("v2", [P, N_V2])
        onc = sb("onc", [P, N_ONCE])
        trig = sb("trig", [P, 2, 4, S])
        ring = sb("ring", [P, RING, TILE])
        x = sb("x", [P, KC, S])
        wH = sb("wH", [P, SPLIT, UNIT], F32R)
        wL = sb("wL", [P, SPLIT, UNIT], F32R)
        h_at = nc.sbuf_base
        hH = sb("hH", [P, KC, S], F32R)
        hL = sb("hL", [P, KC, S], F32R)
        BIG = 24 * S
        WORK = F1 * S * 2 - BIG
        region_at = nc.sbuf_base
        region = sb("region", [P, F1 * S * 2])

        def rounded(name, at, k):
            return nc.alloc_sbuf_tensor_at(name, [P, k, S], F32R, offset=region_at + 4 * at)

        aH, aL = rounded("aH", 0, F1), rounded("aL", F1 * S, F1)
        big = region[:, 0:BIG].rearrange("p (c s) -> p c s", s=S)
        work = region[:, BIG:BIG + WORK]
        nv = sb("nv", [P, 2, S])
        ny = sb("ny", [P, 2, S])
        nt = sb("nt", [P, S])
        rstd = sb("rstd", [P, S])
        tcs = sb("tcs", [P, 2, S])
        tss = sb("tss", [P, 2, S])
        tc, ts = tcs[:, 0, :], tss[:, 0, :]
        tmp4 = [tcs[:, 0, :], tcs[:, 1, :], tss[:, 0, :], tss[:, 1, :]]
        sq_in = work[:, 0:KC * S].rearrange("p (c s) -> p c s", c=KC)
        sq_h = nc.alloc_sbuf_tensor_at("sq_h", [P, KC, S], F32, offset=h_at)
        cursor = [0]

        def piece(*shape):
            n = 1
            for s_ in shape:
                n *= s_
            a = work[:, cursor[0]:cursor[0] + n]
            cursor[0] += n
            assert cursor[0] <= WORK
            if len(shape) == 2:
                a = a.rearrange("p (a b) -> p a b", a=shape[0])
            elif len(shape) == 3:
                a = a.rearrange("p (a b c) -> p a b c", a=shape[0], b=shape[1])
            return a

        rope1 = piece(11, S)
        tokm = piece(TT, TM1)
        qm = piece(MLA_HEADS, S)
        km = piece(MLA_HEADS, S)
        vm = piece(TT, 320)
        hid = piece(2, 32)
        gel = piece(3, 64)
        kcT = piece(NP16)
        grep = piece(2, 96)
        vbd = piece(384)
        pc = piece(192)
        pcT = piece(S)
        cst12 = piece(3, 12)
        gate = piece(TT, 18)
        gnst = piece(6, 10)
        cursor[0] = 0
        qk2 = piece(8, S)
        vv = piece(TT, 512)
        ya = piece(TT, 512)
        up_ = piece(2, 16 + S)
        sw = piece(4, 16 + S)
        yc = piece(2, S)
        cu = piece(2, S)
        cb = piece(2, S)
        cv = piece(2, 2 + S)
        cursor[0] = 0
        cursor[0] = 2048
        merged = piece(4, S)
        y1H = rounded("y1H", BIG + 8192, 4)
        y1L = rounded("y1L", BIG + 9216, 4)
        y2H = rounded("y2H", BIG + 0, 4)
        y2L = rounded("y2L", BIG + 1024, 4)
        modall = sb("modall", [P, LAYERS, 48])
        mod = sb("mod", [P, 48])
        mods = sb("mods", [P, 3, KC])
        adac = sb("adac", [P, 48])
        cb2 = onc[:, KC:KC + D]
        sm = sb("sm", [P, 2, 384])
        pr = sb("pr", [P, 2, 384])
        prT = sb("prT", [P, 2, 384])
        latsq3 = pr[:, :, :].rearrange("p a b -> p (a b)").rearrange("p (c s) -> p c s", c=3)
        nmax = sb("nmax", [P, NH1, 2])
        psumv = sb("psumv", [P, NH1, 2])
        coef = sb("coef", [P, NH1, 2])
        ada_t = big[:, 0:4, :].rearrange("p c s -> p (c s)")
        ada_v = big[:, 4:8, :].rearrange("p c s -> p (c s)")
        ada_p = [big[:, 8 + 4 * j:12 + 4 * j, :].rearrange("p c s -> p (c s)") for j in range(2)]
        sq2 = big[:, 8:16, :]
        raw = big[:, 0:16, :]
        mixed = big[:, 16:24, :].rearrange("p a s -> p (a s)").rearrange("p (t f) -> p t f", t=TT)
        fk = [big[:, 16 + 2 * j:18 + 2 * j, :].rearrange("p a s -> p (a s)")[:, 0:480]
              .rearrange("p (m g n) -> p m g n", m=16, g=2) for j in range(2)]
        xk = [big[:, 20 + 2 * j:22 + 2 * j, :] for j in range(2)]
        cqn = big[:, 12:15, :]

        acc = [bank(f"acc{i}") for i in range(BANKS)]
        ps_s = [bank(f"ps_s{i}") for i in range(2)]
        ps_t = bank("ps_t")
        ps_o = bank("ps_o")

        def C(name, rows=P):
            at, w = CONSTS[name]
            return cst[0:rows, at:at + w]

        def V1(name, i=None):
            at, w = VEC1[name]
            return v1[:, at:at + w] if i is None else v1[:, at + i:at + i + 1]

        def V2(name, i=None):
            at, w = VEC2[name]
            return v2[:, at:at + w] if i is None else v2[:, at + i:at + i + 1]

        decay = C("decay").rearrange("p (h s) -> p h s", h=RET_HEADS)
        invc = C("invc").rearrange("p (b s) -> p b s", b=2)

        inputs_in = sem("inputs_in")
        got = [sem(f"got{i}") for i in range(RING)]
        acc_full = sem("acc_full")
        acc_drained = [sem(f"acc_drained{i}") for i in range(BANKS)]
        x_ready = sem("x_ready")
        vec_ready = sem("vec_ready")
        trig_arg = sem("trig_arg")
        trig_ready = sem("trig_ready")
        sq_ready = sem("sq_ready")
        y_ready = sem("y_ready")
        h_ready = sem("h_ready")
        h_pre = sem("h_pre")
        hh_ready = sem("hh_ready")
        hi_ready = sem("hi_ready")
        lo_ready = sem("lo_ready")
        tH_ready = sem("tH_ready")
        aT_ready = sem("aT_ready")
        aH_ready = sem("aH_ready")
        ypH_ready = sem("ypH_ready")
        ycf_ready, ycH_ready = sem("ycf_ready"), sem("ycH_ready")
        mgH_ready = sem("mgH_ready")
        tanh_ready = sem("tanh_ready")
        a2H_ready = sem("a2H_ready")
        mg_ready = sem("mg_ready")
        rope_ready = sem("rope_ready")
        lat_ready = sem("lat_ready")
        latsq = sem("latsq")
        f_ready = sem("f_ready")
        xk_ready = sem("xk_ready")
        ge = sem("ge")
        hid_ready = sem("hid_ready")
        gel_ready = sem("gel_ready")
        grep_ready = sem("grep_ready")
        km_ready = sem("km_ready")
        kcT_ready = sem("kcT_ready")
        vbd_ready = sem("vbd_ready")
        csub = sem("csub")
        cexp = sem("cexp")
        pc_ready = sem("pc_ready")
        gexp = sem("gexp")
        gate_ready = sem("gate_ready")
        rw_ready = sem("rw_ready")
        gn_v = sem("gn_v")
        gn_y = sem("gn_y")
        mixed_ready = sem("mixed_ready")
        mixT_ready = sem("mixT_ready")
        a_ready = sem("a_ready")
        s_full, s_drained = sem("s_full"), sem("s_drained")
        nmax_ready, p_ready = sem("nmax_ready"), sem("p_ready")
        pt_full, pt_copied = sem("pt_full"), sem("pt_copied")
        o_full, o_drained = sem("o_full"), sem("o_drained")
        ctanh, x_in = sem("ctanh"), sem("x_in")
        ada_dve, ada_pool, ada_act = sem("ada_dve"), sem("ada_pool"), sem("ada_act")
        mod_ready = sem("mod_ready")
        raw2_sq = sem("raw2_sq")
        qn2_ready = sem("qn2_ready")
        qk2_ready = sem("qk2_ready")
        pool_in = sem("pool_in")
        pad_ready = sem("pad_ready")
        pooled = sem("pooled")
        yc_ready = sem("yc_ready")
        merged_ready = sem("merged_ready")
        ya_ready = sem("ya_ready")
        a2_ready = sem("a2_ready")
        stored = sem("stored")
        dve_step, act_step, pool_step = sem("dve_step"), sem("act_step"), sem("pool_step")

        ROPE1 = {"q0": 0, "q1": 1, "q2": 2, "ks": 3, "kw": 4, "rqa": 5, "rqb": 6, "rka": 7, "rkb": 8}

        def q_nsa(hh):
            g, r = hh // REP, hh % REP
            return slice(64 * g, 64 * g + 64), r

        def ret_q(hh):
            return (slice(64 * (hh % 2), 64 * (hh % 2) + 64), 5 + hh // 2) if hh < 4 else (slice(0, 64), 9)

        def ret_k(hh):
            return (slice(64 * (hh % 2), 64 * (hh % 2) + 64), 7 + hh // 2) if hh < 4 else (slice(0, 64), 10)

        def head1(i):
            kind, hh = HEADS1[i]
            if kind == "mla":
                return qm[0:96, hh, :], km[0:96, hh, :], [vm[:, t, 64 * hh:64 * hh + 64] for t in range(TT)]
            rows, r = q_nsa(hh)
            g = hh // REP
            c = (VS if kind == "slc" else VW) + 64 * g
            return (rope1[rows, r, :], rope1[rows, 3 if kind == "slc" else 4, :],
                    [tokm[:, t, c:c + 64] for t in range(TT)])

        def scale1(i):
            return 96 ** -0.5 if HEADS1[i][0] == "mla" else HD ** -0.5

        def head2(i):
            rows = slice(64 * (i % 2), 64 * (i % 2) + 64)
            return qk2[rows, i // 2, :], qk2[rows, 4 + i // 2, :], [vv[:, t, 64 * i:64 * i + 64] for t in range(TT)]

        X2 = LAYERS * 2 * KC + KC
        X_FINAL = X2 + (2 * LAYERS - 1) * KC
        H2 = LAYERS * 2 * KC
        Q2 = LAYERS * 8 + 4
        Y1, Y2N = 4, 10
        YF, Y2 = LAYERS * Y1, LAYERS * Y1 + 1
        VISITS2 = [LAYERS * len([u for u in range(T1) if u % RING == s_]) for s_ in range(RING)]
        M2 = LAYERS * KC
        r4 = [nv[:, 0, :], nv[:, 1, :], ny[:, 0, :], ny[:, 1, :]]
        pair2 = [nt[:, :], rstd[:, :]]
        LO2 = LAYERS * NU1

        def ro_all(k):
            return big[:, 3 * k:3 * k + 3, :].rearrange("p a s -> p (a s)")[:, 0:640]

        def ro_(hh):
            return ro_all(0).rearrange("p (t f) -> p t f", t=TT)[:, :, 64 * hh:64 * hh + 64]

        def rgx_():
            return ro_all(1).rearrange("p (t f) -> p t f", t=TT)

        block = ctx.enter_context(nc.Block())

        @block.sync
        def _(sp):
            sp.dma_start(x[:], xin).then_inc(x_in, 16)
            sp.dma_start(cst[:], consts).then_inc(inputs_in, 16)

            def load(slot, at):
                sp.dma_start(ring[:, slot, :], stream[at]).then_inc(got[slot], 16)

            def wait_free(tiles, turns, units, lo_base, layer, t):
                if tiles[t][0] == "ada":
                    sp.wait_ge(ada_pool, layer * N_ADA + (tiles[t][1] + 1))
                elif tiles[t][0] in WHOLE:
                    sp.wait_ge(acc_full, turns.full(last_user(tiles, t, 1), layer))
                else:
                    n = max(u for u, (tile_, _, _) in enumerate(units) if tile_ == t)
                    sp.wait_ge(lo_ready, layer * len(units) + (lo_base + n + 1))

            def rest(tiles, turns, units, lo_base, layer, first):
                for t in range(RING, len(tiles)):
                    wait_free(tiles, turns, units, lo_base, layer, t - RING)
                    load(t % RING, first + t)

            def ahead(tiles, turns, units, lo_base, layer, first):
                n = len(tiles)
                for t in range(n - RING, n):
                    wait_free(tiles, turns, units, lo_base, layer, t)
                    load(t % RING, first + n + t % RING)

            sp.dma_start(v2all[:], vec2).then_inc(inputs_in, 16)
            for s_ in range(RING):
                load(s_, s_)
            with sp.Fori(0, LAYERS) as layer:
                rest(TILES1, A1, SU1, 0, layer, layer * T1)
                ahead(TILES1, A1, SU1, 0, layer, layer * T1)
            with sp.Fori(0, LAYERS - 1) as layer:
                rest(TILES2, A2, SU2, LO2, layer, layer * T2 + LAYERS * T1)
                ahead(TILES2, A2, SU2, LO2, layer, layer * T2 + LAYERS * T1)
            rest(TILES2, A2, SU2, LO2, LAYERS - 1, (LAYERS - 1) * T2 + LAYERS * T1)
            for c in range(0, KC, 2):
                sp.wait_ge(x_ready, X_FINAL + c + 2)
                sp.dma_start(out[:, c:c + 2, :], x[:, c:c + 2, :]).then_inc(stored, 16)
            sp.wait_ge(stored, 16 * KC // 2)


        @block.tensor
        def _(pe):
            for b in range(BANKS):
                pe.sem_inc(acc_drained[b], 1)
            pe.wait_ge(inputs_in, 16 * 5)

            state = {}

            def enter(turns, layer, tiles, visits_base, units, lo_base):
                state.update(turns=turns, layer=layer, next=0, tiles=tiles, visits=visits_base, units=units,
                             lo_base=lo_base, unit=0)

            def open_acc(name):
                tn = state["turns"]
                assert tn.turn[name] == state["next"], name
                state["next"] += 1
                pe.wait_ge(acc_drained[tn.bank(name)], tn.free(name, state["layer"]))
                return acc[tn.bank(name)]

            def tile(kind, j):
                t = state["tiles"].index((kind, j))
                slot = t % RING
                n = len([u for u in range(len(state["tiles"])) if u % RING == slot])
                pe.wait_ge(got[slot], state["layer"] * (16 * n) + 16 * (state["visits"][slot] + t // RING + 1))
                return ring[:, slot, :]

            def next_unit():
                u = state["unit"]
                state["unit"] += 1
                pe.wait_ge(lo_ready, state["layer"] * len(state["units"]) + (state["lo_base"] + u + 1))
                return wH[:, u % SPLIT, :], wL[:, u % SPLIT, :]

            def split_product(out, w, y, first, last):
                pe.matmul(out, w[0], y[0], start=first, stop=False)
                pe.matmul(out, w[0], y[1], start=False, stop=False)
                return pe.matmul(out, w[1], y[0], start=False, stop=last)

            def blocks(parts):
                return [v.rearrange("p (c n) -> p c n", n=P) for v in parts]

            def project(name, y, h_base=None):
                wh, wl = blocks(next_unit())
                a = open_acc(name)
                for c in range(KC):
                    if h_base is not None:
                        pe.wait_ge(h_ready, state["layer"] * (2 * KC) + (h_base + c + 1))
                    last = split_product(a[:, 0:S], (wh[:, c, :], wl[:, c, :]), y(c), c == 0, c == KC - 1)
                last.then_inc(acc_full, 1)

            def project_tokens(kind, j, n):
                parts = [[v.rearrange("p (c n) -> p c n", n=256) for v in next_unit()] for _ in range(2)]
                for t in range(TT):
                    a = open_acc(f"{kind}{j}{t}")
                    for c in range(KC):
                        wh, wl = (v[:, c % 4, 0:n] for v in parts[c // 4])
                        hh, hl = hH[:, c, t * P:(t + 1) * P], hL[:, c, t * P:(t + 1) * P]
                        last = split_product(a[:, 0:n], (hh, hl), (wh, wl), c == 0, c == KC - 1)
                    last.then_inc(acc_full, 1)
                    if (kind, j, t) == ("tm", 0, 0):
                        rot1("r4")

            def down(kf, ready, base):
                wh = wl = None
                for n in range(KC):
                    a = open_acc(f"dn{n}")
                    for k in range(kf):
                        m = n * kf + k
                        if m % 8 == 0:
                            wh, wl = blocks(next_unit())
                        if n == 0:
                            pe.wait_ge(ready, state["layer"] * kf + (base + k + 1))
                        last = split_product(a[:, 0:S], (wh[:, m % 8, :], wl[:, m % 8, :]), (aH[:, k, :], aL[:, k, :]),
                                             k == 0, k == kf - 1)
                        if m % 8 == 7 and k < kf - 1:
                            last.then_inc(acc_full, 1)
                    last.then_inc(acc_full, 1)

            def sum_squares(name, base):
                sq = sq_in if name == "ss2" else sq_h
                a = open_acc(name)
                for c in range(KC):
                    if c % 2 == 0:
                        pe.wait_ge(sq_ready, base + c // 2 + 1)
                    last = pe.matmul(a[:, 0:S], C("ones"), sq[:, c, :], start=c == 0, stop=c == KC - 1)
                last.then_inc(acc_full, 1)

            def rotate(name, m, src, rows=slice(0, P)):
                a = open_acc("rot_" + name)
                pe.matmul(a[rows, 0:S], m, src, start=True, stop=True).then_inc(acc_full, 1)

            def drained(name):
                tn = state["turns"]
                pe.wait_ge(acc_drained[tn.bank(name)], tn.drained(name, state["layer"]))

            def attention(head, n, base, filler):
                L = state["layer"]
                for i in range(n + 2):
                    if i < n:
                        q, k, _ = head(i)
                        pe.wait_ge(s_drained, L * n + (base + i + 1))
                        b = ps_s[i % 2]
                        pe.matmul(b[:, 0:P], q[:, 0:P], k[:, 0:P], start=True, stop=True)
                        pe.matmul(b[:, P:3 * P], q[:, P:S], k, start=True, stop=True).then_inc(s_full, 1)
                    if 1 <= i <= n:
                        j = i - 1
                        pe.wait_ge(p_ready, L * n + (base + j + 1))
                        pe.wait_ge(pt_copied, L * n + (base + j + 1))
                        for c in range(3):
                            last = pe.transpose(ps_t[:, c * P:(c + 1) * P], pr[:, j % 2, c * P:(c + 1) * P], C("ident"))
                        last.then_inc(pt_full, 1)
                    if i >= 2:
                        j = i - 2
                        _, _, v = head(j)
                        pe.wait_ge(pt_copied, L * n + (base + j + 2))
                        pe.wait_ge(o_drained, L * n + (base + j + 1))
                        pe.matmul(ps_o[:, 0:HD], prT[:, j % 2, 0:P], v[0], start=True, stop=True)
                        pe.matmul(ps_o[:, HD:2 * HD], prT[:, j % 2, P:2 * P], v[0], start=True, stop=False)
                        pe.matmul(ps_o[:, HD:2 * HD], prT[:, j % 2, 2 * P:3 * P], v[1], start=False, stop=True)\
                            .then_inc(o_full, 1)
                    filler(i)

            pe.sem_inc(s_drained, 2)
            pe.sem_inc(pt_copied, 1)
            pe.sem_inc(o_drained, 1)

            hs = lambda c: (hH[:, c, :], hL[:, c, :])
            with pe.Fori(0, LAYERS) as L:
                enter(A1, L, TILES1, [0] * RING, SU1, 0)
                sum_squares("ss1", L * 8)

                def rot1(u):
                    drained(u)
                    i = UNITS1.index(u)
                    if u == "kpe":
                        rotate(u, C("rotm")[0:96, 0:96], raw[0:96, i, :], slice(0, 96))
                    else:
                        rotate(u, C("rotr" if u[0] == "r" else "rotp"), raw[:, i, :])

                for i, u in enumerate(UNITS1):
                    project(u, hs, 0 if i == 0 else None)
                    if i >= 1 and UNITS1[i - 1] in ROPED1:
                        rot1(UNITS1[i - 1])
                pe.wait_ge(latsq, L * 3 + 2)
                a = open_acc("ssq")
                pe.matmul(a[:, 0:S], C("ones"), latsq3[:, 0, :], start=True, stop=False)
                pe.matmul(a[:, 0:S], C("ones"), latsq3[:, 1, :], start=False, stop=True).then_inc(acc_full, 1)
                pe.wait_ge(latsq, L * 3 + 3)
                a = open_acc("ssk")
                pe.matmul(a[:, 0:S], C("ones"), latsq3[:, 2, :], start=True, stop=True).then_inc(acc_full, 1)
                for j in range(4):
                    project_tokens("tm", j, TM_W[j])
                for j, kind in enumerate(("k", "v")):
                    tl = tile("cmp" + kind, 0).rearrange("p (m n) -> p m n", m=16)
                    pe.wait_ge(f_ready, L * 2 + (j + 1))
                    a = open_acc("hid" + kind)
                    for m in range(16):
                        last = pe.matmul(a[:, 0:30], tl[:, m, :], fk[j][:, m, :, :].rearrange("p g n -> p (g n)"),
                                         start=m == 0, stop=m == 15)
                    last.then_inc(acc_full, 1)
                tl = tile("small", 0)
                uq = tl[:, UQ:UQ + 960].rearrange("p (c n) -> p c n", c=2)
                pe.wait_ge(lat_ready, L * 3 + 2)
                for hh in range(MLA_HEADS + 1):
                    if hh < MLA_HEADS:
                        a = open_acc(f"mq{hh}")
                        for c in range(2):
                            last = pe.matmul(a[0:96, 0:S], uq[:, c, 96 * hh:96 * hh + 96], cqn[:, c, :],
                                             start=c == 0, stop=c == 1)
                        last.then_inc(acc_full, 1)
                    if hh >= 1:
                        drained(f"mq{hh - 1}")
                        rotate(f"mq{hh - 1}", C("rotm")[0:96, 0:96], qm[0:96, hh - 1, :], slice(0, 96))
                pe.wait_ge(lat_ready, L * 3 + 3)
                ukv = tl[:, UKV:UKV + 640]
                for hh in range(MLA_HEADS):
                    a = open_acc(f"mk{hh}")
                    pe.matmul(a[0:64, 0:S], ukv[:, 128 * hh:128 * hh + 64], cqn[:, 2, :], start=True, stop=True)\
                        .then_inc(acc_full, 1)
                for t in range(TT):
                    a = open_acc(f"mv{t}")
                    pe.matmul(a[:, 0:320], cqn[:, 2, t * P:(t + 1) * P],
                              ukv.rearrange("p (h n) -> p h n", h=MLA_HEADS)[:, :, 64:128], start=True, stop=True)\
                        .then_inc(acc_full, 1)
                pe.wait_ge(gel_ready, L + 1)
                a = open_acc("kcc")
                pe.matmul(a[:, 0:32], tl[:, W2K:W2K + 128], hid[:, 0, :], start=True, stop=True).then_inc(acc_full, 1)
                pe.wait_ge(grep_ready, L + 1)
                a = open_acc("vbd")
                for g in range(2):
                    last = pe.matmul(a[0:96, 192 * g:192 * g + 192], grep[:, g, :], tl[:, W2V:W2V + 192],
                                     start=True, stop=True)
                last.then_inc(acc_full, 1)
                pe.wait_ge(kcT_ready, L * 2 + 2)
                pe.wait_ge(rope_ready, L * 17 + 3)
                for g in range(2):
                    a = open_acc(f"cs{g}")
                    for t in range(TT):
                        for r in range(REP):
                            rows = slice(64 * g, 64 * g + 64)
                            at = 48 * t + 16 * r
                            last = pe.matmul(a[:, at:at + 16], rope1[rows, r, t * P:(t + 1) * P], kcT[rows, :],
                                             start=True, stop=True)
                    last.then_inc(acc_full, 1)
                pe.wait_ge(pc_ready, L + 1)
                a = open_acc("ct")
                for t in range(TT):
                    last = pe.transpose(a[0:96, t * P:(t + 1) * P], pc[:, 96 * t:96 * t + 96], C("ident"))
                last.then_inc(acc_full, 1)
                drained("ct")
                pe.wait_ge(vbd_ready, L + 1)
                for t in range(TT):
                    a = open_acc(f"co{t}")
                    pe.matmul(a[:, 0:384], pcT[0:96, t * P:(t + 1) * P], vbd[0:96, :], start=True, stop=True)\
                        .then_inc(acc_full, 1)
                pe.wait_ge(rope_ready, L * 17 + 12)
                for hh in range(RET_HEADS + 1):
                    if hh < RET_HEADS:
                        a = open_acc(f"rs{hh}")
                        rq, iq = ret_q(hh)
                        rk, ik = ret_k(hh)
                        pe.matmul(a[:, 0:S], rope1[rk, ik, 0:P], rope1[rq, iq, :], start=True, stop=True)
                        pe.matmul(a[:, S:S + P], rope1[rk, ik, P:S], rope1[rq, iq, P:S], start=True, stop=True)\
                            .then_inc(acc_full, 1)
                    if hh >= 1:
                        j = hh - 1
                        pe.wait_ge(rw_ready, L * RET_HEADS + (j + 1))
                        a = open_acc(f"ro{j}")
                        w = sm[:, j % 2, :]
                        v = [tokm[:, t, RV + 64 * j:RV + 64 * j + 64] for t in range(TT)]
                        pe.matmul(a[:, 0:HD], w[:, 0:P], v[0], start=True, stop=True)
                        pe.matmul(a[:, HD:2 * HD], w[:, P:S], v[0], start=True, stop=False)
                        pe.matmul(a[:, HD:2 * HD], w[:, S:S + P], v[1], start=False, stop=True).then_inc(acc_full, 1)
                pe.wait_ge(km_ready, L + 1)
                pe.wait_ge(rope_ready, L * 17 + 17)

                attention(head1, NH1, 0, lambda i: None)
                pe.wait_ge(mixed_ready, L + 1)
                for c in range(KC):
                    a = open_acc(f"mt{c}")
                    for t in range(TT):
                        last = pe.transpose(a[:, t * P:(t + 1) * P], mixed[:, t, c * P:(c + 1) * P], C("ident"))
                    last.then_inc(acc_full, 1)
                for c in range(KC):
                    drained(f"mt{c}")
                for n in range(KC):
                    project(f"wo{n}", hs)
                sum_squares("ss2", L * 8 + 4)
                for n in range(F1):
                    project(f"up{n}", hs, KC if n == 0 else None)
                down(F1, a_ready, 0)

            enter(AF, 0, TILES2, VISITS2, SU2, LO2)
            sum_squares("ssf", LAYERS * 8)

            with pe.Fori(0, LAYERS) as L:
                enter(A2, L, TILES2, VISITS2, SU2, LO2)
                sum_squares("ss1", L * 8 + Q2)
                for b in range(len(UNITS2) + 3):
                    if b < 8:
                        project(UNITS2[b], hs, H2 if b == 0 else None)
                    if 1 <= b < 9:
                        pe.wait_ge(raw2_sq, L * 8 + b)
                        a = open_acc("ss_" + UNITS2[b - 1])
                        pe.matmul(a[:, 0:S], C("half"), sq2[:, b - 1, :], start=True, stop=True).then_inc(acc_full, 1)
                    if b >= 3:
                        pe.wait_ge(qn2_ready, L * 8 + (b - 2))
                        rotate(UNITS2[b - 3], C("rotp"), qk2[:, b - 3, :])
                for j in range(2):
                    project_tokens("v", j, 256)
                for u in LATER2:
                    project(u, hs)
                for b in range(2):
                    pe.wait_ge(pooled, L * 2 + (b + 1))
                    a = open_acc(f"pw{b}")
                    pe.matmul(a[:, 0:S], V2("poolw")[:, 128 * b:128 * b + 128], sw[:, 2 * b, 16:16 + S],
                              start=True, stop=True).then_inc(acc_full, 1)

                def gates(i):
                    for n in gates_at(i):
                        project(f"g{n}", hs)

                pe.wait_ge(qk2_ready, L * 8 + 8)
                drained(f"v{1}{1}")
                drained(f"v{1}{0}")
                attention(head2, NH2, LAYERS * NH1, gates)
                pe.wait_ge(ya_ready, L + 1)
                for c in range(4):
                    a = open_acc(f"yt{c}")
                    for t in range(TT):
                        last = pe.transpose(a[:, t * P:(t + 1) * P], ya[:, t, c * P:(c + 1) * P], C("ident"))
                    last.then_inc(acc_full, 1)
                for name in ["pw0", "pw1"] + [f"yt{c}" for c in range(4)]:
                    drained(name)
                pe.wait_ge(yc_ready, L * 2 + 2)
                for n in range(KC):
                    wh, wl = blocks(next_unit())
                    for name, first, k in (("P", 0, 2), ("C", 2, 2), ("A", 4, 4)):
                        a = open_acc(f"{name}{n}")
                        for c in range(first, first + k):
                            yh, yl = (y1H, y1L) if c < 4 else (y2H, y2L)
                            last = split_product(a[:, 0:S], (wh[:, c, :], wl[:, c, :]), (yh[:, c % 4, :], yl[:, c % 4, :]),
                                                 c == first, c == first + k - 1)
                        last.then_inc(acc_full, 1)
                pe.wait_ge(merged_ready, L * KC + KC)
                for n in range(KC):
                    project(f"wo{n}", hs)
                sum_squares("ss2", L * 8 + (Q2 + 4))
                for n in range(F2):
                    project(f"gt{n}", hs, H2 + KC if n == 0 else None)
                    project(f"up{n}", hs)
                down(F2, a2_ready, 0)

        def psum_of(tn, name):
            return acc[tn.bank(name)]

        @block.scalar
        def _(act):
            act.dma_start(v1all[:], vec1).then_inc(inputs_in, 16)
            act.dma_start(onc[:], once).then_inc(inputs_in, 16)
            act.dma_start(nv[:].bitcast(I32), pos).then_inc(inputs_in, 16)
            act.wait_ge(x_in, 16)
            for i in range(4):
                act.activation(sq_h[:, 2 * i:2 * i + 2, :], x[:, 2 * i:2 * i + 2, :], ACT.Square).then_inc(sq_ready, 1)
            act.wait_ge(inputs_in, 16 * 5)
            act.wait_ge(trig_arg, 2)
            for j in range(2):
                act.activation(trig[:, j, :, :], trig[:, j, :, :], ACT.Sin).then_inc(trig_ready, 1)
            act.activation(ada_t, cb2, ACT.Tanh, scale=0.5).then_inc(ctanh, 1)

            own = [0]

            def link(ins):
                own[0] += 1
                ins.then_inc(act_step, 1)
                act.wait_ge(act_step, own[0])

            def end_layer():
                act.sem_clear(act_step)
                own[0] = 0

            def full(tn, name, L):
                act.wait_ge(acc_full, tn.full(name, L))
                return psum_of(tn, name)

            def take(tn, name, L, dst, rows=slice(0, P), n=S, func=ACT.Copy, **kw):
                a = full(tn, name, L)
                act.activation(dst, a[rows, 0:n], func, **kw).then_inc(acc_drained[tn.bank(name)], 1)

            def square_pair(i, sq):
                act.activation(sq[:, 2 * i:2 * i + 2, :], x[:, 2 * i:2 * i + 2, :], ACT.Square).then_inc(sq_ready, 1)

            def round_h(count):
                for c in range(KC):
                    act.wait_ge(h_pre, count + (c + 1))
                    act.activation(hH[:, c, :], tmp4[c % 4], ACT.Copy).then_inc(hh_ready, 1)

            def out_and_norm(first_unit, x_count, tn, L):
                for n in range(KC):
                    feed(first_unit + n + 1 + SPLIT)
                    if n % 2 == 1:
                        act.wait_ge(x_ready, x_count + (n + 1))
                        square_pair(n // 2, sq_in)
                estimate(tn, "ss2", L, 0)

            fed = {}

            def feed_layer(tn, tiles, units, lo_base, visits, L):
                fed.update(tn=tn, tiles=tiles, units=units, visits=visits, L=L, next=0)

            def feed(count):
                tn, L = fed["tn"], fed["L"]
                for u in range(fed["next"], min(count, len(fed["units"]))):
                    t, half, _ = fed["units"][u]
                    slot = t % RING
                    if half == 0:
                        n = len([v for v in range(len(fed["tiles"])) if v % RING == slot])
                        act.wait_ge(got[slot], L * (16 * n) + 16 * (fed["visits"][slot] + t // RING + 1))
                    if u >= SPLIT:
                        act.wait_ge(acc_full, tn.full(fed["units"][u - SPLIT][2], L))
                    act.activation(wH[:, u % SPLIT, :], ring[:, slot, half * UNIT:(half + 1) * UNIT], ACT.Copy)\
                        .then_inc(hi_ready, 1)
                    fed["next"] = u + 1

            def estimate(tn, name, L, i):
                act.wait_ge(acc_drained[tn.bank(name)], tn.drained(name, L))
                link(act.activation(ny[:, i, :], nv[:, i, :], ACT.Ln))
                act.activation(ny[:, i, :], ny[:, i, :], ACT.Exp, scale=-0.5).then_inc(y_ready, 1)

            def down_squares(steps, x_count):
                release = {name: u for u, (_, _, name) in enumerate(fed["units"]) if name.startswith("dn")}
                for name in steps:
                    if "." not in name and int(name[2:]) % 2 == 1:
                        n = int(name[2:])
                        act.wait_ge(x_ready, x_count + (n + 1))
                        square_pair(n // 2, sq_h)
                    if name in release:
                        feed(release[name] + 1 + SPLIT)

            def attention(n, base, L, extra):
                for i in range(n + 1):
                    if i < n:
                        act.wait_ge(nmax_ready, L * n + (base + i + 1))
                        act.activation(pr[:, i % 2, 0:P], sm[:, i % 2, 0:P], ACT.Exp,
                                       bias=nmax[:, i, 0:1], accum_out=psumv[:, i, 0:1])
                        act.activation(pr[:, i % 2, P:3 * P], sm[:, i % 2, P:3 * P], ACT.Exp,
                                       bias=nmax[:, i, 1:2], accum_out=psumv[:, i, 1:2]).then_inc(p_ready, 1)
                    if i >= 1:
                        act.wait_ge(pt_full, L * n + (base + i))
                        act.activation(prT[:, (i - 1) % 2, :], ps_t[:, 0:3 * P], ACT.Copy).then_inc(pt_copied, 1)
                    extra(i)

            with act.Fori(0, LAYERS) as L:
                act.wait_ge(vec_ready, L + 1)
                feed_layer(A1, TILES1, SU1, 0, [0] * RING, L)
                feed(2)
                estimate(A1, "ss1", L, 0)
                round_h(L * (2 * KC))
                feed(SPLIT)
                for i, u in enumerate(UNITS1):
                    take(A1, u, L, raw[:, i, :])
                    if u in ("cq0", "cq1", "ckv"):
                        k = ("cq0", "cq1", "ckv").index(u)
                        act.wait_ge(acc_drained[A1.bank(u)], A1.drained(u, L))
                        act.activation(latsq3[:, k, :], raw[:, i, :], ACT.Square).then_inc(latsq, 1)
                    feed(i + 1 + SPLIT)
                estimate(A1, "ssq", L, 0)
                estimate(A1, "ssk", L, 1)
                for j in range(4):
                    for t in range(TT):
                        take(A1, f"tm{j}{t}", L, tokm[:, t, 256 * j:256 * j + TM_W[j]], n=TM_W[j])
                    feed(min(16 + 2 * (j + 1) + SPLIT, 24))
                act.wait_ge(acc_drained[A1.bank("tm11")], A1.drained("tm11", L))
                act.activation(gate, tokm[:, :, GT:GT + 18], ACT.Exp, scale=-1.0).then_inc(gexp, 1)
                for j, kind in enumerate(("k", "v")):
                    a = full(A1, "hid" + kind, L)
                    act.activation(gel[:, 0, 30 * j:30 * j + 30], a[:, 0:30], ACT.Copy)\
                        .then_inc(acc_drained[A1.bank("hid" + kind)], 1)
                for hh in range(MLA_HEADS):
                    take(A1, f"mq{hh}", L, qm[0:96, hh, :], rows=slice(0, 96))
                for hh in range(MLA_HEADS):
                    take(A1, f"mk{hh}", L, km[0:64, hh, :], rows=slice(0, 64))
                for t in range(TT):
                    take(A1, f"mv{t}", L, vm[:, t, :], n=320)
                act.wait_ge(ge, L * 2 + 1)
                act.activation(gel[:, 1, 0:60], gel[:, 1, 0:60], ACT.Exp, scale=-2.0 * GELU_C).then_inc(ge, 1)
                act.wait_ge(csub, L + 1)
                act.activation(pc[:], pc[:], ACT.Exp).then_inc(cexp, 1)
                take(A1, "ct", L, pcT[0:96, :], rows=slice(0, 96))
                for t in range(TT):
                    take(A1, f"co{t}", L, mixed[:, t, 0:384], n=384)
                for hh in range(RET_HEADS):
                    a = full(A1, f"ro{hh}", L)
                    act.activation(ro_(hh), a[:, 0:2 * HD].rearrange("p (t d) -> p t d", t=TT), ACT.Copy)\
                        .then_inc(acc_drained[A1.bank(f"ro{hh}")], 1)
                act.activation(rgx_(), tokm[:, :, RG:RG + 320], ACT.Exp, scale=-1.0).then_inc(gexp, 1)
                act.wait_ge(gn_v, L + 1)
                link(act.activation(gnst[:, 3, :], gnst[:, 2, :], ACT.Ln))
                act.activation(gnst[:, 3, :], gnst[:, 3, :], ACT.Exp, scale=-0.5).then_inc(gn_y, 1)

                def ada(i):
                    for j in ada_at(i - 1) if i >= 1 else ():
                        act.wait_ge(ada_pool, L * N_ADA + (j + 1))
                        act.activation(ada_p[j % 2], ada_p[j % 2], ACT.Copy, accum_out=adac[:, 2 * j + 1:2 * j + 2])\
                            .then_inc(ada_act, 1)

                attention(NH1, 0, L, ada)
                ada(NH1 + 1)
                feed(24 + SPLIT)
                ada(NH1 + 2)
                for c in range(KC):
                    a = full(A1, f"mt{c}", L)
                    act.activation(hH[:, c, :], a[:, 0:S], ACT.Copy).then_inc(tH_ready, 1)
                out_and_norm(24, L * (2 * KC), A1, L)
                round_h(L * (2 * KC) + KC)
                for n in range(F1):
                    a = full(A1, f"up{n}", L)
                    if n >= 4:
                        act.wait_ge(a_ready, L * F1 + (n - 3))
                    act.activation(r4[n % 4], a[:, 0:S], ACT.Relu).then_inc(acc_drained[A1.bank(f"up{n}")], 1)
                    act.wait_ge(acc_drained[A1.bank(f"up{n}")], A1.drained(f"up{n}", L))
                    act.activation(aH[:, n, :], r4[n % 4], ACT.Square).then_inc(aH_ready, 1)
                    feed(32 + n + 1 + SPLIT)
                down_squares(down_steps(F1), L * (2 * KC) + KC)
                end_layer()
            estimate(AF, "ssf", 0, 0)
            for i in range(4):
                act.wait_ge(x_ready, LAYERS * 2 * KC + 2 * i + 2)
                square_pair(i, sq_h)
            end_layer()
            with act.Fori(0, LAYERS) as L:
                act.wait_ge(vec_ready, L + (LAYERS + 1))
                feed_layer(A2, TILES2, SU2, LO2, VISITS2, L)
                feed(2)
                estimate(A2, "ss1", L, 0)
                round_h(L * (2 * KC) + H2)
                feed(SPLIT)
                for b in range(len(UNITS2) + 1):
                    if b < 8:
                        u = UNITS2[b]
                        take(A2, u, L, raw[:, b, :])
                        act.wait_ge(acc_drained[A2.bank(u)], A2.drained(u, L))
                        act.activation(sq2[:, b, :], raw[:, b, :], ACT.Square).then_inc(raw2_sq, 1)
                        feed(b + 1 + SPLIT)
                    if b >= 1:
                        estimate(A2, "ss_" + UNITS2[b - 1], L, (b - 1) % 2)
                for j in range(2):
                    for t in range(TT):
                        take(A2, f"v{j}{t}", L, vv[:, t, 256 * j:256 * j + 256])
                    feed(8 + 2 * (j + 1) + SPLIT)
                act.wait_ge(pad_ready, L + 1)
                for i, u in enumerate(LATER2):
                    if u[:2] != "cc":
                        dst = up_[:, i, 16:16 + S] if i < 2 else (cu if i < 4 else cb)[:, i % 2, :]
                        take(A2, u, L, dst)
                    feed(12 + i + 1 + SPLIT)
                for b in range(2):
                    a = full(A2, f"pw{b}", L)
                    act.activation(y1H[:, b, :], a[:, 0:S], ACT.Identity, scale=V2("pscale", b)).then_inc(ypH_ready, 1)
                for b in range(2):
                    act.wait_ge(ycf_ready, L * 2 + (b + 1))
                    act.activation(y1H[:, 2 + b, :], yc[:, b, :], ACT.Copy).then_inc(ycH_ready, 1)

                def gates(i):
                    for n in gates_at(i):
                        take(A2, f"g{n}", L, big[:, n, :], func=ACT.Tanh, scale=0.5)
                        feed(20 + n + 1 + SPLIT)

                attention(NH2, LAYERS * NH1, L, gates)
                gates(NH2 + 1)
                for c in range(4):
                    a = full(A2, f"yt{c}", L)
                    act.activation(y2H[:, c, :], a[:, 0:S], ACT.Copy).then_inc(tH_ready, 1)
                for n in range(KC):
                    feed(44 + n + 1 + SPLIT)
                    act.wait_ge(mg_ready, L * KC + (n + 1))
                    act.activation(hH[:, n, :], merged[:, n % 4, :], ACT.Copy).then_inc(mgH_ready, 1)
                out_and_norm(52, L * (2 * KC) + X2, A2, L)
                round_h(L * (2 * KC) + (H2 + KC))
                for n in range(F2):
                    a = full(A2, f"gt{n}", L)
                    if n >= 4:
                        act.wait_ge(a2_ready, L * F2 + (n - 3))
                    act.activation(r4[n % 4], a[:, 0:S], ACT.Tanh, scale=0.5).then_inc(tanh_ready, 1)
                    feed(60 + 2 * n + 1 + SPLIT)
                    act.wait_ge(aT_ready, L * F2 + (n + 1))
                    act.activation(aH[:, n, :], pair2[n % 2], ACT.Copy).then_inc(a2H_ready, 1)
                    feed(60 + 2 * n + 2 + SPLIT)
                down_squares(down_steps(F2), L * (2 * KC) + (X2 + KC))
                end_layer()

        @block.vector
        def _(dve):
            own = [0]

            def link(ins):
                own[0] += 1
                ins.then_inc(dve_step, 1)
                dve.wait_ge(dve_step, own[0])

            def end_layer():
                dve.sem_clear(dve_step)
                own[0] = 0

            turn_of_rope = [0]
            TTN, TSC, STT = nc.vector.tensor_tensor, nc.vector.tensor_scalar, nc.vector.scalar_tensor_tensor

            dve.wait_ge(inputs_in, 16 * 5)
            posf, ang, k, r = big[:, 0:2, :], big[:, 2:6, :], big[:, 6:10, :], big[:, 10:14, :]
            link(nc.vector.tensor_copy(posf, nv[:].bitcast(I32)))
            iat = CONSTS["inv"][0]
            for j in range(4):
                last = TSC(ang[:, j, :], posf[:, j // 3, :], cst[:, iat + j:iat + j + 1], None, ALU.mult)
                link(last)
            magic = 12582912.0
            turn = 2.0 * np.pi
            c1 = 6.28125
            c2 = float(np.float32(turn - c1))
            c3 = float(np.float32(turn - c1 - np.float64(np.float32(turn - c1))))
            link(TSC(k, ang, float(1.0 / turn), None, ALU.mult))
            link(TSC(k, k, magic, None, ALU.add))
            link(TSC(k, k, magic, None, ALU.subtract))
            link(STT(r, k, -c1, ang, ALU.mult, ALU.add))
            link(STT(r, k, -c2, r, ALU.mult, ALU.add))
            link(STT(r, k, -c3, r, ALU.mult, ALU.add))
            lim = 3.1415925
            TSC(trig[:, 1, :, :], r, lim, -lim, ALU.min, ALU.max).then_inc(trig_arg, 1)
            link(STT(k, r, -1.0, r, ALU.mult, ALU.max))
            TSC(trig[:, 0, :, :], k, -1.0, float(np.pi / 2), ALU.mult, ALU.add).then_inc(trig_arg, 1)
            dve.wait_ge(ctanh, 1)
            link(STT(cb2, ada_t, 1.0, cb2, ALU.add, ALU.mult))
            dve.wait_ge(trig_ready, 2)
            end_layer()

            def full(tn, name, L):
                dve.wait_ge(acc_full, tn.full(name, L))
                return psum_of(tn, name)

            fed = {}

            def feed_layer(units, lo_base, L):
                fed.update(units=units, lo_base=lo_base, L=L, next=0)

            def feed(count):
                for u in range(fed["next"], min(count, len(fed["units"]))):
                    t, half, _ = fed["units"][u]
                    dve.wait_ge(hi_ready, fed["L"] * len(fed["units"]) + (fed["lo_base"] + u + 1))
                    TTN(wL[:, u % SPLIT, :], ring[:, t % RING, half * UNIT:(half + 1) * UNIT],
                        wH[:, u % SPLIT, :].bitcast(F32), ALU.subtract).then_inc(lo_ready, 1)
                    fed["next"] = u + 1

            def rest_of(dst, src, hi):
                return TTN(dst, src, hi.bitcast(F32), ALU.subtract)

            def norm_out(gain, shift, count):
                for c in range(KC + 1):
                    if c < KC:
                        last = STT(tmp4[c % 4], x[:, c, :], gain(c), rstd[:], ALU.mult, ALU.mult)
                        if shift is not None:
                            link(last)
                            last = TSC(tmp4[c % 4], tmp4[c % 4], shift(c), None, ALU.add)
                        last.then_inc(h_pre, 1)
                    if c >= 1:
                        dve.wait_ge(hh_ready, count + c)
                        rest_of(hL[:, c - 1, :], tmp4[(c - 1) % 4], hH[:, c - 1, :]).then_inc(h_ready, 1)

            def last_product(steps, units, turns, L, evac):
                release = {name: u for u, (_, _, name) in enumerate(units) if name.startswith("dn")}
                for name in steps:
                    if "." not in name:
                        evac(int(name[2:]))
                    if name in release:
                        feed(release[name] + 1 + SPLIT)

            def mean_square(tn, name, L, i, n):
                a = full(tn, name, L)
                TSC(nv[:, i, :], a[:, 0:S], 1.0 / n, EPS, ALU.mult, ALU.add).then_inc(acc_drained[tn.bank(name)], 1)

            def refine(i, count, v=None, y=None, t=None, dst=None):
                v = nv[:, i, :] if v is None else v
                y = ny[:, i, :] if y is None else y
                t = nt[:, :] if t is None else t
                dst = rstd[:, :] if dst is None else dst
                link(TTN(t, y, y, ALU.mult))
                link(STT(t, v, -0.5, t, ALU.mult, ALU.mult))
                link(STT(dst, t, 1.5, y, ALU.add, ALU.mult))

            def rope(tn, name, L, src, tab, outs, signal, rows=slice(0, P)):
                turn_of_rope[0] ^= 1
                tc, ts = tcs[:, turn_of_rope[0], :], tss[:, turn_of_rope[0], :]
                TTN(tc[rows, :], src, trig[rows, 0, tab, :], ALU.mult)
                a = full(tn, "rot_" + name, L)
                TTN(ts[rows, :], a[rows, 0:S], trig[rows, 1, tab, :], ALU.mult)\
                    .then_inc(acc_drained[tn.bank("rot_" + name)], 1)
                dve.wait_ge(acc_drained[tn.bank("rot_" + name)], tn.drained("rot_" + name, L))
                for dst, part in outs:
                    last = TTN(dst, tc[part, :], ts[part, :], ALU.add)
                last.then_inc(signal, 1)

            def scores(i, n, base, L, scale):
                if i >= 2:
                    dve.wait_ge(p_ready, L * n + (base + i - 1))
                dve.wait_ge(s_full, L * n + (base + i + 1))
                STT(sm[:, i % 2, :], ps_s[i % 2][:, 0:384], scale, C("mask"), ALU.mult, ALU.add).then_inc(s_drained, 1)
                dve.wait_ge(s_drained, L * n + (base + i + 3))
                nc.vector.tensor_reduce(nmax[:, i, 0:1], sm[:, i % 2, 0:P], AX.X, ALU.max, negate=True)
                nc.vector.tensor_reduce(nmax[:, i, 1:2], sm[:, i % 2, P:3 * P], AX.X, ALU.max, negate=True)\
                    .then_inc(nmax_ready, 1)

            with dve.Fori(0, LAYERS) as L:
                own[0] = 0
                nc.vector.tensor_copy(v1[:], v1all[:, L, :]).then_inc(vec_ready, 1)
                dve.wait_ge(vec_ready, L + 1)
                feed_layer(SU1, 0, L)
                mean_square(A1, "ss1", L, 0, D)
                feed(2)
                dve.wait_ge(y_ready, L * Y1 + 1)
                refine(0, None)
                norm_out(lambda c: V1("ln1", c), None, L * (2 * KC))
                feed(SPLIT)

                def rope1_block(u):
                    i = UNITS1.index(u)
                    dve.wait_ge(acc_drained[A1.bank(u)], A1.drained(u, L))
                    allr = slice(0, P)
                    if u == "kpe":
                        rope(A1, u, L, raw[64:96, i, :], 1, [(km[64:96, 0, :], slice(64, 96))], rope_ready, slice(64, 96))
                        dve.wait_ge(rope_ready, L * 17 + 7)
                        nc.vector.tensor_copy(km[64:96, 1:5, :], km[64:96, 0:1, :].to_broadcast([32, 4, S]))\
                            .then_inc(km_ready, 1)
                    elif u == "kc":
                        rope(A1, u, L, raw[:, i, :], 0, [(nt[:, :], allr)], rope_ready)
                        dve.wait_ge(rope_ready, L * 17 + 6)
                        shifted(nt[:, :], 0)
                    elif u == "r4":
                        rope(A1, u, L, raw[:, i, :], 2, [(rope1[0:64, 9, :], slice(0, 64)), (rope1[0:64, 10, :], slice(64, 128))],
                             rope_ready)
                    else:
                        rope(A1, u, L, raw[:, i, :], 2 if u[0] == "r" else 0, [(rope1[:, ROPE1[u], :], allr)], rope_ready)

                def shifted(src, j):
                    cp = nc.vector.tensor_copy
                    cp(xk[j][0:64, 0, :], src[0:64, :])
                    cp(xk[j][64:128, 1, 0:S - 1], src[64:128, 1:S])
                    cp(xk[j][64:128, 0, 0:S - 1], src[0:64, 1:S])
                    link(cp(xk[j][0:64, 1, :], src[64:128, :]))
                    for g in range(2):
                        part = fk[j][:, :, g, :]
                        a0 = xk[j][:, g, 0:240].rearrange("p (n m two) -> p m two n", m=8, two=2)[:, :, 0, :]
                        a1 = xk[j][:, g, 16:256].rearrange("p (n m two) -> p m two n", m=8, two=2)[:, :, 0, :]
                        pos_ = V1("posk" if j == 0 else "posv")
                        TTN(part[:, 0:8, :], a0, pos_[:, 0:8].unsqueeze(2).to_broadcast([P, 8, N_CMP]), ALU.add)
                        last = TTN(part[:, 8:16, :], a1, pos_[:, 8:16].unsqueeze(2).to_broadcast([P, 8, N_CMP]), ALU.add)
                    last.then_inc(f_ready, 1)

                for i, u in enumerate(UNITS1):
                    if i >= 1 and UNITS1[i - 1] in ROPED1:
                        rope1_block(UNITS1[i - 1])
                    if u == "vc":
                        dve.wait_ge(acc_drained[A1.bank(u)], A1.drained(u, L))
                        vraw = raw[:, i, :]
                    feed(i + 1 + SPLIT)
                mean_square(A1, "ssq", L, 0, 256)
                mean_square(A1, "ssk", L, 1, 128)
                dve.wait_ge(y_ready, L * Y1 + 2)
                refine(0, None)
                for c in range(2):
                    STT(cqn[:, c, :], raw[:, 7 + c, :], V1("qn", c), rstd[:], ALU.mult, ALU.mult).then_inc(lat_ready, 1)
                dve.wait_ge(y_ready, L * Y1 + 3)
                refine(1, None)
                STT(cqn[:, 2, :], raw[:, 9, :], V1("kvn", 0), rstd[:], ALU.mult, ALU.mult).then_inc(lat_ready, 1)
                rope1_block("r4")
                shifted(vraw, 1)
                for j in range(4):
                    feed(min(16 + 2 * (j + 1) + SPLIT, 24))
                for kind in ("k", "v"):
                    dve.wait_ge(acc_drained[A1.bank("hid" + kind)], A1.drained("hid" + kind, L))
                gx, gu, gd = gel[:, 0, 0:60], gel[:, 1, 0:60], gel[:, 2, 0:60]
                link(TTN(gu, gx, gx, ALU.mult))
                link(TSC(gu, gu, 0.044715, 1.0, ALU.mult, ALU.add))
                TTN(gu, gu, gx, ALU.mult).then_inc(ge, 1)
                for hh in range(MLA_HEADS):
                    dve.wait_ge(acc_drained[A1.bank(f"mq{hh}")], A1.drained(f"mq{hh}", L))
                    rope(A1, f"mq{hh}", L, qm[64:96, hh, :], 1, [(qm[64:96, hh, :], slice(64, 96))], rope_ready, slice(64, 96))
                dve.wait_ge(ge, L * 2 + 2)
                link(TSC(gd, gu, 1.0, None, ALU.add))
                link(nc.vector.reciprocal(gu, gd))
                link(nc.vector.memset(hid[:, :, :], 0.0))
                TTN(hid[:, 0, :].rearrange("p (g n) -> p g n", g=2)[:, :, 0:N_CMP],
                    gel[:, 0, 0:30].rearrange("p (g n) -> p g n", g=2), gel[:, 1, 0:30].rearrange("p (g n) -> p g n", g=2),
                    ALU.mult)
                TTN(hid[:, 1, :].rearrange("p (g n) -> p g n", g=2)[:, :, 0:N_CMP],
                    gel[:, 0, 30:60].rearrange("p (g n) -> p g n", g=2), gel[:, 1, 30:60].rearrange("p (g n) -> p g n", g=2),
                    ALU.mult).then_inc(gel_ready, 1)
                dve.wait_ge(gel_ready, L + 1)
                for g in range(2):
                    last = nc.vector.tensor_copy(grep[:, g, :].rearrange("p (h n) -> p h n", h=NSA_HEADS),
                                                 hid[:, 1, 16 * g:16 * g + 16].unsqueeze(1).to_broadcast([P, NSA_HEADS, 16]))
                last.then_inc(grep_ready, 1)
                a = full(A1, "kcc", L)
                nc.vector.tensor_copy(kcT[0:64, :], a[0:64, 0:16]).then_inc(kcT_ready, 1)
                nc.vector.tensor_copy(kcT[64:128, :], a[64:128, 16:32]).then_inc(kcT_ready, 1)
                dve.wait_ge(kcT_ready, L * 2 + 2)
                dve.sem_inc(acc_drained[A1.bank("kcc")], 1)
                a = full(A1, "vbd", L)
                TTN(vbd[0:96, :].rearrange("p (h d) -> p h d", h=NSA_HEADS), a[0:96, 0:384].rearrange("p (h d) -> p h d", h=NSA_HEADS),
                    C("bmask", 96).unsqueeze(2).to_broadcast([96, NSA_HEADS, HD]), ALU.mult).then_inc(vbd_ready, 1)
                dve.wait_ge(vbd_ready, L + 1)
                dve.sem_inc(acc_drained[A1.bank("vbd")], 1)
                dve.wait_ge(gexp, L * 2 + 1)
                link(TSC(gate, gate, 1.0, None, ALU.add))
                nc.vector.reciprocal(gate, gate).then_inc(gate_ready, 1)
                dve.wait_ge(gate_ready, L + 1)
                split = lambda v: v.rearrange("p (t g n) -> p g t n", t=TT, g=2)
                for g in range(2):
                    a = full(A1, f"cs{g}", L)
                    STT(split(pc)[:, g, :, :], a[:, 0:96].rearrange("p (t n) -> p t n", t=TT), HD ** -0.5,
                        split(C("cmask"))[:, g, :, :], ALU.mult, ALU.add).then_inc(acc_drained[A1.bank(f"cs{g}")], 1)
                    dve.wait_ge(acc_drained[A1.bank(f"cs{g}")], A1.drained(f"cs{g}", L))
                pc3 = pc.rearrange("p (h n) -> p h n", n=NP16)
                bc = lambda v: v.unsqueeze(2).to_broadcast([P, 12, NP16])
                link(nc.vector.tensor_reduce(cst12[:, 0, :], pc3, AX.X, ALU.max))
                TTN(pc3, pc3, bc(cst12[:, 0, :]), ALU.subtract).then_inc(csub, 1)
                dve.wait_ge(cexp, L + 1)
                link(TTN(pc[:], pc[:], C("ckeep"), ALU.mult))
                link(nc.vector.tensor_reduce(cst12[:, 1, :], pc3, AX.X, ALU.add))
                link(TSC(cst12[:, 1, :], cst12[:, 1, :], 1e-30, None, ALU.max))
                link(nc.vector.reciprocal(cst12[:, 2, :], cst12[:, 1, :]))
                g4 = gate.rearrange("p t (h b) -> p t h b", b=N_BRANCH)
                link(TTN(cst12[:, 2, :].rearrange("p (t h) -> p t h", t=TT), cst12[:, 2, :].rearrange("p (t h) -> p t h", t=TT),
                         g4[:, :, :, 0], ALU.mult))
                TTN(pc3, pc3, bc(cst12[:, 2, :]), ALU.mult).then_inc(pc_ready, 1)
                for hh in range(RET_HEADS):
                    a = full(A1, f"rs{hh}", L)
                    w = sm[:, hh % 2, :]
                    if hh >= 2:
                        dve.wait_ge(acc_full, A1.full(f"ro{hh - 2}", L))
                    TTN(w[:, 0:S], a[:, 0:S], decay[:, hh, :], ALU.mult)
                    TTN(w[:, S:S + P], a[:, S:S + P], decay[:, hh, 0:P], ALU.mult).then_inc(rw_ready, 1)
                    dve.wait_ge(rw_ready, L * RET_HEADS + (hh + 1))
                    dve.sem_inc(acc_drained[A1.bank(f"rs{hh}")], 1)
                for hh in range(RET_HEADS):
                    dve.wait_ge(acc_drained[A1.bank(f"ro{hh}")], A1.drained(f"ro{hh}", L))
                o10 = ro_all(0).rearrange("p (h d) -> p h d", d=HD)
                s10 = ro_all(2).rearrange("p (h d) -> p h d", d=HD)
                bg = lambda v: v.unsqueeze(2).to_broadcast([P, 10, HD])
                link(nc.vector.tensor_reduce(gnst[:, 0, :], o10, AX.X, ALU.add))
                link(TSC(gnst[:, 1, :], gnst[:, 0, :], 1.0 / HD, None, ALU.mult))
                link(TTN(o10, o10, bg(gnst[:, 1, :]), ALU.subtract))
                link(TTN(s10, o10, o10, ALU.mult))
                link(nc.vector.tensor_reduce(gnst[:, 4, :], s10, AX.X, ALU.add))
                TSC(gnst[:, 2, :], gnst[:, 4, :], 1.0 / HD, EPS, ALU.mult, ALU.add).then_inc(gn_v, 1)
                dve.wait_ge(gexp, L * 2 + 2)
                gx_ = rgx_()
                link(TSC(gx_, gx_, 1.0, None, ALU.add))
                link(nc.vector.reciprocal(gx_, gx_))
                link(TTN(gx_, gx_, tokm[:, :, RG:RG + 320], ALU.mult))
                link(TTN(gx_, gx_, V1("gn").unsqueeze(1).to_broadcast([P, TT, 320]), ALU.mult))
                dve.wait_ge(gn_y, L + 1)
                refine(0, None, gnst[:, 2, :], gnst[:, 3, :], gnst[:, 4, :], gnst[:, 5, :])
                link(TTN(o10, o10, bg(gnst[:, 5, :]), ALU.mult))
                link(TTN(mixed[:, :, 704:1024], ro_all(0).rearrange("p (t f) -> p t f", t=TT), gx_, ALU.mult))
                for t in range(TT):
                    dve.wait_ge(acc_drained[A1.bank(f"co{t}")], A1.drained(f"co{t}", L))

                def output(i):
                    kind, hh = HEADS1[i]
                    dve.wait_ge(p_ready, L * NH1 + (i + 1))
                    link(nc.vector.reciprocal(coef[:, i, :], psumv[:, i, :]))
                    if kind != "mla":
                        b = 3 * hh + (1 if kind == "slc" else 2)
                        link(TTN(coef[:, i, :].unsqueeze(2), coef[:, i, :].unsqueeze(2), gate[:, :, b:b + 1], ALU.mult))
                    dve.wait_ge(o_full, L * NH1 + (i + 1))
                    for t in range(TT):
                        o = ps_o[:, 64 * t:64 * t + 64]
                        if kind == "mla":
                            m = mixed[:, t, 384 + 64 * hh:448 + 64 * hh]
                            last = TSC(m, o, coef[:, i, t:t + 1], None, ALU.mult)
                        else:
                            m = mixed[:, t, 64 * hh:64 * hh + 64]
                            last = STT(m, o, coef[:, i, t:t + 1], m, ALU.mult, ALU.add)
                    last.then_inc(o_drained, 1)

                def ada(j):
                    t = TILES1.index(("ada", j))
                    n = len([u for u in range(T1) if u % RING == t % RING])
                    dve.wait_ge(got[t % RING], L * (16 * n) + 16 * (t // RING + 1))
                    if j >= 1:
                        dve.wait_ge(ada_dve, L * N_ADA + j)
                    STT(ada_v, ring[:, t % RING, 0:UNIT], 1.0, cb2, ALU.mult, ALU.mult, accum_out=adac[:, 2 * j:2 * j + 1])\
                        .then_inc(ada_dve, 1)

                for i in range(NH1 + 2):
                    if i < NH1:
                        scores(i, NH1, 0, L, scale1(i))
                    if i >= 2:
                        output(i - 2)
                    for j in ada_at(i):
                        ada(j)
                dve.wait_ge(ada_act, L * N_ADA + N_ADA)
                dve.wait_ge(ada_dve, L * N_ADA + N_ADA)
                nc.vector.tensor_copy(modall[:, L, :], adac[:])
                feed(24 + SPLIT)
                dve.wait_ge(o_drained, L * NH1 + (NH1 + 1))
                dve.sem_inc(mixed_ready, 1)
                for c in range(KC):
                    dve.wait_ge(tH_ready, L * KC + (c + 1))
                    rest_of(hL[:, c, :], psum_of(A1, f"mt{c}")[:, 0:S], hH[:, c, :])\
                        .then_inc(acc_drained[A1.bank(f"mt{c}")], 1)
                for n in range(KC):
                    a = full(A1, f"wo{n}", L)
                    TTN(x[:, n, :], a[:, 0:S], x[:, n, :], ALU.add).then_inc(x_ready, 1)
                    dve.wait_ge(x_ready, L * (2 * KC) + (n + 1))
                    dve.sem_inc(acc_drained[A1.bank(f"wo{n}")], 1)
                    feed(24 + n + 1 + SPLIT)
                mean_square(A1, "ss2", L, 0, D)
                dve.wait_ge(y_ready, L * Y1 + 4)
                refine(0, None)
                norm_out(lambda c: V1("ln2", c), None, L * (2 * KC) + KC)
                for n in range(F1):
                    dve.wait_ge(acc_drained[A1.bank(f"up{n}")], A1.drained(f"up{n}", L))
                    link(TTN(tmp4[n % 4], r4[n % 4], r4[n % 4], ALU.mult))
                    dve.wait_ge(aH_ready, L * F1 + (n + 1))
                    rest_of(aL[:, n, :], tmp4[n % 4], aH[:, n, :]).then_inc(a_ready, 1)
                    feed(32 + n + 1 + SPLIT)

                def evac(n):
                    a = full(A1, f"dn{n}", L)
                    TTN(x[:, n, :], a[:, 0:S], x[:, n, :], ALU.add).then_inc(x_ready, 1)
                    dve.wait_ge(x_ready, L * (2 * KC) + (KC + n + 1))
                    dve.sem_inc(acc_drained[A1.bank(f"dn{n}")], 1)

                last_product(down_steps(F1), SU1, A1, L, evac)
                end_layer()

            mean_square(AF, "ssf", 0, 0, D)
            dve.wait_ge(y_ready, YF + 1)
            refine(0, None)
            for c in range(KC):
                STT(x[:, c, :], x[:, c, :], onc[:, c:c + 1], rstd[:], ALU.mult, ALU.mult).then_inc(x_ready, 1)
            dve.wait_ge(x_ready, X2)
            end_layer()

            with dve.Fori(0, LAYERS) as L:
                own[0] = 0
                nc.vector.tensor_copy(v2[:], v2all[:, L, :]).then_inc(vec_ready, 1)
                dve.wait_ge(vec_ready, L + (LAYERS + 1))
                feed_layer(SU2, LO2, L)
                nc.vector.memset(up_[:, :, 0:16], 0.0)
                nc.vector.memset(sw[:, :, 0:16], 0.0)
                nc.vector.memset(cv[:, :, 0:2], 0.0).then_inc(pad_ready, 1)
                link(STT(mod[:], modall[:, L, :], 0.5, V2("bada"), ALU.mult, ALU.add))
                link(STT(mods[:, 0, :], mod[:, 8:16], 1.0, V2("n1"), ALU.add, ALU.mult))
                link(STT(mods[:, 1, :], mod[:, 32:40], 1.0, V2("n2"), ALU.add, ALU.mult))
                link(TSC(mods[:, 2, :], mod[:, 16:24], 0.5, None, ALU.mult))
                mean_square(A2, "ss1", L, 0, D)
                feed(2)
                dve.wait_ge(y_ready, L * Y2N + (Y2 + 1))
                refine(0, None)
                norm_out(lambda c: mods[:, 0, c:c + 1], lambda c: mod[:, c:c + 1], L * (2 * KC) + H2)
                feed(SPLIT)
                for b in range(len(UNITS2) + 3):
                    if 1 <= b < 9:
                        mean_square(A2, "ss_" + UNITS2[b - 1], L, (b - 1) % 2, HD)
                    if 2 <= b < 10:
                        j = b - 2
                        dve.wait_ge(y_ready, L * Y2N + (Y2 + 2 + j))
                        refine(j % 2, None)
                        STT(qk2[:, j, :], raw[:, j, :], V2("qn" if j < 4 else "kn", 0), rstd[:], ALU.mult, ALU.mult)\
                            .then_inc(qn2_ready, 1)
                    if b >= 3:
                        j = b - 3
                        dve.wait_ge(qn2_ready, L * 8 + (j + 1))
                        rope(A2, UNITS2[j], L, qk2[:, j, :], 3, [(qk2[:, j, :], slice(0, P))], qk2_ready)
                    if b < 8:
                        feed(b + 1 + SPLIT)
                for j in range(2):
                    feed(8 + 2 * (j + 1) + SPLIT)
                for i, u in enumerate(LATER2):
                    if u[:2] == "cc":
                        b = i % 2
                        for other in ("cu", "cb"):
                            dve.wait_ge(acc_drained[A2.bank(other + "ab"[b])], A2.drained(other + "ab"[b], L))
                        a = full(A2, u, L)
                        TTN(cv[:, b, 2:2 + S], a[:, 0:S], cu[:, b, :], ALU.mult).then_inc(acc_drained[A2.bank(u)], 1)
                        dve.wait_ge(acc_drained[A2.bank(u)], A2.drained(u, L))
                        link(TSC(tc, cv[:, b, 2:2 + S], V2("conv", 4 + b), None, ALU.mult))
                        link(STT(tc, cv[:, b, 1:1 + S], V2("conv", 2 + b), tc, ALU.mult, ALU.add))
                        link(STT(tc, cv[:, b, 0:S], V2("conv", b), tc, ALU.mult, ALU.add))
                        TTN(yc[:, b, :], tc, cb[:, b, :], ALU.mult).then_inc(ycf_ready, 1)
                    feed(12 + i + 1 + SPLIT)
                for b in range(2):
                    dve.wait_ge(ypH_ready, L * 2 + (b + 1))
                    STT(y1L[:, b, :], psum_of(A2, f"pw{b}")[:, 0:S], V2("pscale", b), y1H[:, b, :].bitcast(F32),
                        ALU.mult, ALU.subtract).then_inc(acc_drained[A2.bank(f"pw{b}")], 1)
                for b in range(2):
                    dve.wait_ge(ycH_ready, L * 2 + (b + 1))
                    rest_of(y1L[:, 2 + b, :], yc[:, b, :], y1H[:, 2 + b, :]).then_inc(yc_ready, 1)

                def output(i):
                    dve.wait_ge(p_ready, L * NH2 + (LAYERS * NH1 + i + 1))
                    link(nc.vector.reciprocal(coef[:, i, :], psumv[:, i, :]))
                    dve.wait_ge(o_full, L * NH2 + (LAYERS * NH1 + i + 1))
                    for t in range(TT):
                        last = TSC(ya[:, t, 64 * i:64 * i + 64], ps_o[:, 64 * t:64 * t + 64], coef[:, i, t:t + 1], None, ALU.mult)
                    last.then_inc(o_drained, 1)

                def gates(i):
                    for n in gates_at(i):
                        feed(20 + n + 1 + SPLIT)

                for i in range(NH2 + 2):
                    if i < NH2:
                        scores(i, NH2, LAYERS * NH1, L, HD ** -0.5)
                    if i >= 1:
                        gates(i - 1)
                    if i >= 2:
                        output(i - 2)
                dve.wait_ge(o_drained, L * NH2 + (LAYERS * NH1 + NH2 + 1))
                dve.sem_inc(ya_ready, 1)
                gates(NH2 + 1)
                for c in range(4):
                    dve.wait_ge(tH_ready, L * 4 + (M2 + c + 1))
                    rest_of(y2L[:, c, :], psum_of(A2, f"yt{c}")[:, 0:S], y2H[:, c, :])\
                        .then_inc(acc_drained[A2.bank(f"yt{c}")], 1)
                for n in range(KC + 1):
                    if n < KC:
                        mg = merged[:, n % 4, :]
                        for m, name in enumerate(MIXERS):
                            a = full(A2, f"{name}{n}", L)
                            dst = tc if m else mg
                            STT(dst, big[:, KC * m + n, :], 1.0, a[:, 0:S], ALU.add, ALU.mult)\
                                .then_inc(acc_drained[A2.bank(f"{name}{n}")], 1)
                            dve.wait_ge(acc_drained[A2.bank(f"{name}{n}")], A2.drained(f"{name}{n}", L))
                            if m == 1:
                                link(TTN(mg, mg, tc, ALU.add))
                            if m == 2:
                                TTN(mg, mg, tc, ALU.add).then_inc(mg_ready, 1)
                        feed(44 + n + 1 + SPLIT)
                    if n >= 1:
                        dve.wait_ge(mgH_ready, L * KC + n)
                        rest_of(hL[:, n - 1, :], merged[:, (n - 1) % 4, :], hH[:, n - 1, :]).then_inc(merged_ready, 1)
                for n in range(KC):
                    a = full(A2, f"wo{n}", L)
                    STT(x[:, n, :], a[:, 0:S], mods[:, 2, n:n + 1], x[:, n, :], ALU.mult, ALU.add).then_inc(x_ready, 1)
                    dve.wait_ge(x_ready, L * (2 * KC) + (X2 + n + 1))
                    dve.sem_inc(acc_drained[A2.bank(f"wo{n}")], 1)
                    feed(52 + n + 1 + SPLIT)
                mean_square(A2, "ss2", L, 0, D)
                dve.wait_ge(y_ready, L * Y2N + (Y2 + 10))
                refine(0, None)
                norm_out(lambda c: mods[:, 1, c:c + 1], lambda c: mod[:, 24 + c:25 + c], L * (2 * KC) + (H2 + KC))
                for n in range(F2):
                    dve.wait_ge(tanh_ready, L * F2 + (n + 1))
                    g = psum_of(A2, f"gt{n}")
                    STT(tmp4[n % 4], r4[n % 4], 1.0, g[:, 0:S], ALU.add, ALU.mult)\
                        .then_inc(acc_drained[A2.bank(f"gt{n}")], 1)
                    feed(60 + 2 * n + 1 + SPLIT)
                    dve.wait_ge(acc_drained[A2.bank(f"gt{n}")], A2.drained(f"gt{n}", L))
                    u = full(A2, f"up{n}", L)
                    STT(pair2[n % 2], tmp4[n % 4], 0.5, u[:, 0:S], ALU.mult, ALU.mult).then_inc(aT_ready, 1)
                    dve.wait_ge(aT_ready, L * F2 + (n + 1))
                    dve.sem_inc(acc_drained[A2.bank(f"up{n}")], 1)
                    feed(60 + 2 * n + 2 + SPLIT)
                    dve.wait_ge(a2H_ready, L * F2 + (n + 1))
                    rest_of(aL[:, n, :], pair2[n % 2], aH[:, n, :]).then_inc(a2_ready, 1)

                def evac(n):
                    a = full(A2, f"dn{n}", L)
                    STT(x[:, n, :], a[:, 0:S], mod[:, 40 + n:41 + n], x[:, n, :], ALU.mult, ALU.add).then_inc(x_ready, 1)
                    dve.wait_ge(x_ready, L * (2 * KC) + (X2 + KC + n + 1))
                    dve.sem_inc(acc_drained[A2.bank(f"dn{n}")], 1)

                last_product(down_steps(F2), SU2, A2, L, evac)
                end_layer()

        @block.gpsimd
        def _(pool):
            own = [0]

            def link(ins):
                own[0] += 1
                ins.then_inc(pool_step, 1)
                pool.wait_ge(pool_step, own[0])

            TTN = nc.gpsimd.tensor_tensor
            with pool.Fori(0, LAYERS) as L:
                pool.wait_ge(nmax_ready, L * NH1 + 1)
                for j in range(N_ADA):
                    if j >= 2:
                        pool.wait_ge(ada_act, L * N_ADA + (j - 1))
                    pool.wait_ge(ada_dve, L * N_ADA + (j + 1))
                    t = TILES1.index(("ada", j))
                    TTN(ada_p[j % 2], ring[:, t % RING, UNIT:2 * UNIT], cb2, ALU.mult).then_inc(ada_pool, 1)

            with pool.Fori(0, LAYERS) as L:
                own[0] = 0
                pool.wait_ge(pad_ready, L + 1)
                w0 = 16
                for b, u in enumerate(("pa", "pb")):
                    pool.wait_ge(acc_drained[A2.bank(u)], A2.drained(u, L))
                    for j in range(2 if b == 0 else 4):
                        src, dst = (up_[:, b, :] if j == 0 else sw[:, (j - 1) % 2 * 2 + 1, :]), sw[:, j % 2 * 2 + 1, :]
                        link(TTN(dst[:, w0:w0 + S], src[:, w0:w0 + S], src[:, w0 - 2 ** j:w0 - 2 ** j + S], ALU.add))
                    lo, hi = sw[:, 1, :], sw[:, 3, :]
                    res = sw[:, 2 * b, w0:w0 + S]
                    TTN(res[0:64, :], lo[0:64, w0:w0 + S], invc[0:64, b, :], ALU.mult)
                    link(TTN(res[64:128, :], hi[64:128, w0:w0 + S], invc[64:128, b, :], ALU.mult))
                    link(TTN(res, res, up_[:, b, w0:w0 + S], ALU.subtract))
                    pool.sem_inc(pooled, 1)
                pool.sem_clear(pool_step)


def _blocks(w):
    k, n = w.shape
    b = np.zeros((P, k // P, P), np.float32)
    b[:, :, :n] = w.reshape(k // P, P, n).transpose(1, 0, 2)
    return b.reshape(P, -1)


def _wide(w):
    b = np.zeros((P, KC, 256), np.float32)
    b[:, :, :w.shape[1]] = w.reshape(KC, P, -1).transpose(1, 0, 2)
    return b.reshape(P, -1)


def _columns(v):
    return v.reshape(-1, P).T


def _stream(i):
    out = np.zeros((LAYERS * (T1 + T2), P, TILE), np.float32)
    for l in range(LAYERS):
        w = i["w_in"][l]
        cols = {}
        for r in range(3):
            cols[f"q{r}"] = np.r_[64 * r:64 * r + 64, 64 * (3 + r):64 * (3 + r) + 64]
        cols.update(kc=np.r_[384:512], vc=np.r_[512:640], ks=np.r_[640:768], kw=np.r_[896:1024],
                    cq0=np.r_[1170:1298], cq1=np.r_[1298:1426], ckv=np.r_[1426:1554], kpe=np.r_[1490:1586],
                    rqa=np.r_[1586:1714], rqb=np.r_[1714:1842], rka=np.r_[1906:2034], rkb=np.r_[2034:2162],
                    r4=np.r_[1842:1906, 2162:2226])
        tm = np.r_[768:896, 1024:1152, 1152:1170, 2226:2546, 2546:2866]
        w1k, w1v = i["cmp_w1_k"][l], i["cmp_w1_v"][l]
        for t, (kind, j) in enumerate(TILES1):
            o = out[l * T1 + t]
            if kind in cols:
                o[:, :1024], o[:, 1024:] = _blocks(w[:, cols[kind]]), _blocks(w[:, cols[j]])
            elif kind == "tm":
                o[:] = _wide(w[:, tm[256 * j:256 * j + 256]])
            elif kind == "cmpk":
                o[:] = w1k.reshape(16, P, P).transpose(1, 0, 2).reshape(P, -1)
            elif kind == "cmpv":
                o[:] = w1v.reshape(16, P, P).transpose(1, 0, 2).reshape(P, -1)
            elif kind == "small":
                o[:, UQ:UQ + 960] = i["mla_w_uq"][l].reshape(2, P, 480).transpose(1, 0, 2).reshape(P, -1)
                o[:, UKV:UKV + 640] = i["mla_w_ukv"][l]
                o[:, W2K:W2K + 128] = np.tile(i["cmp_w2_k"][l], (1, 2))
                o[:, W2V:W2V + 192] = np.tile(i["cmp_w2_v"][l], (1, 3))
            elif kind in ("wout", "up"):
                m = i["w_out" if kind == "wout" else "w_up"][l]
                for b in range(2):
                    o[:, 1024 * b:1024 * b + 1024] = _blocks(m[:, P * (2 * j + b):P * (2 * j + b + 1)])
            elif kind == "ada":
                for b in range(2):
                    o[:, 1024 * b:1024 * b + 1024] = i["w_ada_2"][l][:, P * (2 * j + b):P * (2 * j + b + 1)].T
            else:
                m = i["w_down"][l][2048 * (j % 2):2048 * (j % 2 + 1), P * (j // 2):P * (j // 2 + 1)]
                o[:] = _blocks(m)
        w = i["w_in_2"][l]
        cols = {f"q{b}": np.r_[1024 + P * b:1024 + P * b + P] for b in range(4)}
        cols.update({f"k{b}": np.r_[1536 + P * b:1536 + P * b + P] for b in range(4)})
        for b, u in enumerate(LATER2):
            cols[u] = np.r_[P * b:P * b + P]
        down = i["w_down_2"][l].reshape(F2, P, KC, P).transpose(2, 0, 1, 3).reshape(KC * F2, P, P)
        for t, (kind, j) in enumerate(TILES2):
            o = out[LAYERS * T1 + l * T2 + t]
            if kind in cols:
                o[:, :1024], o[:, 1024:] = _blocks(w[:, cols[kind]]), _blocks(w[:, cols[j]])
            elif kind == "v":
                o[:] = _wide(w[:, 2048 + 256 * j:2048 + 256 * j + 256])
            elif kind in ("wout", "gate"):
                m, at = {"wout": (i["w_out_2"][l], 0), "gate": (w, 2560)}[kind]
                for b in range(2):
                    c = at + P * (2 * j + b)
                    o[:, 1024 * b:1024 * b + 1024] = _blocks(m[:, c:c + P])
            elif kind == "mix":
                m = np.concatenate([i["p_pool_2"][l], i["p_conv_2"][l], i["p_attn_2"][l]], axis=0)
                for b in range(2):
                    o[:, 1024 * b:1024 * b + 1024] = _blocks(m[:, P * (2 * j + b):P * (2 * j + b + 1)])
            elif kind == "gu":
                for b, m in enumerate((i["w_gate_2"][l], i["w_up_2"][l])):
                    o[:, 1024 * b:1024 * b + 1024] = _blocks(m[:, P * j:P * j + P])
            else:
                o[:] = down[16 * j:16 * j + 16].transpose(1, 0, 2).reshape(P, -1)
    return out


def kernel(**inputs):
    import concourse.bacc as _bacc
    from concourse import mybir as _mybir
    from concourse.bass_utils import run_bass_kernel_spmd as _run

    i = {k: np.asarray(v) for k, v in inputs.items()}
    vec1 = np.zeros((P, LAYERS, N_V1), np.float32)
    vec2 = np.zeros((P, LAYERS, N_V2), np.float32)
    for l in range(LAYERS):
        def put(arr, table, name, a):
            at, w = table[name]
            arr[:, l, at:at + w] = a
        put(vec1, VEC1, "ln1", _columns(i["ln1_gain"][l]))
        put(vec1, VEC1, "ln2", _columns(i["ln2_gain"][l]))
        put(vec1, VEC1, "qn", _columns(i["mla_q_norm"][l]))
        put(vec1, VEC1, "kvn", _columns(i["mla_kv_norm"][l]))
        put(vec1, VEC1, "posk", i["cmp_pos_k"][l].reshape(16, P).T)
        put(vec1, VEC1, "posv", i["cmp_pos_v"][l].reshape(16, P).T)
        put(vec1, VEC1, "gn", np.broadcast_to(i["ret_gn_gain"][l].reshape(1, 320), (P, 320)))
        put(vec2, VEC2, "n1", _columns(i["norm1_w_2"][l]))
        put(vec2, VEC2, "n2", _columns(i["norm2_w_2"][l]))
        put(vec2, VEC2, "bada", _columns(i["b_ada_2"][l]))
        put(vec2, VEC2, "pscale", _columns(i["pool_scale_2"][l]))
        put(vec2, VEC2, "conv", i["conv_w_2"][l].reshape(3, 2, P).transpose(2, 0, 1).reshape(P, 6))
        put(vec2, VEC2, "qn", np.tile(i["q_norm_w_2"][l], 2)[:, None])
        put(vec2, VEC2, "kn", np.tile(i["k_norm_w_2"][l], 2)[:, None])
        bd = np.zeros((P, 2, P), np.float32)
        for g in range(4):
            r = 64 * (g % 2)
            bd[r:r + 64, g // 2, r:r + 64] = i["pool_w_2"][l][g]
        put(vec2, VEC2, "poolw", bd.reshape(P, 256))
    once = np.concatenate([_columns(i["final_gain"]), np.broadcast_to(i["c_2"][0][None], (P, D))], axis=1)
    pos = np.stack([i["positions"][0], i["positions_2"][0]])
    arrays = {
        "consts": constants(), "vec1": vec1, "vec2": vec2, "once": np.ascontiguousarray(once),
        "pos": np.ascontiguousarray(np.broadcast_to(pos[None].astype(np.int32), (P, 2, S))),
        "xin": np.ascontiguousarray(i["x"][0].T.reshape(KC, P, S).transpose(1, 0, 2)),
        "stream": _stream(i),
    }
    nc = _bacc.Bacc("TRN2", target_bir_lowering=False, num_devices=1)
    args = [nc.dram_tensor(n, a.shape, _mybir.dt.from_np(a.dtype), kind="ExternalInput").ap() for n, a in arrays.items()]
    out = nc.dram_tensor("out", (P, KC, S), _mybir.dt.float32, kind="ExternalOutput").ap()
    trn_kernel(nc, *args, out)
    r = _run(nc, [arrays], core_ids=[0])
    got = r.results[0]["out"]
    return np.ascontiguousarray(got.transpose(1, 0, 2).reshape(D, S).T)[None]
```

```python
import concourse.bass as bass
from concourse import mybir
from contextlib import ExitStack
import numpy as np

F32 = mybir.dt.float32
I32 = mybir.dt.int32
F32R = mybir.dt.float32r
ALU = mybir.AluOpType
ACT = mybir.ActivationFunctionType
AX = mybir.AxisListType

P = 128
D = 1024
S = 256
TT = S // P
KC = D // P
LAYERS = 2
HD = 64
NSA_HEADS, REP, N_BRANCH = 6, 3, 3
CMP_LEN, CMP_STRIDE = 32, 16
N_CMP = (S - CMP_LEN) // CMP_STRIDE + 1
NP16 = 16
MLA_HEADS, MLA_Q, MLA_PE = 5, 96, 32
RET_HEADS = 5
D_FF1 = 4096
F1 = D_FF1 // P
ATTN_HEADS = 8
D_FF2 = 2816
F2 = D_FF2 // P
GATES = 3 * KC
EPS = 1e-6
NEG = -1e30
GELU_C = 0.7978845608028654

TILE = 2048
RING = 4
UNIT = TILE // 2
SPLIT = 4
assert KC * 256 == TILE

UNITS1 = ["q0", "q1", "q2", "ks", "kw", "kc", "vc", "cq0", "cq1", "ckv", "kpe", "rqa", "rqb", "rka", "rkb", "r4"]
ROPED1 = ["q0", "q1", "q2", "ks", "kw", "kc", "kpe", "rqa", "rqb", "rka", "rkb", "r4"]
UNITS2 = [f"q{b}" for b in range(4)] + [f"k{b}" for b in range(4)]
LATER2 = ["pa", "pb", "cua", "cub", "cba", "cbb", "cca", "ccb"]
MIXERS = ["P", "C", "A"]
VS, VW, GT, RV, RG = 0, 128, 256, 274, 594
TM1 = 914
TM_W = [256, 256, 256, TM1 - 768]

N_ADA, ADA_ATTENTION = 24, 14


def _up_tiles():
    out = []
    for j in range(F1 // 2):
        out.append(("up", j))
        if 3 <= j < 3 + N_ADA - ADA_ATTENTION:
            out.append(("ada", ADA_ATTENTION + j - 3))
    return out


TILES1 = (
    [(UNITS1[2 * i], UNITS1[2 * i + 1]) for i in range(8)]
    + [("tm", j) for j in range(4)]
    + [("cmpk", 0), ("cmpv", 0), ("small", 0)]
    + [("ada", j) for j in range(ADA_ATTENTION)]
    + [("wout", j) for j in range(4)]
    + _up_tiles()
    + [("down", j) for j in range(2 * KC)]
)
TILES2 = (
    [(UNITS2[2 * i], UNITS2[2 * i + 1]) for i in range(4)]
    + [("v", j) for j in range(2)]
    + [(LATER2[2 * i], LATER2[2 * i + 1]) for i in range(4)]
    + [("gate", j) for j in range(GATES // 2)]
    + [("mix", j) for j in range(KC // 2)]
    + [("wout", j) for j in range(4)]
    + [("gu", j) for j in range(F2)]
    + [("down", j) for j in range(KC * F2 // 16)]
)
T1, T2 = len(TILES1), len(TILES2)
WHOLE = ("cmpk", "cmpv", "small", "ada")


def last_user(tiles, t, half):
    kind, j = tiles[t]
    n = 2 * j + half if isinstance(j, int) else None
    if kind in ("tm", "v"):
        return f"{kind}{j}{TT - 1}"
    if kind in ("cmpk", "cmpv"):
        return "hid" + kind[-1]
    if kind == "small":
        return "vbd"
    if kind in ("wout", "up", "gate", "mix"):
        return {"wout": "wo", "up": "up", "gate": "g", "mix": "A"}[kind] + str(n)
    if kind == "gu":
        return ("gt", "up")[half] + str(j)
    if kind == "down":
        k = F1 if tiles is TILES1 else F2
        m = 8 * n + 7
        return f"dn{m // k}" + (f".{m % k}" if m % k != k - 1 else "")
    return (kind, j)[half]


def split_units(tiles):
    return [(t, half, last_user(tiles, t, half)) for t, (kind, _) in enumerate(tiles) if kind not in WHOLE
            for half in range(2)]


SU1, SU2 = split_units(TILES1), split_units(TILES2)
NU1, NU2 = len(SU1), len(SU2)

HEADS1 = [("slc", h) for h in range(NSA_HEADS)] + [("win", h) for h in range(NSA_HEADS)] \
    + [("mla", h) for h in range(MLA_HEADS)]
NH1, NH2 = len(HEADS1), ATTN_HEADS


def down_steps(kf):
    out = []
    for n in range(KC):
        for k in range(kf):
            if (n * kf + k) % 8 == 7 and k < kf - 1:
                out.append(f"dn{n}.{k}")
        out.append(f"dn{n}")
    return out


def ada_at(i):
    first, steps = 6, NH1 - 6
    if i < first:
        return range(i // 2, (i + 1) // 2)
    i = min(i, NH1)
    return range(3 + (ADA_ATTENTION - 3) * (i - first) // steps,
                 min(ADA_ATTENTION, 3 + (ADA_ATTENTION - 3) * (i + 1 - first) // steps))


def behind1(i):
    steps = {
        0: ["hidk"],
        1: ["hidv", "mq0"],
        2: ["mq1", "rot_mq0", "mk0", "mk1"],
        3: ["mq2", "rot_mq1", "mk2", "mk3"],
        4: ["mq3", "rot_mq2", "mk4", "mv0", "kcc"],
        5: ["mq4", "rot_mq3", "mv1", "vbd"],
        6: ["rot_mq4", "cs0", "cs1"],
        7: ["rs0"],
        8: ["rs1", "ro0"],
        9: ["ct", "rs2", "ro1"],
        10: ["co0", "co1", "rs3", "ro2"],
        11: ["rs4", "ro3"],
        12: ["ro4"],
    }
    return steps.get(i, [])


def order1():
    out = ["ss1"]
    for i, u in enumerate(UNITS1):
        out.append(u)
        if i >= 1 and UNITS1[i - 1] in ROPED1:
            out.append("rot_" + UNITS1[i - 1])
    out += ["ssq", "ssk"]
    for j in range(4):
        for t in range(TT):
            out.append(f"tm{j}{t}")
            if (j, t) == (0, 0):
                out.append("rot_r4")
    for i in range(NH1 + 2):
        out += behind1(i)
    out += [f"mt{c}" for c in range(KC)] + [f"wo{n}" for n in range(KC)] + ["ss2"]
    out += [f"up{n}" for n in range(F1)]
    return out + down_steps(F1)


def gates_at(i):
    steps = NH2 + 2
    return range(GATES * i // steps, GATES * (i + 1) // steps)


def order2():
    out = ["ss1"]
    for b in range(len(UNITS2) + 3):
        if b < 8:
            out.append(UNITS2[b])
        if 1 <= b < 9:
            out.append("ss_" + UNITS2[b - 1])
        if b >= 3:
            out.append("rot_" + UNITS2[b - 3])
    out += [f"v{j}{t}" for j in range(2) for t in range(TT)] + LATER2 + ["pw0", "pw1"]
    for i in range(NH2 + 2):
        out += [f"g{n}" for n in gates_at(i)]
    out += [f"yt{c}" for c in range(4)]
    for n in range(KC):
        out += [f"{m}{n}" for m in MIXERS]
    out += [f"wo{n}" for n in range(KC)] + ["ss2"]
    for n in range(F2):
        out += [f"gt{n}", f"up{n}"]
    return out + down_steps(F2)


BANKS = 4


class Turns:

    def __init__(self, names, full, drained):
        self.names, self.base, self.free_base = names, full, drained
        self.at = {n: i for i, n in enumerate(names)}
        assert len(self.at) == len(names)
        self.total = len(names)
        self.turn = {n: i for i, n in enumerate([n for n in names if "." not in n])}
        self.uses = [len([i for i in range(len(self.turn)) if i % BANKS == b]) for b in range(BANKS)]

    def bank(self, name):
        return self.turn[name] % BANKS

    def full(self, name, layer):
        return layer * self.total + (self.base + self.at[name] + 1)

    def free(self, name, layer):
        b = self.bank(name)
        return layer * self.uses[b] + (self.free_base[b] + self.turn[name] // BANKS)

    def drained(self, name, layer):
        return self.free(name, layer) + 1

    def after(self, layers):
        return self.base + layers * self.total, [f + layers * u for f, u in zip(self.free_base, self.uses)]


A1 = Turns(order1(), 0, [1] * BANKS)
AF = Turns(["ssf"], *A1.after(LAYERS))
A2 = Turns(order2(), *AF.after(1))

CONSTS = {}


def _place(table, items):
    at = 0
    for name, width in items:
        table[name] = (at, width)
        at += width
    return at


N_CONST = _place(CONSTS, [("ident", 128), ("rotp", 128), ("rotm", 128), ("rotr", 128), ("half", 128), ("ones", 128),
                          ("mask", 384), ("cmask", 192), ("ckeep", 192), ("bmask", 6), ("inv", 4),
                          ("decay", RET_HEADS * S), ("invc", 2 * S)])
VEC1, VEC2 = {}, {}
N_V1 = _place(VEC1, [("ln1", 8), ("ln2", 8), ("qn", 2), ("kvn", 1), ("posk", 16), ("posv", 16), ("gn", 320)])
N_V2 = _place(VEC2, [("n1", 8), ("n2", 8), ("pscale", 2), ("conv", 6), ("qn", 1), ("kn", 1), ("poolw", 256),
                      ("bada", 48)])
N_ONCE = KC + D
UQ, UKV, W2K, W2V = 0, 960, 1600, 1728


def constants():
    c = np.zeros((P, N_CONST), np.float32)

    def put(name, a):
        at, w = CONSTS[name]
        c[:a.shape[0], at:at + w] = a.reshape(a.shape[0], w)

    def rotation(starts, half):
        m = np.zeros((P, P), np.float32)
        for s in starts:
            for i in range(half):
                m[s + half + i, s + i] = -1.0
                m[s + i, s + half + i] = 1.0
        return m

    i = np.arange(P)
    put("ident", np.eye(P, dtype=np.float32))
    put("rotp", rotation((0, 64), 8))
    put("rotm", rotation((64,), 16))
    put("rotr", rotation((0, 64), 32))
    put("half", (i[:, None] // HD == i[None, :] // HD).astype(np.float32))
    put("ones", np.ones((P, P), np.float32))
    tri = np.where(i[None, :] > i[:, None], NEG, 0.0)
    put("mask", np.concatenate([tri, np.zeros((P, P)), tri], axis=1))
    n = np.arange(NP16)
    t = (np.arange(TT)[None, :] * P + i[:, None])[:, :, None]
    seen = (n * CMP_STRIDE + CMP_LEN - 1 <= t) & (n < N_CMP)
    seen = np.broadcast_to(seen[:, :, None, :], (P, TT, NSA_HEADS, NP16))
    put("cmask", np.where(seen, 0.0, NEG).reshape(P, 192))
    put("ckeep", seen.astype(np.float32).reshape(P, 192))
    r = np.arange(NSA_HEADS * NP16)
    put("bmask", ((r[:, None] // NP16 == np.arange(NSA_HEADS)[None, :]) & (r[:, None] % NP16 < N_CMP)).astype(np.float32))
    inv = np.zeros((P, 4), np.float32)
    e16, e32, e64 = (np.arange(0, d, 2, dtype=np.float32) / np.float32(d) for d in (16, 32, 64))
    power = lambda base, e: np.power(base, e.astype(np.float64)).astype(np.float32)
    one = np.float32(1.0)
    for s in (0, 64):
        inv[s:s + 16, 0] = np.tile(one / power(5e5, e16), 2)
        inv[s:s + 64, 2] = np.tile(one / power(1e4, e64), 2)
        inv[s:s + 16, 3] = np.tile(power(5e5, -e16), 2)
    inv[64:96, 1] = np.tile(one / power(5e5, e32), 2)
    put("inv", inv)
    g = np.log(1.0 - 2.0 ** (-5.0 - np.arange(RET_HEADS)))
    diff = (np.arange(S)[None, :] - i[:, None])[:, None, :]
    put("decay", np.where(diff >= 0, np.exp(np.maximum(diff, 0) * g[None, :, None]), 0.0) * HD ** -0.5)
    win = np.array([[2, 8], [4, 16]])
    w = win[i // HD]
    put("invc", 1.0 / np.minimum(np.arange(S)[None, None, :] + 1, w[:, :, None]))
    return c


def trn_kernel(nc, consts, vec1, vec2, once, pos, xin, stream, out):
    ctx = ExitStack()
    with ctx:
        def sb(name, shape, dt=F32):
            return ctx.enter_context(nc.sbuf_tensor(name, shape, dt))

        def bank(name):
            return ctx.enter_context(nc.psum_tensor(name, [P, 512], F32))

        def sem(name):
            return ctx.enter_context(nc.semaphore(name))

        cst = sb("cst", [P, N_CONST])
        v1all = sb("v1all", [P, LAYERS, N_V1])
        v1 = sb("v1", [P, N_V1])
        v2all = sb("v2all", [P, LAYERS, N_V2])
        v2 = sb("v2", [P, N_V2])
        onc = sb("onc", [P, N_ONCE])
        trig = sb("trig", [P, 2, 4, S])
        ring = sb("ring", [P, RING, TILE])
        x = sb("x", [P, KC, S])
        wH = sb("wH", [P, SPLIT, UNIT], F32R)
        wL = sb("wL", [P, SPLIT, UNIT], F32R)
        h_at = nc.sbuf_base
        hH = sb("hH", [P, KC, S], F32R)
        hL = sb("hL", [P, KC, S], F32R)
        BIG = 24 * S
        WORK = F1 * S * 2 - BIG
        region_at = nc.sbuf_base
        region = sb("region", [P, F1 * S * 2])

        def rounded(name, at, k):
            return nc.alloc_sbuf_tensor_at(name, [P, k, S], F32R, offset=region_at + 4 * at)

        aH, aL = rounded("aH", 0, F1), rounded("aL", F1 * S, F1)
        big = region[:, 0:BIG].rearrange("p (c s) -> p c s", s=S)
        work = region[:, BIG:BIG + WORK]
        nv = sb("nv", [P, 2, S])
        ny = sb("ny", [P, 2, S])
        nt = sb("nt", [P, S])
        rstd = sb("rstd", [P, S])
        tcs = sb("tcs", [P, 2, S])
        tss = sb("tss", [P, 2, S])
        tc, ts = tcs[:, 0, :], tss[:, 0, :]
        tmp4 = [tcs[:, 0, :], tcs[:, 1, :], tss[:, 0, :], tss[:, 1, :]]
        sq_in = work[:, 0:KC * S].rearrange("p (c s) -> p c s", c=KC)
        sq_h = nc.alloc_sbuf_tensor_at("sq_h", [P, KC, S], F32, offset=h_at)
        cursor = [0]

        def piece(*shape):
            n = 1
            for s_ in shape:
                n *= s_
            a = work[:, cursor[0]:cursor[0] + n]
            cursor[0] += n
            assert cursor[0] <= WORK
            if len(shape) == 2:
                a = a.rearrange("p (a b) -> p a b", a=shape[0])
            elif len(shape) == 3:
                a = a.rearrange("p (a b c) -> p a b c", a=shape[0], b=shape[1])
            return a

        rope1 = piece(11, S)
        tokm = piece(TT, TM1)
        qm = piece(MLA_HEADS, S)
        km = piece(MLA_HEADS, S)
        vm = piece(TT, 320)
        hid = piece(2, 32)
        gel = piece(3, 64)
        kcT = piece(NP16)
        grep = piece(2, 96)
        vbd = piece(384)
        pc = piece(192)
        pcT = piece(S)
        cst12 = piece(3, 12)
        gate = piece(TT, 18)
        gnst = piece(6, 10)
        cursor[0] = 0
        qk2 = piece(8, S)
        vv = piece(TT, 512)
        ya = piece(TT, 512)
        up_ = piece(2, 16 + S)
        sw = piece(4, 16 + S)
        yc = piece(2, S)
        cu = piece(2, S)
        cb = piece(2, S)
        cv = piece(2, 2 + S)
        cursor[0] = 0
        cursor[0] = 2048
        merged = piece(4, S)
        y1H = rounded("y1H", BIG + 8192, 4)
        y1L = rounded("y1L", BIG + 9216, 4)
        y2H = rounded("y2H", BIG + 0, 4)
        y2L = rounded("y2L", BIG + 1024, 4)
        modall = sb("modall", [P, LAYERS, 48])
        mod = sb("mod", [P, 48])
        mods = sb("mods", [P, 3, KC])
        adac = sb("adac", [P, 48])
        cb2 = onc[:, KC:KC + D]
        sm = sb("sm", [P, 2, 384])
        pr = sb("pr", [P, 2, 384])
        prT = sb("prT", [P, 2, 384])
        latsq3 = pr[:, :, :].rearrange("p a b -> p (a b)").rearrange("p (c s) -> p c s", c=3)
        nmax = sb("nmax", [P, NH1, 2])
        psumv = sb("psumv", [P, NH1, 2])
        coef = sb("coef", [P, NH1, 2])
        ada_t = big[:, 0:4, :].rearrange("p c s -> p (c s)")
        flat = lambda v: v.rearrange("p c s -> p (c s)")
        decayed = [flat(sq_h[:, 0:4, :])[:, 640:1024], flat(big[:, 6:8, :])[:, 0:384]]
        gn_squares = flat(sq_h[:, 0:3, :])[:, 0:640]
        sq2 = big[:, 8:16, :]
        raw = big[:, 0:16, :]
        mixed = big[:, 16:24, :].rearrange("p a s -> p (a s)").rearrange("p (t f) -> p t f", t=TT)
        fk = [big[:, 16 + 2 * j:18 + 2 * j, :].rearrange("p a s -> p (a s)")[:, 0:480]
              .rearrange("p (m g n) -> p m g n", m=16, g=2) for j in range(2)]
        xk = [big[:, 20 + 2 * j:22 + 2 * j, :] for j in range(2)]
        cqn = big[:, 3:6, :]

        acc = [bank(f"acc{i}") for i in range(BANKS)]
        ps_s = [bank(f"ps_s{i}") for i in range(2)]
        ps_t = bank("ps_t")
        ps_o = bank("ps_o")

        def C(name, rows=P):
            at, w = CONSTS[name]
            return cst[0:rows, at:at + w]

        def V1(name, i=None):
            at, w = VEC1[name]
            return v1[:, at:at + w] if i is None else v1[:, at + i:at + i + 1]

        def V2(name, i=None):
            at, w = VEC2[name]
            return v2[:, at:at + w] if i is None else v2[:, at + i:at + i + 1]

        decay = C("decay").rearrange("p (h s) -> p h s", h=RET_HEADS)
        invc = C("invc").rearrange("p (b s) -> p b s", b=2)

        inputs_in = sem("inputs_in")
        got = [sem(f"got{i}") for i in range(RING)]
        acc_full = sem("acc_full")
        acc_drained = [sem(f"acc_drained{i}") for i in range(BANKS)]
        x_ready = sem("x_ready")
        vec_ready = sem("vec_ready")
        trig_arg = sem("trig_arg")
        trig_ready = sem("trig_ready")
        sq_ready = sem("sq_ready")
        y_ready = sem("y_ready")
        h_ready = sem("h_ready")
        h_pre = sem("h_pre")
        hh_ready = sem("hh_ready")
        hi_ready = sem("hi_ready")
        lo_ready = sem("lo_ready")
        tH_ready = sem("tH_ready")
        aT_ready = sem("aT_ready")
        aH_ready = sem("aH_ready")
        ypH_ready = sem("ypH_ready")
        ycf_ready, ycH_ready = sem("ycf_ready"), sem("ycH_ready")
        mgH_ready = sem("mgH_ready")
        tanh_ready = sem("tanh_ready")
        a2H_ready = sem("a2H_ready")
        mg_ready = sem("mg_ready")
        rope_ready = sem("rope_ready")
        lat_ready = sem("lat_ready")
        latsq = sem("latsq")
        f_ready = sem("f_ready")
        ge = sem("ge")
        gel_ready = sem("gel_ready")
        grep_ready = sem("grep_ready")
        km_ready = sem("km_ready")
        kcT_ready = sem("kcT_ready")
        vbd_ready = sem("vbd_ready")
        csub = sem("csub")
        cexp = sem("cexp")
        pc_ready = sem("pc_ready")
        gexp = sem("gexp")
        gate_ready = sem("gate_ready")
        rw_ready = sem("rw_ready")
        gn_v = sem("gn_v")
        gn_y = sem("gn_y")
        mixed_ready = sem("mixed_ready")
        a_ready = sem("a_ready")
        s_full, s_drained = sem("s_full"), sem("s_drained")
        nmax_ready, p_ready = sem("nmax_ready"), sem("p_ready")
        pt_full, pt_copied = sem("pt_full"), sem("pt_copied")
        o_full, o_drained = sem("o_full"), sem("o_drained")
        ctanh, x_in = sem("ctanh"), sem("x_in")
        ada_dve, ada_pool, ada_act = sem("ada_dve"), sem("ada_pool"), sem("ada_act")
        raw2_sq = sem("raw2_sq")
        qn2_ready = sem("qn2_ready")
        qk2_ready = sem("qk2_ready")
        pad_ready = sem("pad_ready")
        pooled = sem("pooled")
        yc_ready = sem("yc_ready")
        merged_ready = sem("merged_ready")
        ya_ready = sem("ya_ready")
        a2_ready = sem("a2_ready")
        stored = sem("stored")
        dve_step, act_step, pool_step = sem("dve_step"), sem("act_step"), sem("pool_step")

        ROPE1 = {"q0": 0, "q1": 1, "q2": 2, "ks": 3, "kw": 4, "rqa": 5, "rqb": 6, "rka": 7, "rkb": 8}

        def q_nsa(hh):
            g, r = hh // REP, hh % REP
            return slice(64 * g, 64 * g + 64), r

        def ret_q(hh):
            return (slice(64 * (hh % 2), 64 * (hh % 2) + 64), 5 + hh // 2) if hh < 4 else (slice(0, 64), 9)

        def ret_k(hh):
            return (slice(64 * (hh % 2), 64 * (hh % 2) + 64), 7 + hh // 2) if hh < 4 else (slice(0, 64), 10)

        def head1(i):
            kind, hh = HEADS1[i]
            if kind == "mla":
                return qm[0:96, hh, :], km[0:96, hh, :], [vm[:, t, 64 * hh:64 * hh + 64] for t in range(TT)]
            rows, r = q_nsa(hh)
            g = hh // REP
            c = (VS if kind == "slc" else VW) + 64 * g
            return (rope1[rows, r, :], rope1[rows, 3 if kind == "slc" else 4, :],
                    [tokm[:, t, c:c + 64] for t in range(TT)])

        def scale1(i):
            return 96 ** -0.5 if HEADS1[i][0] == "mla" else HD ** -0.5

        def head2(i):
            rows = slice(64 * (i % 2), 64 * (i % 2) + 64)
            return qk2[rows, i // 2, :], qk2[rows, 4 + i // 2, :], [vv[:, t, 64 * i:64 * i + 64] for t in range(TT)]

        X2 = LAYERS * 2 * KC + KC
        X_FINAL = X2 + (2 * LAYERS - 1) * KC
        H2 = LAYERS * 2 * KC
        Q2 = LAYERS * 8 + 4
        Y1, Y2N = 4, 10
        YF, Y2 = LAYERS * Y1, LAYERS * Y1 + 1
        VISITS2 = [LAYERS * len([u for u in range(T1) if u % RING == s_]) for s_ in range(RING)]
        M2 = LAYERS * KC
        r4 = [nv[:, 0, :], nv[:, 1, :], ny[:, 0, :], ny[:, 1, :]]
        pair2 = [nt[:, :], rstd[:, :]]
        LO2 = LAYERS * NU1

        def ro_all(k):
            return big[:, 3 * k:3 * k + 3, :].rearrange("p a s -> p (a s)")[:, 0:640]

        def ro_(hh):
            return ro_all(0).rearrange("p (t f) -> p t f", t=TT)[:, :, 64 * hh:64 * hh + 64]

        def rgx_():
            return ro_all(1).rearrange("p (t f) -> p t f", t=TT)

        def product(n, m):
            return tmp4[2 * (n % 2) + m - 1] if m else merged[:, n % 4, :]

        block = ctx.enter_context(nc.Block())

        @block.sync
        def _(sp):
            sp.dma_start(x[:], xin).then_inc(x_in, 16)
            sp.dma_start(cst[:], consts).then_inc(inputs_in, 16)

            def load(slot, at):
                sp.dma_start(ring[:, slot, :], stream[at]).then_inc(got[slot], 16)

            def wait_free(tiles, turns, units, lo_base, layer, t):
                if tiles[t][0] == "ada":
                    sp.wait_ge(ada_act, layer * N_ADA + (tiles[t][1] + 1))
                elif tiles[t][0] in WHOLE:
                    sp.wait_ge(acc_full, turns.full(last_user(tiles, t, 1), layer))
                else:
                    n = max(u for u, (tile_, _, _) in enumerate(units) if tile_ == t)
                    sp.wait_ge(lo_ready, layer * len(units) + (lo_base + n + 1))

            def rest(tiles, turns, units, lo_base, layer, first):
                for t in range(RING, len(tiles)):
                    wait_free(tiles, turns, units, lo_base, layer, t - RING)
                    load(t % RING, first + t)

            def ahead(tiles, turns, units, lo_base, layer, first):
                n = len(tiles)
                for t in range(n - RING, n):
                    wait_free(tiles, turns, units, lo_base, layer, t)
                    load(t % RING, first + n + t % RING)

            sp.dma_start(v2all[:], vec2).then_inc(inputs_in, 16)
            for s_ in range(RING):
                load(s_, s_)
            with sp.Fori(0, LAYERS) as layer:
                rest(TILES1, A1, SU1, 0, layer, layer * T1)
                ahead(TILES1, A1, SU1, 0, layer, layer * T1)
            with sp.Fori(0, LAYERS - 1) as layer:
                rest(TILES2, A2, SU2, LO2, layer, layer * T2 + LAYERS * T1)
                ahead(TILES2, A2, SU2, LO2, layer, layer * T2 + LAYERS * T1)
            rest(TILES2, A2, SU2, LO2, LAYERS - 1, (LAYERS - 1) * T2 + LAYERS * T1)
            for c in range(0, KC, 2):
                sp.wait_ge(x_ready, X_FINAL + c + 2)
                sp.dma_start(out[:, c:c + 2, :], x[:, c:c + 2, :]).then_inc(stored, 16)
            sp.wait_ge(stored, 16 * KC // 2)


        @block.tensor
        def _(pe):
            for b in range(BANKS):
                pe.sem_inc(acc_drained[b], 1)
            pe.wait_ge(inputs_in, 16 * 5)

            state = {}

            def enter(turns, layer, tiles, visits_base, units, lo_base):
                state.update(turns=turns, layer=layer, next=0, tiles=tiles, visits=visits_base, units=units,
                             lo_base=lo_base, unit=0)

            def open_acc(name):
                tn = state["turns"]
                assert tn.turn[name] == state["next"], name
                state["next"] += 1
                pe.wait_ge(acc_drained[tn.bank(name)], tn.free(name, state["layer"]))
                return acc[tn.bank(name)]

            def tile(kind, j):
                t = state["tiles"].index((kind, j))
                slot = t % RING
                n = len([u for u in range(len(state["tiles"])) if u % RING == slot])
                pe.wait_ge(got[slot], state["layer"] * (16 * n) + 16 * (state["visits"][slot] + t // RING + 1))
                return ring[:, slot, :]

            def next_unit():
                u = state["unit"]
                state["unit"] += 1
                pe.wait_ge(lo_ready, state["layer"] * len(state["units"]) + (state["lo_base"] + u + 1))
                return wH[:, u % SPLIT, :], wL[:, u % SPLIT, :]

            def split_product(out, w, y, first, last):
                pe.matmul(out, w[0], y[0], start=first, stop=False)
                pe.matmul(out, w[0], y[1], start=False, stop=False)
                return pe.matmul(out, w[1], y[0], start=False, stop=last)

            def blocks(parts):
                return [v.rearrange("p (c n) -> p c n", n=P) for v in parts]

            def project(name, y, h_base=None, merged_base=None):
                wh, wl = blocks(next_unit())
                a = open_acc(name)
                for c in range(KC):
                    if h_base is not None:
                        pe.wait_ge(h_ready, state["layer"] * (2 * KC) + (h_base + c + 1))
                    if merged_base is not None:
                        pe.wait_ge(merged_ready, state["layer"] * KC + (merged_base + c + 1))
                    last = split_product(a[:, 0:S], (wh[:, c, :], wl[:, c, :]), y(c), c == 0, c == KC - 1)
                last.then_inc(acc_full, 1)

            def project_tokens(kind, j, n):
                parts = [[v.rearrange("p (c n) -> p c n", n=256) for v in next_unit()] for _ in range(2)]
                for t in range(TT):
                    a = open_acc(f"{kind}{j}{t}")
                    for c in range(KC):
                        wh, wl = (v[:, c % 4, 0:n] for v in parts[c // 4])
                        hh, hl = hH[:, c, t * P:(t + 1) * P], hL[:, c, t * P:(t + 1) * P]
                        last = split_product(a[:, 0:n], (hh, hl), (wh, wl), c == 0, c == KC - 1)
                    last.then_inc(acc_full, 1)
                    if (kind, j, t) == ("tm", 0, 0):
                        rot1("r4")

            def down(kf, ready, base):
                wh = wl = None
                for n in range(KC):
                    a = open_acc(f"dn{n}")
                    for k in range(kf):
                        m = n * kf + k
                        if m % 8 == 0:
                            wh, wl = blocks(next_unit())
                        if n == 0:
                            pe.wait_ge(ready, state["layer"] * kf + (base + k + 1))
                        last = split_product(a[:, 0:S], (wh[:, m % 8, :], wl[:, m % 8, :]), (aH[:, k, :], aL[:, k, :]),
                                             k == 0, k == kf - 1)
                        if m % 8 == 7 and k < kf - 1:
                            last.then_inc(acc_full, 1)
                    last.then_inc(acc_full, 1)

            def sum_squares(name, base):
                sq = sq_in if name == "ss2" else sq_h
                a = open_acc(name)
                for c in range(KC):
                    if c % 2 == 0:
                        pe.wait_ge(sq_ready, base + c // 2 + 1)
                    last = pe.matmul(a[:, 0:S], C("ones"), sq[:, c, :], start=c == 0, stop=c == KC - 1)
                last.then_inc(acc_full, 1)

            def rotate(name, m, src, rows=slice(0, P)):
                a = open_acc("rot_" + name)
                pe.matmul(a[rows, 0:S], m, src, start=True, stop=True).then_inc(acc_full, 1)

            def drained(name):
                tn = state["turns"]
                pe.wait_ge(acc_drained[tn.bank(name)], tn.drained(name, state["layer"]))

            def attention(head, n, base, filler):
                L = state["layer"]
                for i in range(n + 2):
                    if i < n:
                        q, k, _ = head(i)
                        pe.wait_ge(s_drained, L * n + (base + i + 1))
                        b = ps_s[i % 2]
                        pe.matmul(b[:, 0:P], q[:, 0:P], k[:, 0:P], start=True, stop=True)
                        pe.matmul(b[:, P:3 * P], q[:, P:S], k, start=True, stop=True).then_inc(s_full, 1)
                    if 1 <= i <= n:
                        j = i - 1
                        pe.wait_ge(p_ready, L * n + (base + j + 1))
                        pe.wait_ge(pt_copied, L * n + (base + j + 1))
                        for c in range(3):
                            last = pe.transpose(ps_t[:, c * P:(c + 1) * P], pr[:, j % 2, c * P:(c + 1) * P], C("ident"))
                        last.then_inc(pt_full, 1)
                    if i >= 2:
                        j = i - 2
                        _, _, v = head(j)
                        pe.wait_ge(pt_copied, L * n + (base + j + 2))
                        pe.wait_ge(o_drained, L * n + (base + j + 1))
                        pe.matmul(ps_o[:, 0:HD], prT[:, j % 2, 0:P], v[0], start=True, stop=True)
                        pe.matmul(ps_o[:, HD:2 * HD], prT[:, j % 2, P:2 * P], v[0], start=True, stop=False)
                        pe.matmul(ps_o[:, HD:2 * HD], prT[:, j % 2, 2 * P:3 * P], v[1], start=False, stop=True)\
                            .then_inc(o_full, 1)
                    filler(i)

            pe.sem_inc(s_drained, 2)
            pe.sem_inc(pt_copied, 1)
            pe.sem_inc(o_drained, 1)

            hs = lambda c: (hH[:, c, :], hL[:, c, :])
            with pe.Fori(0, LAYERS) as L:
                enter(A1, L, TILES1, [0] * RING, SU1, 0)
                sum_squares("ss1", L * 8)

                def rot1(u):
                    drained(u)
                    i = UNITS1.index(u)
                    if u == "kpe":
                        rotate(u, C("rotm")[0:96, 0:96], raw[0:96, i, :], slice(0, 96))
                    else:
                        rotate(u, C("rotr" if u[0] == "r" else "rotp"), raw[:, i, :])

                for i, u in enumerate(UNITS1):
                    project(u, hs, 0 if i == 0 else None)
                    if i >= 1 and UNITS1[i - 1] in ROPED1:
                        rot1(UNITS1[i - 1])
                pe.wait_ge(latsq, L * 3 + 2)
                a = open_acc("ssq")
                pe.matmul(a[:, 0:S], C("ones"), latsq3[:, 0, :], start=True, stop=False)
                pe.matmul(a[:, 0:S], C("ones"), latsq3[:, 1, :], start=False, stop=True).then_inc(acc_full, 1)
                pe.wait_ge(latsq, L * 3 + 3)
                a = open_acc("ssk")
                pe.matmul(a[:, 0:S], C("ones"), latsq3[:, 2, :], start=True, stop=True).then_inc(acc_full, 1)
                for j in range(4):
                    project_tokens("tm", j, TM_W[j])
                drained("tm30")
                drained("tm31")
                pe.wait_ge(rope_ready, L * 17 + 12)
                uq_of = lambda tl: tl[:, UQ:UQ + 960].rearrange("p (c n) -> p c n", c=2)

                def hidden(kind):
                    j = ("k", "v").index(kind)
                    tl = tile("cmp" + kind, 0).rearrange("p (m n) -> p m n", m=16)
                    pe.wait_ge(f_ready, L * 2 + (j + 1))
                    a = open_acc("hid" + kind)
                    for m in range(16):
                        last = pe.matmul(a[:, 0:30], tl[:, m, :], fk[j][:, m, :, :].rearrange("p g n -> p (g n)"),
                                         start=m == 0, stop=m == 15)
                    last.then_inc(acc_full, 1)

                def mla_queries(hh):
                    if hh == 0:
                        pe.wait_ge(lat_ready, L * 3 + 3)
                    uq = uq_of(tile("small", 0))
                    a = open_acc(f"mq{hh}")
                    for c in range(2):
                        last = pe.matmul(a[0:96, 0:S], uq[:, c, 96 * hh:96 * hh + 96], cqn[:, c, :],
                                         start=c == 0, stop=c == 1)
                    last.then_inc(acc_full, 1)

                def mla_rotate(hh):
                    drained(f"mq{hh}")
                    rotate(f"mq{hh}", C("rotm")[0:96, 0:96], qm[0:96, hh, :], slice(0, 96))

                def mla_keys(hh):
                    a = open_acc(f"mk{hh}")
                    at = UKV + 128 * hh
                    pe.matmul(a[0:64, 0:S], tile("small", 0)[:, at:at + 64], cqn[:, 2, :], start=True, stop=True)\
                        .then_inc(acc_full, 1)

                def mla_values(t):
                    a = open_acc(f"mv{t}")
                    pe.matmul(a[:, 0:320], cqn[:, 2, t * P:(t + 1) * P],
                              tile("small", 0)[:, UKV:UKV + 640].rearrange("p (h n) -> p h n", h=MLA_HEADS)[:, :, 64:128],
                              start=True, stop=True).then_inc(acc_full, 1)

                def compressed_keys():
                    pe.wait_ge(gel_ready, L + 1)
                    a = open_acc("kcc")
                    pe.matmul(a[:, 0:32], tile("small", 0)[:, W2K:W2K + 128], hid[:, 0, :], start=True, stop=True)\
                        .then_inc(acc_full, 1)

                def compressed_values():
                    pe.wait_ge(grep_ready, L + 1)
                    tl = tile("small", 0)
                    a = open_acc("vbd")
                    for g in range(2):
                        last = pe.matmul(a[0:96, 192 * g:192 * g + 192], grep[:, g, :], tl[:, W2V:W2V + 192],
                                         start=True, stop=True)
                    last.then_inc(acc_full, 1)

                def compressed_scores(g):
                    if g == 0:
                        pe.wait_ge(kcT_ready, L * 2 + 2)
                    a = open_acc(f"cs{g}")
                    for t in range(TT):
                        for r in range(REP):
                            rows = slice(64 * g, 64 * g + 64)
                            at = 48 * t + 16 * r
                            last = pe.matmul(a[:, at:at + 16], rope1[rows, r, t * P:(t + 1) * P], kcT[rows, :],
                                             start=True, stop=True)
                    last.then_inc(acc_full, 1)

                def compressed_transposes():
                    pe.wait_ge(pc_ready, L + 1)
                    a = open_acc("ct")
                    for t in range(TT):
                        last = pe.transpose(a[0:96, t * P:(t + 1) * P], pc[:, 96 * t:96 * t + 96], C("ident"))
                    last.then_inc(acc_full, 1)

                def compressed_outputs(t):
                    if t == 0:
                        drained("ct")
                        pe.wait_ge(vbd_ready, L + 1)
                    a = open_acc(f"co{t}")
                    pe.matmul(a[:, 0:384], pcT[0:96, t * P:(t + 1) * P], vbd[0:96, :], start=True, stop=True)\
                        .then_inc(acc_full, 1)

                def retention_scores(hh):
                    a = open_acc(f"rs{hh}")
                    rq, iq = ret_q(hh)
                    rk, ik = ret_k(hh)
                    pe.matmul(a[:, 0:S], rope1[rk, ik, 0:P], rope1[rq, iq, :], start=True, stop=True)
                    pe.matmul(a[:, S:S + P], rope1[rk, ik, P:S], rope1[rq, iq, P:S], start=True, stop=True)\
                        .then_inc(acc_full, 1)

                def retention_outputs(j):
                    pe.wait_ge(rw_ready, L * RET_HEADS + (j + 1))
                    a = open_acc(f"ro{j}")
                    w = decayed[j % 2]
                    v = [tokm[:, t, RV + 64 * j:RV + 64 * j + 64] for t in range(TT)]
                    pe.matmul(a[:, 0:HD], w[:, 0:P], v[0], start=True, stop=True)
                    pe.matmul(a[:, HD:2 * HD], w[:, P:S], v[0], start=True, stop=False)
                    pe.matmul(a[:, HD:2 * HD], w[:, S:S + P], v[1], start=False, stop=True).then_inc(acc_full, 1)

                def others(i):
                    for name in behind1(i):
                        n = int(name[-1]) if name[-1].isdigit() else None
                        if name[:3] == "hid":
                            hidden(name[3])
                        elif name[:3] == "rot":
                            mla_rotate(n)
                        elif name == "kcc":
                            compressed_keys()
                        elif name == "vbd":
                            compressed_values()
                        elif name == "ct":
                            compressed_transposes()
                        else:
                            {"mq": mla_queries, "mk": mla_keys, "mv": mla_values, "cs": compressed_scores,
                             "co": compressed_outputs, "rs": retention_scores, "ro": retention_outputs}[name[:2]](n)
                    if i == 2 * NSA_HEADS - 1:
                        pe.wait_ge(km_ready, L + 1)
                        pe.wait_ge(rope_ready, L * 17 + 17)

                attention(head1, NH1, 0, others)
                pe.wait_ge(mixed_ready, L + 1)
                for c in range(KC):
                    a = open_acc(f"mt{c}")
                    for t in range(TT):
                        last = pe.transpose(a[:, t * P:(t + 1) * P], mixed[:, t, c * P:(c + 1) * P], C("ident"))
                    last.then_inc(acc_full, 1)
                for c in range(KC):
                    drained(f"mt{c}")
                for n in range(KC):
                    project(f"wo{n}", hs)
                sum_squares("ss2", L * 8 + 4)
                for n in range(F1):
                    project(f"up{n}", hs, KC if n == 0 else None)
                down(F1, a_ready, 0)

            enter(AF, 0, TILES2, VISITS2, SU2, LO2)
            sum_squares("ssf", LAYERS * 8)

            with pe.Fori(0, LAYERS) as L:
                enter(A2, L, TILES2, VISITS2, SU2, LO2)
                sum_squares("ss1", L * 8 + Q2)
                for b in range(len(UNITS2) + 3):
                    if b < 8:
                        project(UNITS2[b], hs, H2 if b == 0 else None)
                    if 1 <= b < 9:
                        pe.wait_ge(raw2_sq, L * 8 + b)
                        a = open_acc("ss_" + UNITS2[b - 1])
                        pe.matmul(a[:, 0:S], C("half"), sq2[:, b - 1, :], start=True, stop=True).then_inc(acc_full, 1)
                    if b >= 3:
                        pe.wait_ge(qn2_ready, L * 8 + (b - 2))
                        rotate(UNITS2[b - 3], C("rotp"), qk2[:, b - 3, :])
                for j in range(2):
                    project_tokens("v", j, 256)
                for u in LATER2:
                    project(u, hs)
                for b in range(2):
                    pe.wait_ge(pooled, L * 2 + (b + 1))
                    a = open_acc(f"pw{b}")
                    pe.matmul(a[:, 0:S], V2("poolw")[:, 128 * b:128 * b + 128], sw[:, 2 * b, 16:16 + S],
                              start=True, stop=True).then_inc(acc_full, 1)

                def gates(i):
                    for n in gates_at(i):
                        project(f"g{n}", hs)

                pe.wait_ge(qk2_ready, L * 8 + 8)
                drained(f"v{1}{1}")
                drained(f"v{1}{0}")
                attention(head2, NH2, LAYERS * NH1, gates)
                pe.wait_ge(ya_ready, L + 1)
                for c in range(4):
                    a = open_acc(f"yt{c}")
                    for t in range(TT):
                        last = pe.transpose(a[:, t * P:(t + 1) * P], ya[:, t, c * P:(c + 1) * P], C("ident"))
                    last.then_inc(acc_full, 1)
                for name in ["pw0", "pw1"] + [f"yt{c}" for c in range(4)]:
                    drained(name)
                pe.wait_ge(yc_ready, L * 2 + 2)
                for n in range(KC):
                    wh, wl = blocks(next_unit())
                    for name, first, k in (("P", 0, 2), ("C", 2, 2), ("A", 4, 4)):
                        a = open_acc(f"{name}{n}")
                        for c in range(first, first + k):
                            yh, yl = (y1H, y1L) if c < 4 else (y2H, y2L)
                            last = split_product(a[:, 0:S], (wh[:, c, :], wl[:, c, :]), (yh[:, c % 4, :], yl[:, c % 4, :]),
                                                 c == first, c == first + k - 1)
                        last.then_inc(acc_full, 1)
                for n in range(KC):
                    project(f"wo{n}", hs, merged_base=0 if n == 0 else None)
                sum_squares("ss2", L * 8 + (Q2 + 4))
                for n in range(F2):
                    project(f"gt{n}", hs, H2 + KC if n == 0 else None)
                    project(f"up{n}", hs)
                down(F2, a2_ready, 0)

        def psum_of(tn, name):
            return acc[tn.bank(name)]

        @block.scalar
        def _(act):
            act.dma_start(v1all[:], vec1).then_inc(inputs_in, 16)
            act.dma_start(onc[:], once).then_inc(inputs_in, 16)
            act.dma_start(nv[:].bitcast(I32), pos).then_inc(inputs_in, 16)
            act.wait_ge(x_in, 16)
            for i in range(4):
                act.activation(sq_h[:, 2 * i:2 * i + 2, :], x[:, 2 * i:2 * i + 2, :], ACT.Square).then_inc(sq_ready, 1)
            act.wait_ge(inputs_in, 16 * 5)
            act.wait_ge(trig_arg, 2)
            for j in range(2):
                act.activation(trig[:, j, :, :], trig[:, j, :, :], ACT.Sin).then_inc(trig_ready, 1)
            act.activation(ada_t, cb2, ACT.Tanh, scale=0.5).then_inc(ctanh, 1)

            own = [0]

            def link(ins):
                own[0] += 1
                ins.then_inc(act_step, 1)
                act.wait_ge(act_step, own[0])

            def end_layer():
                act.sem_clear(act_step)
                own[0] = 0

            def full(tn, name, L):
                act.wait_ge(acc_full, tn.full(name, L))
                return psum_of(tn, name)

            def take(tn, name, L, dst, rows=slice(0, P), n=S, func=ACT.Copy, **kw):
                a = full(tn, name, L)
                act.activation(dst, a[rows, 0:n], func, **kw).then_inc(acc_drained[tn.bank(name)], 1)

            def square_pair(i, sq):
                act.activation(sq[:, 2 * i:2 * i + 2, :], x[:, 2 * i:2 * i + 2, :], ACT.Square).then_inc(sq_ready, 1)

            def round_h(count):
                for c in range(KC):
                    act.wait_ge(h_pre, count + (c + 1))
                    act.activation(hH[:, c, :], tmp4[c % 4], ACT.Copy).then_inc(hh_ready, 1)

            def out_and_norm(first_unit, x_count, tn, L):
                for n in range(KC):
                    feed(first_unit + n + 1 + SPLIT)
                    if n % 2 == 1:
                        act.wait_ge(x_ready, x_count + (n + 1))
                        square_pair(n // 2, sq_in)
                estimate(tn, "ss2", L, 0)

            def ada_sum(j, L):
                act.wait_ge(ada_pool, L * N_ADA + (j + 1))
                slot = TILES1.index(("ada", j)) % RING
                products = ring[:, slot, UNIT:2 * UNIT]
                act.activation(products, products, ACT.Copy, accum_out=adac[:, 2 * j + 1:2 * j + 2]).then_inc(ada_act, 1)

            fed = {}

            def feed_layer(tn, tiles, units, lo_base, visits, L):
                fed.update(tn=tn, tiles=tiles, units=units, visits=visits, L=L, next=0)

            def feed(count):
                tn, L = fed["tn"], fed["L"]
                for u in range(fed["next"], min(count, len(fed["units"]))):
                    t, half, _ = fed["units"][u]
                    slot = t % RING
                    if half == 0:
                        n = len([v for v in range(len(fed["tiles"])) if v % RING == slot])
                        act.wait_ge(got[slot], L * (16 * n) + 16 * (fed["visits"][slot] + t // RING + 1))
                    if u >= SPLIT:
                        act.wait_ge(acc_full, tn.full(fed["units"][u - SPLIT][2], L))
                    act.activation(wH[:, u % SPLIT, :], ring[:, slot, half * UNIT:(half + 1) * UNIT], ACT.Copy)\
                        .then_inc(hi_ready, 1)
                    fed["next"] = u + 1
                    kind, j = fed["tiles"][t - 1]
                    if half == 1 and kind == "ada" and j >= ADA_ATTENTION:
                        ada_sum(j, L)

            def estimate(tn, name, L, i):
                act.wait_ge(acc_drained[tn.bank(name)], tn.drained(name, L))
                link(act.activation(ny[:, i, :], nv[:, i, :], ACT.Ln))
                act.activation(ny[:, i, :], ny[:, i, :], ACT.Exp, scale=-0.5).then_inc(y_ready, 1)

            def down_squares(steps, x_count):
                release = {name: u for u, (_, _, name) in enumerate(fed["units"]) if name.startswith("dn")}
                for name in steps:
                    if "." not in name and int(name[2:]) % 2 == 1:
                        n = int(name[2:])
                        act.wait_ge(x_ready, x_count + (n + 1))
                        square_pair(n // 2, sq_h)
                    if name in release:
                        feed(release[name] + 1 + SPLIT)

            def attention(n, base, L, extra):
                for i in range(n + 1):
                    if i < n:
                        act.wait_ge(nmax_ready, L * n + (base + i + 1))
                        act.activation(pr[:, i % 2, 0:P], sm[:, i % 2, 0:P], ACT.Exp,
                                       bias=nmax[:, i, 0:1], accum_out=psumv[:, i, 0:1])
                        act.activation(pr[:, i % 2, P:3 * P], sm[:, i % 2, P:3 * P], ACT.Exp,
                                       bias=nmax[:, i, 1:2], accum_out=psumv[:, i, 1:2]).then_inc(p_ready, 1)
                    if i >= 1:
                        act.wait_ge(pt_full, L * n + (base + i))
                        act.activation(prT[:, (i - 1) % 2, :], ps_t[:, 0:3 * P], ACT.Copy).then_inc(pt_copied, 1)
                    extra(i)

            with act.Fori(0, LAYERS) as L:
                act.wait_ge(vec_ready, L + 1)
                feed_layer(A1, TILES1, SU1, 0, [0] * RING, L)
                feed(2)
                estimate(A1, "ss1", L, 0)
                round_h(L * (2 * KC))
                feed(SPLIT)
                for i, u in enumerate(UNITS1):
                    take(A1, u, L, raw[:, i, :])
                    if u in ("cq0", "cq1", "ckv"):
                        k = ("cq0", "cq1", "ckv").index(u)
                        act.wait_ge(acc_drained[A1.bank(u)], A1.drained(u, L))
                        act.activation(latsq3[:, k, :], raw[:, i, :], ACT.Square).then_inc(latsq, 1)
                    feed(i + 1 + SPLIT)
                estimate(A1, "ssq", L, 0)
                estimate(A1, "ssk", L, 1)
                for j in range(4):
                    for t in range(TT):
                        take(A1, f"tm{j}{t}", L, tokm[:, t, 256 * j:256 * j + TM_W[j]], n=TM_W[j])
                    feed(min(16 + 2 * (j + 1) + SPLIT, 24))
                act.wait_ge(acc_drained[A1.bank("tm11")], A1.drained("tm11", L))
                act.activation(gate, tokm[:, :, GT:GT + 18], ACT.Exp, scale=-1.0).then_inc(gexp, 1)
                def ada(i):
                    for j in ada_at(i - 1) if i >= 1 else ():
                        ada_sum(j, L)

                def behind(i):
                    if i == 3:
                        act.wait_ge(ge, L * 2 + 1)
                        act.activation(gel[:, 1, 0:60], gel[:, 1, 0:60], ACT.Exp, scale=-2.0 * GELU_C).then_inc(ge, 1)
                    if i == 7:
                        act.wait_ge(csub, L + 1)
                        act.activation(pc[:], pc[:], ACT.Exp).then_inc(cexp, 1)
                    if i == 8:
                        act.activation(rgx_(), tokm[:, :, RG:RG + 320], ACT.Tanh, scale=0.5).then_inc(gexp, 1)
                    for name in behind1(i) + [n for n in behind1(i - 1) if n[:2] == "ro" and n[:3] != "rot"]:
                        n = int(name[-1]) if name[-1].isdigit() else None
                        if name[:3] == "hid":
                            take(A1, name, L, gel[:, 0, 30 * (name == "hidv"):30 * (name == "hidv") + 30], n=30)
                        elif name[:2] == "mq":
                            take(A1, name, L, qm[0:96, n, :], rows=slice(0, 96))
                        elif name[:2] == "mk":
                            take(A1, name, L, km[0:64, n, :], rows=slice(0, 64))
                        elif name[:2] == "mv":
                            take(A1, name, L, vm[:, n, :], n=320)
                        elif name == "ct":
                            take(A1, name, L, pcT[0:96, :], rows=slice(0, 96))
                        elif name[:2] == "ro" and name[:3] != "rot" and name in behind1(i - 1):
                            a = full(A1, name, L)
                            act.activation(ro_(n), a[:, 0:2 * HD].rearrange("p (t d) -> p t d", t=TT), ACT.Copy)\
                                .then_inc(acc_drained[A1.bank(name)], 1)
                    if i == 16:
                        act.wait_ge(gn_v, L + 1)
                        link(act.activation(gnst[:, 3, :], gnst[:, 2, :], ACT.Ln))
                        act.activation(gnst[:, 3, :], gnst[:, 3, :], ACT.Exp, scale=-0.5).then_inc(gn_y, 1)
                    ada(i)

                attention(NH1, 0, L, behind)
                feed(24 + SPLIT // 2)
                for c in range(KC):
                    a = full(A1, f"mt{c}", L)
                    act.activation(hH[:, c, :], a[:, 0:S], ACT.Copy).then_inc(tH_ready, 1)
                feed(24 + SPLIT)
                out_and_norm(24, L * (2 * KC), A1, L)
                round_h(L * (2 * KC) + KC)
                for n in range(F1):
                    a = full(A1, f"up{n}", L)
                    if n >= 4:
                        act.wait_ge(a_ready, L * F1 + (n - 3))
                    act.activation(r4[n % 4], a[:, 0:S], ACT.Relu).then_inc(acc_drained[A1.bank(f"up{n}")], 1)
                    act.wait_ge(acc_drained[A1.bank(f"up{n}")], A1.drained(f"up{n}", L))
                    act.activation(aH[:, n, :], r4[n % 4], ACT.Square).then_inc(aH_ready, 1)
                    feed(32 + n + 1 + SPLIT)
                down_squares(down_steps(F1), L * (2 * KC) + KC)
                end_layer()
            estimate(AF, "ssf", 0, 0)
            for i in range(4):
                act.wait_ge(x_ready, LAYERS * 2 * KC + 2 * i + 2)
                square_pair(i, sq_h)
            end_layer()
            with act.Fori(0, LAYERS) as L:
                act.wait_ge(vec_ready, L + (LAYERS + 1))
                feed_layer(A2, TILES2, SU2, LO2, VISITS2, L)
                feed(2)
                estimate(A2, "ss1", L, 0)
                round_h(L * (2 * KC) + H2)
                feed(SPLIT)
                for b in range(len(UNITS2) + 1):
                    if b < 8:
                        u = UNITS2[b]
                        take(A2, u, L, raw[:, b, :])
                        act.wait_ge(acc_drained[A2.bank(u)], A2.drained(u, L))
                        act.activation(sq2[:, b, :], raw[:, b, :], ACT.Square).then_inc(raw2_sq, 1)
                        feed(b + 1 + SPLIT)
                    if b >= 1:
                        estimate(A2, "ss_" + UNITS2[b - 1], L, (b - 1) % 2)
                for j in range(2):
                    for t in range(TT):
                        take(A2, f"v{j}{t}", L, vv[:, t, 256 * j:256 * j + 256])
                    feed(8 + 2 * (j + 1) + SPLIT)
                act.wait_ge(pad_ready, L + 1)
                for i, u in enumerate(LATER2):
                    if u[:2] != "cc":
                        dst = up_[:, i, 16:16 + S] if i < 2 else (cu if i < 4 else cb)[:, i % 2, :]
                        take(A2, u, L, dst)
                    feed(12 + i + 1 + SPLIT)
                for b in range(2):
                    a = full(A2, f"pw{b}", L)
                    act.activation(y1H[:, b, :], a[:, 0:S], ACT.Identity, scale=V2("pscale", b)).then_inc(ypH_ready, 1)
                for b in range(2):
                    act.wait_ge(ycf_ready, L * 2 + (b + 1))
                    act.activation(y1H[:, 2 + b, :], yc[:, b, :], ACT.Copy).then_inc(ycH_ready, 1)

                def gates(i):
                    for n in gates_at(i):
                        take(A2, f"g{n}", L, big[:, n, :], func=ACT.Tanh, scale=0.5)
                        feed(20 + n + 1 + SPLIT)

                attention(NH2, LAYERS * NH1, L, gates)
                gates(NH2 + 1)
                for c in range(4):
                    a = full(A2, f"yt{c}", L)
                    act.activation(y2H[:, c, :], a[:, 0:S], ACT.Copy).then_inc(tH_ready, 1)
                for n in range(KC):
                    feed(44 + n + 1 + SPLIT)
                    act.wait_ge(mg_ready, L * KC + (n + 1))
                    act.activation(hH[:, n, :], merged[:, n % 4, :], ACT.Copy).then_inc(mgH_ready, 1)
                out_and_norm(52, L * (2 * KC) + X2, A2, L)
                round_h(L * (2 * KC) + (H2 + KC))
                for n in range(F2):
                    a = full(A2, f"gt{n}", L)
                    if n >= 4:
                        act.wait_ge(a2_ready, L * F2 + (n - 3))
                    act.activation(r4[n % 4], a[:, 0:S], ACT.Tanh, scale=0.5).then_inc(tanh_ready, 1)
                    feed(60 + 2 * n + 1 + SPLIT)
                    act.wait_ge(aT_ready, L * F2 + (n + 1))
                    act.activation(aH[:, n, :], pair2[n % 2], ACT.Copy).then_inc(a2H_ready, 1)
                    feed(60 + 2 * n + 2 + SPLIT)
                down_squares(down_steps(F2), L * (2 * KC) + (X2 + KC))
                end_layer()

        @block.vector
        def _(dve):
            own = [0]

            def link(ins):
                own[0] += 1
                ins.then_inc(dve_step, 1)
                dve.wait_ge(dve_step, own[0])

            def end_layer():
                dve.sem_clear(dve_step)
                own[0] = 0

            turn_of_rope = [0]
            TTN, TSC, STT = nc.vector.tensor_tensor, nc.vector.tensor_scalar, nc.vector.scalar_tensor_tensor

            dve.wait_ge(inputs_in, 16 * 5)
            posf, ang, k, r = big[:, 0:2, :], big[:, 2:6, :], big[:, 6:10, :], big[:, 10:14, :]
            link(nc.vector.tensor_copy(posf, nv[:].bitcast(I32)))
            iat = CONSTS["inv"][0]
            for j in range(4):
                last = TSC(ang[:, j, :], posf[:, j // 3, :], cst[:, iat + j:iat + j + 1], None, ALU.mult)
                link(last)
            magic = 12582912.0
            turn = 2.0 * np.pi
            c1 = 6.28125
            c2 = float(np.float32(turn - c1))
            c3 = float(np.float32(turn - c1 - np.float64(np.float32(turn - c1))))
            link(TSC(k, ang, float(1.0 / turn), None, ALU.mult))
            link(TSC(k, k, magic, None, ALU.add))
            link(TSC(k, k, magic, None, ALU.subtract))
            link(STT(r, k, -c1, ang, ALU.mult, ALU.add))
            link(STT(r, k, -c2, r, ALU.mult, ALU.add))
            link(STT(r, k, -c3, r, ALU.mult, ALU.add))
            lim = 3.1415925
            TSC(trig[:, 1, :, :], r, lim, -lim, ALU.min, ALU.max).then_inc(trig_arg, 1)
            link(STT(k, r, -1.0, r, ALU.mult, ALU.max))
            TSC(trig[:, 0, :, :], k, -1.0, float(np.pi / 2), ALU.mult, ALU.add).then_inc(trig_arg, 1)
            dve.wait_ge(ctanh, 1)
            link(STT(cb2, ada_t, 1.0, cb2, ALU.add, ALU.mult))
            dve.wait_ge(trig_ready, 2)
            end_layer()

            def full(tn, name, L):
                dve.wait_ge(acc_full, tn.full(name, L))
                return psum_of(tn, name)

            def ada(j, L):
                slot = TILES1.index(("ada", j)) % RING
                n = len([u for u in range(T1) if u % RING == slot])
                dve.wait_ge(got[slot], L * (16 * n) + 16 * (TILES1.index(("ada", j)) // RING + 1))
                products = ring[:, slot, 0:UNIT]
                STT(products, products, 1.0, cb2, ALU.mult, ALU.mult, accum_out=adac[:, 2 * j:2 * j + 1])\
                    .then_inc(ada_dve, 1)

            fed = {}

            def feed_layer(tiles, units, lo_base, L):
                fed.update(tiles=tiles, units=units, lo_base=lo_base, L=L, next=0)

            def feed(count):
                for u in range(fed["next"], min(count, len(fed["units"]))):
                    t, half, _ = fed["units"][u]
                    dve.wait_ge(hi_ready, fed["L"] * len(fed["units"]) + (fed["lo_base"] + u + 1))
                    TTN(wL[:, u % SPLIT, :], ring[:, t % RING, half * UNIT:(half + 1) * UNIT],
                        wH[:, u % SPLIT, :].bitcast(F32), ALU.subtract).then_inc(lo_ready, 1)
                    fed["next"] = u + 1
                    kind, j = fed["tiles"][min(t + 1, len(fed["tiles"]) - 1)]
                    if half == 1 and kind == "ada" and j >= ADA_ATTENTION:
                        ada(j, fed["L"])

            def rest_of(dst, src, hi):
                return TTN(dst, src, hi.bitcast(F32), ALU.subtract)

            def norm_out(gain, shift, count):
                for c in range(KC + 1):
                    if c < KC:
                        last = STT(tmp4[c % 4], x[:, c, :], gain(c), rstd[:], ALU.mult, ALU.mult)
                        if shift is not None:
                            link(last)
                            last = TSC(tmp4[c % 4], tmp4[c % 4], shift(c), None, ALU.add)
                        last.then_inc(h_pre, 1)
                    if c >= 1:
                        dve.wait_ge(hh_ready, count + c)
                        rest_of(hL[:, c - 1, :], tmp4[(c - 1) % 4], hH[:, c - 1, :]).then_inc(h_ready, 1)

            def last_product(steps, units, turns, L, evac):
                release = {name: u for u, (_, _, name) in enumerate(units) if name.startswith("dn")}
                for name in steps:
                    if "." not in name:
                        evac(int(name[2:]))
                    if name in release:
                        feed(release[name] + 1 + SPLIT)

            def mean_square(tn, name, L, i, n):
                a = full(tn, name, L)
                TSC(nv[:, i, :], a[:, 0:S], 1.0 / n, EPS, ALU.mult, ALU.add).then_inc(acc_drained[tn.bank(name)], 1)

            def refine(i, count, v=None, y=None, t=None, dst=None):
                v = nv[:, i, :] if v is None else v
                y = ny[:, i, :] if y is None else y
                t = nt[:, :] if t is None else t
                dst = rstd[:, :] if dst is None else dst
                link(TTN(t, y, y, ALU.mult))
                link(STT(t, v, -0.5, t, ALU.mult, ALU.mult))
                link(STT(dst, t, 1.5, y, ALU.add, ALU.mult))

            def rope(tn, name, L, src, tab, outs, signal, rows=slice(0, P)):
                turn_of_rope[0] ^= 1
                tc, ts = tcs[:, turn_of_rope[0], :], tss[:, turn_of_rope[0], :]
                TTN(tc[rows, :], src, trig[rows, 0, tab, :], ALU.mult)
                a = full(tn, "rot_" + name, L)
                TTN(ts[rows, :], a[rows, 0:S], trig[rows, 1, tab, :], ALU.mult)\
                    .then_inc(acc_drained[tn.bank("rot_" + name)], 1)
                dve.wait_ge(acc_drained[tn.bank("rot_" + name)], tn.drained("rot_" + name, L))
                for dst, part in outs:
                    last = TTN(dst, tc[part, :], ts[part, :], ALU.add)
                last.then_inc(signal, 1)

            def scores(i, n, base, L, scale):
                if i >= 2:
                    dve.wait_ge(p_ready, L * n + (base + i - 1))
                dve.wait_ge(s_full, L * n + (base + i + 1))
                STT(sm[:, i % 2, :], ps_s[i % 2][:, 0:384], scale, C("mask"), ALU.mult, ALU.add).then_inc(s_drained, 1)
                dve.wait_ge(s_drained, L * n + (base + i + 3))
                nc.vector.tensor_reduce(nmax[:, i, 0:1], sm[:, i % 2, 0:P], AX.X, ALU.max, negate=True)
                nc.vector.tensor_reduce(nmax[:, i, 1:2], sm[:, i % 2, P:3 * P], AX.X, ALU.max, negate=True)\
                    .then_inc(nmax_ready, 1)

            with dve.Fori(0, LAYERS) as L:
                own[0] = 0
                nc.vector.tensor_copy(v1[:], v1all[:, L, :]).then_inc(vec_ready, 1)
                dve.wait_ge(vec_ready, L + 1)
                feed_layer(TILES1, SU1, 0, L)
                mean_square(A1, "ss1", L, 0, D)
                feed(2)
                dve.wait_ge(y_ready, L * Y1 + 1)
                refine(0, None)
                norm_out(lambda c: V1("ln1", c), None, L * (2 * KC))
                feed(SPLIT)

                def rope1_block(u):
                    i = UNITS1.index(u)
                    dve.wait_ge(acc_drained[A1.bank(u)], A1.drained(u, L))
                    allr = slice(0, P)
                    if u == "kpe":
                        rope(A1, u, L, raw[64:96, i, :], 1, [(km[64:96, 0, :], slice(64, 96))], rope_ready, slice(64, 96))
                        dve.wait_ge(rope_ready, L * 17 + 7)
                        nc.vector.tensor_copy(km[64:96, 1:5, :], km[64:96, 0:1, :].to_broadcast([32, 4, S]))\
                            .then_inc(km_ready, 1)
                    elif u == "kc":
                        rope(A1, u, L, raw[:, i, :], 0, [(nt[:, :], allr)], rope_ready)
                        dve.wait_ge(rope_ready, L * 17 + 6)
                        shifted(nt[:, :], 0)
                    elif u == "r4":
                        rope(A1, u, L, raw[:, i, :], 2, [(rope1[0:64, 9, :], slice(0, 64)), (rope1[0:64, 10, :], slice(64, 128))],
                             rope_ready)
                    else:
                        rope(A1, u, L, raw[:, i, :], 2 if u[0] == "r" else 0, [(rope1[:, ROPE1[u], :], allr)], rope_ready)

                def shifted(src, j):
                    cp = nc.vector.tensor_copy
                    cp(xk[j][0:64, 0, :], src[0:64, :])
                    cp(xk[j][64:128, 1, 0:S - 1], src[64:128, 1:S])
                    cp(xk[j][64:128, 0, 0:S - 1], src[0:64, 1:S])
                    link(cp(xk[j][0:64, 1, :], src[64:128, :]))
                    for g in range(2):
                        part = fk[j][:, :, g, :]
                        a0 = xk[j][:, g, 0:240].rearrange("p (n m two) -> p m two n", m=8, two=2)[:, :, 0, :]
                        a1 = xk[j][:, g, 16:256].rearrange("p (n m two) -> p m two n", m=8, two=2)[:, :, 0, :]
                        pos_ = V1("posk" if j == 0 else "posv")
                        TTN(part[:, 0:8, :], a0, pos_[:, 0:8].unsqueeze(2).to_broadcast([P, 8, N_CMP]), ALU.add)
                        last = TTN(part[:, 8:16, :], a1, pos_[:, 8:16].unsqueeze(2).to_broadcast([P, 8, N_CMP]), ALU.add)
                    last.then_inc(f_ready, 1)

                for i, u in enumerate(UNITS1):
                    if i >= 1 and UNITS1[i - 1] in ROPED1:
                        rope1_block(UNITS1[i - 1])
                    if u == "vc":
                        dve.wait_ge(acc_drained[A1.bank(u)], A1.drained(u, L))
                        vraw = raw[:, i, :]
                    feed(i + 1 + SPLIT)
                mean_square(A1, "ssq", L, 0, 256)
                mean_square(A1, "ssk", L, 1, 128)
                dve.wait_ge(y_ready, L * Y1 + 2)
                refine(0, None)
                for c in range(2):
                    STT(cqn[:, c, :], raw[:, 7 + c, :], V1("qn", c), rstd[:], ALU.mult, ALU.mult).then_inc(lat_ready, 1)
                dve.wait_ge(y_ready, L * Y1 + 3)
                refine(1, None)
                STT(cqn[:, 2, :], raw[:, 9, :], V1("kvn", 0), rstd[:], ALU.mult, ALU.mult).then_inc(lat_ready, 1)
                feed(min(16 + 2 + SPLIT, 24))
                rope1_block("r4")
                shifted(vraw, 1)
                for j in range(4):
                    feed(min(16 + 2 * (j + 1) + SPLIT, 24))
                dve.wait_ge(gexp, L * 2 + 1)
                link(TSC(gate, gate, 1.0, None, ALU.add))
                nc.vector.reciprocal(gate, gate).then_inc(gate_ready, 1)
                dve.wait_ge(gate_ready, L + 1)

                def output(i):
                    kind, hh = HEADS1[i]
                    dve.wait_ge(p_ready, L * NH1 + (i + 1))
                    link(nc.vector.reciprocal(coef[:, i, :], psumv[:, i, :]))
                    if kind != "mla":
                        b = 3 * hh + (1 if kind == "slc" else 2)
                        link(TTN(coef[:, i, :].unsqueeze(2), coef[:, i, :].unsqueeze(2), gate[:, :, b:b + 1], ALU.mult))
                    dve.wait_ge(o_full, L * NH1 + (i + 1))
                    for t in range(TT):
                        o = ps_o[:, 64 * t:64 * t + 64]
                        if kind != "win":
                            m = mixed[:, t, 384 + 64 * hh:448 + 64 * hh] if kind == "mla" else \
                                mixed[:, t, 64 * hh:64 * hh + 64]
                            last = TSC(m, o, coef[:, i, t:t + 1], None, ALU.mult)
                        else:
                            m = mixed[:, t, 64 * hh:64 * hh + 64]
                            last = STT(m, o, coef[:, i, t:t + 1], m, ALU.mult, ALU.add)
                    last.then_inc(o_drained, 1)

                def decay_scores(hh):
                    a = full(A1, f"rs{hh}", L)
                    w = decayed[hh % 2]
                    if hh >= 2:
                        dve.wait_ge(acc_full, A1.full(f"ro{hh - 2}", L))
                    TTN(w[:, 0:S], a[:, 0:S], decay[:, hh, :], ALU.mult)
                    TTN(w[:, S:S + P], a[:, S:S + P], decay[:, hh, 0:P], ALU.mult).then_inc(rw_ready, 1)
                    dve.wait_ge(rw_ready, L * RET_HEADS + (hh + 1))
                    dve.sem_inc(acc_drained[A1.bank(f"rs{hh}")], 1)

                o10 = ro_all(0).rearrange("p (h d) -> p h d", d=HD)
                s10 = gn_squares.rearrange("p (h d) -> p h d", d=HD)
                gx_ = rgx_()
                bg = lambda v: v.unsqueeze(2).to_broadcast([P, 10, HD])

                def gelu_argument():
                    for kind in ("k", "v"):
                        dve.wait_ge(acc_drained[A1.bank("hid" + kind)], A1.drained("hid" + kind, L))
                    gx, gu = gel[:, 0, 0:60], gel[:, 1, 0:60]
                    link(TTN(gu, gx, gx, ALU.mult))
                    link(TSC(gu, gu, 0.044715, 1.0, ALU.mult, ALU.add))
                    TTN(gu, gu, gx, ALU.mult).then_inc(ge, 1)

                def gelu():
                    gu, gd = gel[:, 1, 0:60], gel[:, 2, 0:60]
                    dve.wait_ge(ge, L * 2 + 2)
                    link(TSC(gd, gu, 1.0, None, ALU.add))
                    link(nc.vector.reciprocal(gu, gd))
                    link(nc.vector.memset(hid[:, :, :], 0.0))
                    for j in range(2):
                        last = TTN(hid[:, j, :].rearrange("p (g n) -> p g n", g=2)[:, :, 0:N_CMP],
                                   gel[:, 0, 30 * j:30 * j + 30].rearrange("p (g n) -> p g n", g=2),
                                   gel[:, 1, 30 * j:30 * j + 30].rearrange("p (g n) -> p g n", g=2), ALU.mult)
                    last.then_inc(gel_ready, 1)
                    dve.wait_ge(gel_ready, L + 1)
                    for g in range(2):
                        last = nc.vector.tensor_copy(grep[:, g, :].rearrange("p (h n) -> p h n", h=NSA_HEADS),
                                                     hid[:, 1, 16 * g:16 * g + 16].unsqueeze(1).to_broadcast([P, NSA_HEADS, 16]))
                    last.then_inc(grep_ready, 1)

                def rotate_query(hh):
                    dve.wait_ge(acc_drained[A1.bank(f"mq{hh}")], A1.drained(f"mq{hh}", L))
                    rope(A1, f"mq{hh}", L, qm[64:96, hh, :], 1, [(qm[64:96, hh, :], slice(64, 96))], rope_ready,
                         slice(64, 96))

                def take_keys():
                    a = full(A1, "kcc", L)
                    nc.vector.tensor_copy(kcT[0:64, :], a[0:64, 0:16]).then_inc(kcT_ready, 1)
                    nc.vector.tensor_copy(kcT[64:128, :], a[64:128, 16:32]).then_inc(kcT_ready, 1)
                    dve.wait_ge(kcT_ready, L * 2 + 2)
                    dve.sem_inc(acc_drained[A1.bank("kcc")], 1)

                def mask_values():
                    a = full(A1, "vbd", L)
                    TTN(vbd[0:96, :].rearrange("p (h d) -> p h d", h=NSA_HEADS),
                        a[0:96, 0:384].rearrange("p (h d) -> p h d", h=NSA_HEADS),
                        C("bmask", 96).unsqueeze(2).to_broadcast([96, NSA_HEADS, HD]), ALU.mult).then_inc(vbd_ready, 1)
                    dve.wait_ge(vbd_ready, L + 1)
                    dve.sem_inc(acc_drained[A1.bank("vbd")], 1)

                pc3 = pc.rearrange("p (h n) -> p h n", n=NP16)
                bc = lambda v: v.unsqueeze(2).to_broadcast([P, 12, NP16])

                def compressed_softmax():
                    split = lambda v: v.rearrange("p (t g n) -> p g t n", t=TT, g=2)
                    for g in range(2):
                        a = full(A1, f"cs{g}", L)
                        STT(split(pc)[:, g, :, :], a[:, 0:96].rearrange("p (t n) -> p t n", t=TT), HD ** -0.5,
                            split(C("cmask"))[:, g, :, :], ALU.mult, ALU.add).then_inc(acc_drained[A1.bank(f"cs{g}")], 1)
                        dve.wait_ge(acc_drained[A1.bank(f"cs{g}")], A1.drained(f"cs{g}", L))
                    link(nc.vector.tensor_reduce(cst12[:, 0, :], pc3, AX.X, ALU.max))
                    TTN(pc3, pc3, bc(cst12[:, 0, :]), ALU.subtract).then_inc(csub, 1)

                def compressed_weights():
                    dve.wait_ge(cexp, L + 1)
                    link(TTN(pc[:], pc[:], C("ckeep"), ALU.mult))
                    link(nc.vector.tensor_reduce(cst12[:, 1, :], pc3, AX.X, ALU.add))
                    link(TSC(cst12[:, 1, :], cst12[:, 1, :], 1e-30, None, ALU.max))
                    link(nc.vector.reciprocal(cst12[:, 2, :], cst12[:, 1, :]))
                    g4 = gate.rearrange("p t (h b) -> p t h b", b=N_BRANCH)
                    link(TTN(cst12[:, 2, :].rearrange("p (t h) -> p t h", t=TT),
                             cst12[:, 2, :].rearrange("p (t h) -> p t h", t=TT), g4[:, :, :, 0], ALU.mult))
                    TTN(pc3, pc3, bc(cst12[:, 2, :]), ALU.mult).then_inc(pc_ready, 1)

                def add_compressed():
                    dve.wait_ge(o_drained, L * NH1 + 11)
                    for t in range(TT):
                        a = full(A1, f"co{t}", L)
                        TTN(mixed[:, t, 0:384], a[:, 0:384], mixed[:, t, 0:384], ALU.add)\
                            .then_inc(acc_drained[A1.bank(f"co{t}")], 1)
                        dve.wait_ge(acc_drained[A1.bank(f"co{t}")], A1.drained(f"co{t}", L))

                def others(i):
                    if i == 2:
                        gelu_argument()
                    if 3 <= i < 3 + MLA_HEADS:
                        rotate_query(i - 3)
                    if i == 3:
                        gelu()
                    if i == 5:
                        take_keys()
                    if i == 6:
                        mask_values()
                    if i == 7:
                        compressed_softmax()
                    if i == 8:
                        compressed_weights()
                    if i == 11:
                        add_compressed()
                    if 7 <= i < 7 + RET_HEADS:
                        decay_scores(i - 7)
                    group_norm(i)

                def group_norm(i):
                    if i == 14:
                        dve.wait_ge(acc_drained[A1.bank(f"ro{RET_HEADS - 1}")], A1.drained(f"ro{RET_HEADS - 1}", L))
                        link(nc.vector.tensor_reduce(gnst[:, 0, :], o10, AX.X, ALU.add))
                        link(TSC(gnst[:, 1, :], gnst[:, 0, :], 1.0 / HD, None, ALU.mult))
                    if i == 14:
                        link(TTN(o10, o10, bg(gnst[:, 1, :]), ALU.subtract))
                        link(TTN(s10, o10, o10, ALU.mult))
                    if i == 15:
                        link(nc.vector.tensor_reduce(gnst[:, 4, :], s10, AX.X, ALU.add))
                        TSC(gnst[:, 2, :], gnst[:, 4, :], 1.0 / HD, EPS, ALU.mult, ALU.add).then_inc(gn_v, 1)
                    if i == 12:
                        dve.wait_ge(gexp, L * 2 + 2)
                        link(STT(gx_, gx_, 1.0, tokm[:, :, RG:RG + 320], ALU.add, ALU.mult))
                    if i == 13:
                        link(TTN(gx_, gx_, V1("gn").unsqueeze(1).to_broadcast([P, TT, 320]), ALU.mult))
                    if i == 17:
                        dve.wait_ge(gn_y, L + 1)
                        refine(0, None, gnst[:, 2, :], gnst[:, 3, :], gnst[:, 4, :], gnst[:, 5, :])
                        link(TTN(o10, o10, bg(gnst[:, 5, :]), ALU.mult))
                    if i == 17:
                        link(STT(mixed[:, :, 704:1024], ro_all(0).rearrange("p (t f) -> p t f", t=TT), 0.5, gx_,
                                 ALU.mult, ALU.mult))

                for i in range(NH1 + 2):
                    if i < NH1:
                        scores(i, NH1, 0, L, scale1(i))
                    if i >= 2:
                        output(i - 2)
                    others(i)
                    for j in ada_at(i):
                        ada(j, L)
                    if i == NH1:
                        feed(24 + SPLIT // 2)
                dve.wait_ge(o_drained, L * NH1 + (NH1 + 1))
                dve.sem_inc(mixed_ready, 1)
                for c in range(KC):
                    dve.wait_ge(tH_ready, L * KC + (c + 1))
                    rest_of(hL[:, c, :], psum_of(A1, f"mt{c}")[:, 0:S], hH[:, c, :])\
                        .then_inc(acc_drained[A1.bank(f"mt{c}")], 1)
                feed(24 + SPLIT)
                for n in range(KC):
                    a = full(A1, f"wo{n}", L)
                    TTN(x[:, n, :], a[:, 0:S], x[:, n, :], ALU.add).then_inc(x_ready, 1)
                    dve.wait_ge(x_ready, L * (2 * KC) + (n + 1))
                    dve.sem_inc(acc_drained[A1.bank(f"wo{n}")], 1)
                    feed(24 + n + 1 + SPLIT)
                mean_square(A1, "ss2", L, 0, D)
                dve.wait_ge(y_ready, L * Y1 + 4)
                refine(0, None)
                norm_out(lambda c: V1("ln2", c), None, L * (2 * KC) + KC)
                for n in range(F1):
                    dve.wait_ge(acc_drained[A1.bank(f"up{n}")], A1.drained(f"up{n}", L))
                    link(TTN(tmp4[n % 4], r4[n % 4], r4[n % 4], ALU.mult))
                    dve.wait_ge(aH_ready, L * F1 + (n + 1))
                    rest_of(aL[:, n, :], tmp4[n % 4], aH[:, n, :]).then_inc(a_ready, 1)
                    feed(32 + n + 1 + SPLIT)

                def evac(n):
                    a = full(A1, f"dn{n}", L)
                    TTN(x[:, n, :], a[:, 0:S], x[:, n, :], ALU.add).then_inc(x_ready, 1)
                    dve.wait_ge(x_ready, L * (2 * KC) + (KC + n + 1))
                    dve.sem_inc(acc_drained[A1.bank(f"dn{n}")], 1)

                dve.wait_ge(ada_act, L * N_ADA + N_ADA)
                dve.wait_ge(ada_dve, L * N_ADA + N_ADA)
                nc.vector.tensor_copy(modall[:, L, :], adac[:])
                last_product(down_steps(F1), SU1, A1, L, evac)
                end_layer()

            mean_square(AF, "ssf", 0, 0, D)
            dve.wait_ge(y_ready, YF + 1)
            refine(0, None)
            for c in range(KC):
                STT(x[:, c, :], x[:, c, :], onc[:, c:c + 1], rstd[:], ALU.mult, ALU.mult).then_inc(x_ready, 1)
            dve.wait_ge(x_ready, X2)
            end_layer()

            with dve.Fori(0, LAYERS) as L:
                own[0] = 0
                nc.vector.tensor_copy(v2[:], v2all[:, L, :]).then_inc(vec_ready, 1)
                dve.wait_ge(vec_ready, L + (LAYERS + 1))
                feed_layer(TILES2, SU2, LO2, L)
                nc.vector.memset(up_[:, :, 0:16], 0.0)
                nc.vector.memset(sw[:, :, 0:16], 0.0)
                nc.vector.memset(cv[:, :, 0:2], 0.0).then_inc(pad_ready, 1)
                link(STT(mod[:], modall[:, L, :], 0.5, V2("bada"), ALU.mult, ALU.add))
                link(STT(mods[:, 0, :], mod[:, 8:16], 1.0, V2("n1"), ALU.add, ALU.mult))
                link(STT(mods[:, 1, :], mod[:, 32:40], 1.0, V2("n2"), ALU.add, ALU.mult))
                link(TSC(mods[:, 2, :], mod[:, 16:24], 0.5, None, ALU.mult))
                mean_square(A2, "ss1", L, 0, D)
                feed(2)
                dve.wait_ge(y_ready, L * Y2N + (Y2 + 1))
                refine(0, None)
                norm_out(lambda c: mods[:, 0, c:c + 1], lambda c: mod[:, c:c + 1], L * (2 * KC) + H2)
                feed(SPLIT)
                for b in range(len(UNITS2) + 3):
                    if 1 <= b < 9:
                        mean_square(A2, "ss_" + UNITS2[b - 1], L, (b - 1) % 2, HD)
                    if 2 <= b < 10:
                        j = b - 2
                        dve.wait_ge(y_ready, L * Y2N + (Y2 + 2 + j))
                        refine(j % 2, None)
                        STT(qk2[:, j, :], raw[:, j, :], V2("qn" if j < 4 else "kn", 0), rstd[:], ALU.mult, ALU.mult)\
                            .then_inc(qn2_ready, 1)
                    if b >= 3:
                        j = b - 3
                        dve.wait_ge(qn2_ready, L * 8 + (j + 1))
                        rope(A2, UNITS2[j], L, qk2[:, j, :], 3, [(qk2[:, j, :], slice(0, P))], qk2_ready)
                    if b < 8:
                        feed(b + 1 + SPLIT)
                for j in range(2):
                    feed(8 + 2 * (j + 1) + SPLIT)
                for i, u in enumerate(LATER2):
                    if u[:2] == "cc":
                        b = i % 2
                        for other in ("cu", "cb"):
                            dve.wait_ge(acc_drained[A2.bank(other + "ab"[b])], A2.drained(other + "ab"[b], L))
                        a = full(A2, u, L)
                        TTN(cv[:, b, 2:2 + S], a[:, 0:S], cu[:, b, :], ALU.mult).then_inc(acc_drained[A2.bank(u)], 1)
                        dve.wait_ge(acc_drained[A2.bank(u)], A2.drained(u, L))
                        link(TSC(tc, cv[:, b, 2:2 + S], V2("conv", 4 + b), None, ALU.mult))
                        link(STT(tc, cv[:, b, 1:1 + S], V2("conv", 2 + b), tc, ALU.mult, ALU.add))
                        link(STT(tc, cv[:, b, 0:S], V2("conv", b), tc, ALU.mult, ALU.add))
                        TTN(yc[:, b, :], tc, cb[:, b, :], ALU.mult).then_inc(ycf_ready, 1)
                    feed(12 + i + 1 + SPLIT)
                for b in range(2):
                    dve.wait_ge(ypH_ready, L * 2 + (b + 1))
                    STT(y1L[:, b, :], psum_of(A2, f"pw{b}")[:, 0:S], V2("pscale", b), y1H[:, b, :].bitcast(F32),
                        ALU.mult, ALU.subtract).then_inc(acc_drained[A2.bank(f"pw{b}")], 1)
                for b in range(2):
                    dve.wait_ge(ycH_ready, L * 2 + (b + 1))
                    rest_of(y1L[:, 2 + b, :], yc[:, b, :], y1H[:, 2 + b, :]).then_inc(yc_ready, 1)

                def output(i):
                    dve.wait_ge(p_ready, L * NH2 + (LAYERS * NH1 + i + 1))
                    link(nc.vector.reciprocal(coef[:, i, :], psumv[:, i, :]))
                    dve.wait_ge(o_full, L * NH2 + (LAYERS * NH1 + i + 1))
                    for t in range(TT):
                        last = TSC(ya[:, t, 64 * i:64 * i + 64], ps_o[:, 64 * t:64 * t + 64], coef[:, i, t:t + 1], None, ALU.mult)
                    last.then_inc(o_drained, 1)

                def gates(i):
                    for n in gates_at(i):
                        feed(20 + n + 1 + SPLIT)

                for i in range(NH2 + 2):
                    if i < NH2:
                        scores(i, NH2, LAYERS * NH1, L, HD ** -0.5)
                    if i >= 1:
                        gates(i - 1)
                    if i >= 2:
                        output(i - 2)
                dve.wait_ge(o_drained, L * NH2 + (LAYERS * NH1 + NH2 + 1))
                dve.sem_inc(ya_ready, 1)
                gates(NH2 + 1)
                for c in range(4):
                    dve.wait_ge(tH_ready, L * 4 + (M2 + c + 1))
                    rest_of(y2L[:, c, :], psum_of(A2, f"yt{c}")[:, 0:S], y2H[:, c, :])\
                        .then_inc(acc_drained[A2.bank(f"yt{c}")], 1)
                for n in range(KC + 2):
                    if n < KC:
                        if n >= 2:
                            dve.wait_ge(mg_ready, L * KC + (n - 1))
                        if n >= 4:
                            dve.wait_ge(merged_ready, L * KC + (n - 3))
                        for m, name in enumerate(MIXERS):
                            a = full(A2, f"{name}{n}", L)
                            STT(product(n, m), big[:, KC * m + n, :], 1.0, a[:, 0:S], ALU.add, ALU.mult)\
                                .then_inc(acc_drained[A2.bank(f"{name}{n}")], 1)
                        feed(44 + n + 1 + SPLIT)
                    if n >= 2:
                        dve.wait_ge(mgH_ready, L * KC + (n - 1))
                        rest_of(hL[:, n - 2, :], merged[:, (n - 2) % 4, :], hH[:, n - 2, :]).then_inc(merged_ready, 1)
                for n in range(KC):
                    a = full(A2, f"wo{n}", L)
                    STT(x[:, n, :], a[:, 0:S], mods[:, 2, n:n + 1], x[:, n, :], ALU.mult, ALU.add).then_inc(x_ready, 1)
                    dve.wait_ge(x_ready, L * (2 * KC) + (X2 + n + 1))
                    dve.sem_inc(acc_drained[A2.bank(f"wo{n}")], 1)
                    feed(52 + n + 1 + SPLIT)
                mean_square(A2, "ss2", L, 0, D)
                dve.wait_ge(y_ready, L * Y2N + (Y2 + 10))
                refine(0, None)
                norm_out(lambda c: mods[:, 1, c:c + 1], lambda c: mod[:, 24 + c:25 + c], L * (2 * KC) + (H2 + KC))
                for n in range(F2):
                    dve.wait_ge(tanh_ready, L * F2 + (n + 1))
                    g = psum_of(A2, f"gt{n}")
                    STT(tmp4[n % 4], r4[n % 4], 1.0, g[:, 0:S], ALU.add, ALU.mult)\
                        .then_inc(acc_drained[A2.bank(f"gt{n}")], 1)
                    feed(60 + 2 * n + 1 + SPLIT)
                    dve.wait_ge(acc_drained[A2.bank(f"gt{n}")], A2.drained(f"gt{n}", L))
                    u = full(A2, f"up{n}", L)
                    STT(pair2[n % 2], tmp4[n % 4], 0.5, u[:, 0:S], ALU.mult, ALU.mult).then_inc(aT_ready, 1)
                    dve.wait_ge(aT_ready, L * F2 + (n + 1))
                    dve.sem_inc(acc_drained[A2.bank(f"up{n}")], 1)
                    feed(60 + 2 * n + 2 + SPLIT)
                    dve.wait_ge(a2H_ready, L * F2 + (n + 1))
                    rest_of(aL[:, n, :], pair2[n % 2], aH[:, n, :]).then_inc(a2_ready, 1)

                def evac(n):
                    a = full(A2, f"dn{n}", L)
                    STT(x[:, n, :], a[:, 0:S], mod[:, 40 + n:41 + n], x[:, n, :], ALU.mult, ALU.add).then_inc(x_ready, 1)
                    dve.wait_ge(x_ready, L * (2 * KC) + (X2 + KC + n + 1))
                    dve.sem_inc(acc_drained[A2.bank(f"dn{n}")], 1)

                last_product(down_steps(F2), SU2, A2, L, evac)
                end_layer()

        @block.gpsimd
        def _(pool):
            own = [0]

            def link(ins):
                own[0] += 1
                ins.then_inc(pool_step, 1)
                pool.wait_ge(pool_step, own[0])

            TTN = nc.gpsimd.tensor_tensor
            with pool.Fori(0, LAYERS) as L:
                for j in range(N_ADA):
                    pool.wait_ge(ada_dve, L * N_ADA + (j + 1))
                    t = TILES1.index(("ada", j))
                    products = ring[:, t % RING, UNIT:2 * UNIT]
                    TTN(products, products, cb2, ALU.mult).then_inc(ada_pool, 1)

            with pool.Fori(0, LAYERS) as L:
                own[0] = 0
                pool.wait_ge(pad_ready, L + 1)
                w0 = 16
                for b, u in enumerate(("pa", "pb")):
                    pool.wait_ge(acc_drained[A2.bank(u)], A2.drained(u, L))
                    for j in range(2 if b == 0 else 4):
                        src, dst = (up_[:, b, :] if j == 0 else sw[:, (j - 1) % 2 * 2 + 1, :]), sw[:, j % 2 * 2 + 1, :]
                        link(TTN(dst[:, w0:w0 + S], src[:, w0:w0 + S], src[:, w0 - 2 ** j:w0 - 2 ** j + S], ALU.add))
                    lo, hi = sw[:, 1, :], sw[:, 3, :]
                    res = sw[:, 2 * b, w0:w0 + S]
                    TTN(res[0:64, :], lo[0:64, w0:w0 + S], invc[0:64, b, :], ALU.mult)
                    link(TTN(res[64:128, :], hi[64:128, w0:w0 + S], invc[64:128, b, :], ALU.mult))
                    link(TTN(res, res, up_[:, b, w0:w0 + S], ALU.subtract))
                    pool.sem_inc(pooled, 1)
                for n in range(KC):
                    name = f"{MIXERS[-1]}{n}"
                    pool.wait_ge(acc_drained[A2.bank(name)], A2.drained(name, L))
                    mg = product(n, 0)
                    link(TTN(mg, mg, product(n, 1), ALU.add))
                    TTN(mg, mg, product(n, 2), ALU.add).then_inc(mg_ready, 1)
                pool.sem_clear(pool_step)


def _blocks(w):
    k, n = w.shape
    b = np.zeros((P, k // P, P), np.float32)
    b[:, :, :n] = w.reshape(k // P, P, n).transpose(1, 0, 2)
    return b.reshape(P, -1)


def _wide(w):
    b = np.zeros((P, KC, 256), np.float32)
    b[:, :, :w.shape[1]] = w.reshape(KC, P, -1).transpose(1, 0, 2)
    return b.reshape(P, -1)


def _columns(v):
    return v.reshape(-1, P).T


def _stream(i):
    out = np.zeros((LAYERS * (T1 + T2), P, TILE), np.float32)
    for l in range(LAYERS):
        w = i["w_in"][l]
        cols = {}
        for r in range(3):
            cols[f"q{r}"] = np.r_[64 * r:64 * r + 64, 64 * (3 + r):64 * (3 + r) + 64]
        cols.update(kc=np.r_[384:512], vc=np.r_[512:640], ks=np.r_[640:768], kw=np.r_[896:1024],
                    cq0=np.r_[1170:1298], cq1=np.r_[1298:1426], ckv=np.r_[1426:1554], kpe=np.r_[1490:1586],
                    rqa=np.r_[1586:1714], rqb=np.r_[1714:1842], rka=np.r_[1906:2034], rkb=np.r_[2034:2162],
                    r4=np.r_[1842:1906, 2162:2226])
        tm = np.r_[768:896, 1024:1152, 1152:1170, 2226:2546, 2546:2866]
        w1k, w1v = i["cmp_w1_k"][l], i["cmp_w1_v"][l]
        for t, (kind, j) in enumerate(TILES1):
            o = out[l * T1 + t]
            if kind in cols:
                o[:, :1024], o[:, 1024:] = _blocks(w[:, cols[kind]]), _blocks(w[:, cols[j]])
            elif kind == "tm":
                o[:] = _wide(w[:, tm[256 * j:256 * j + 256]])
            elif kind == "cmpk":
                o[:] = w1k.reshape(16, P, P).transpose(1, 0, 2).reshape(P, -1)
            elif kind == "cmpv":
                o[:] = w1v.reshape(16, P, P).transpose(1, 0, 2).reshape(P, -1)
            elif kind == "small":
                o[:, UQ:UQ + 960] = i["mla_w_uq"][l].reshape(2, P, 480).transpose(1, 0, 2).reshape(P, -1)
                o[:, UKV:UKV + 640] = i["mla_w_ukv"][l]
                o[:, W2K:W2K + 128] = np.tile(i["cmp_w2_k"][l], (1, 2))
                o[:, W2V:W2V + 192] = np.tile(i["cmp_w2_v"][l], (1, 3))
            elif kind in ("wout", "up"):
                m = i["w_out" if kind == "wout" else "w_up"][l]
                for b in range(2):
                    o[:, 1024 * b:1024 * b + 1024] = _blocks(m[:, P * (2 * j + b):P * (2 * j + b + 1)])
            elif kind == "ada":
                for b in range(2):
                    o[:, 1024 * b:1024 * b + 1024] = i["w_ada_2"][l][:, P * (2 * j + b):P * (2 * j + b + 1)].T
            else:
                m = i["w_down"][l][2048 * (j % 2):2048 * (j % 2 + 1), P * (j // 2):P * (j // 2 + 1)]
                o[:] = _blocks(m)
        w = i["w_in_2"][l]
        cols = {f"q{b}": np.r_[1024 + P * b:1024 + P * b + P] for b in range(4)}
        cols.update({f"k{b}": np.r_[1536 + P * b:1536 + P * b + P] for b in range(4)})
        for b, u in enumerate(LATER2):
            cols[u] = np.r_[P * b:P * b + P]
        down = i["w_down_2"][l].reshape(F2, P, KC, P).transpose(2, 0, 1, 3).reshape(KC * F2, P, P)
        for t, (kind, j) in enumerate(TILES2):
            o = out[LAYERS * T1 + l * T2 + t]
            if kind in cols:
                o[:, :1024], o[:, 1024:] = _blocks(w[:, cols[kind]]), _blocks(w[:, cols[j]])
            elif kind == "v":
                o[:] = _wide(w[:, 2048 + 256 * j:2048 + 256 * j + 256])
            elif kind in ("wout", "gate"):
                m, at = {"wout": (i["w_out_2"][l], 0), "gate": (w, 2560)}[kind]
                for b in range(2):
                    c = at + P * (2 * j + b)
                    o[:, 1024 * b:1024 * b + 1024] = _blocks(m[:, c:c + P])
            elif kind == "mix":
                m = np.concatenate([i["p_pool_2"][l], i["p_conv_2"][l], i["p_attn_2"][l]], axis=0)
                for b in range(2):
                    o[:, 1024 * b:1024 * b + 1024] = _blocks(m[:, P * (2 * j + b):P * (2 * j + b + 1)])
            elif kind == "gu":
                for b, m in enumerate((i["w_gate_2"][l], i["w_up_2"][l])):
                    o[:, 1024 * b:1024 * b + 1024] = _blocks(m[:, P * j:P * j + P])
            else:
                o[:] = down[16 * j:16 * j + 16].transpose(1, 0, 2).reshape(P, -1)
    return out


def kernel(**inputs):
    import concourse.bacc as _bacc
    from concourse import mybir as _mybir
    from concourse.bass_utils import run_bass_kernel_spmd as _run

    i = {k: np.asarray(v) for k, v in inputs.items()}
    vec1 = np.zeros((P, LAYERS, N_V1), np.float32)
    vec2 = np.zeros((P, LAYERS, N_V2), np.float32)
    for l in range(LAYERS):
        def put(arr, table, name, a):
            at, w = table[name]
            arr[:, l, at:at + w] = a
        put(vec1, VEC1, "ln1", _columns(i["ln1_gain"][l]))
        put(vec1, VEC1, "ln2", _columns(i["ln2_gain"][l]))
        put(vec1, VEC1, "qn", _columns(i["mla_q_norm"][l]))
        put(vec1, VEC1, "kvn", _columns(i["mla_kv_norm"][l]))
        put(vec1, VEC1, "posk", i["cmp_pos_k"][l].reshape(16, P).T)
        put(vec1, VEC1, "posv", i["cmp_pos_v"][l].reshape(16, P).T)
        put(vec1, VEC1, "gn", np.broadcast_to(i["ret_gn_gain"][l].reshape(1, 320), (P, 320)))
        put(vec2, VEC2, "n1", _columns(i["norm1_w_2"][l]))
        put(vec2, VEC2, "n2", _columns(i["norm2_w_2"][l]))
        put(vec2, VEC2, "bada", _columns(i["b_ada_2"][l]))
        put(vec2, VEC2, "pscale", _columns(i["pool_scale_2"][l]))
        put(vec2, VEC2, "conv", i["conv_w_2"][l].reshape(3, 2, P).transpose(2, 0, 1).reshape(P, 6))
        put(vec2, VEC2, "qn", np.tile(i["q_norm_w_2"][l], 2)[:, None])
        put(vec2, VEC2, "kn", np.tile(i["k_norm_w_2"][l], 2)[:, None])
        bd = np.zeros((P, 2, P), np.float32)
        for g in range(4):
            r = 64 * (g % 2)
            bd[r:r + 64, g // 2, r:r + 64] = i["pool_w_2"][l][g]
        put(vec2, VEC2, "poolw", bd.reshape(P, 256))
    once = np.concatenate([_columns(i["final_gain"]), np.broadcast_to(i["c_2"][0][None], (P, D))], axis=1)
    pos = np.stack([i["positions"][0], i["positions_2"][0]])
    arrays = {
        "consts": constants(), "vec1": vec1, "vec2": vec2, "once": np.ascontiguousarray(once),
        "pos": np.ascontiguousarray(np.broadcast_to(pos[None].astype(np.int32), (P, 2, S))),
        "xin": np.ascontiguousarray(i["x"][0].T.reshape(KC, P, S).transpose(1, 0, 2)),
        "stream": _stream(i),
    }
    nc = _bacc.Bacc("TRN2", target_bir_lowering=False, num_devices=1)
    args = [nc.dram_tensor(n, a.shape, _mybir.dt.from_np(a.dtype), kind="ExternalInput").ap() for n, a in arrays.items()]
    out = nc.dram_tensor("out", (P, KC, S), _mybir.dt.float32, kind="ExternalOutput").ap()
    trn_kernel(nc, *args, out)
    r = _run(nc, [arrays], core_ids=[0])
    got = r.results[0]["out"]
    return np.ascontiguousarray(got.transpose(1, 0, 2).reshape(D, S).T)[None]
```
